# Optimizing a Trainium2 kernel written in Bass

```python
import jax, jax.numpy as jnp
from jax import lax
import numpy as np

D_MODEL = 1024
BATCH = 1
SEQ = 1024
DEPTH = 1

D_MIX = 1024
GDN_HEADS = 4
GDN_DK = 128
GDN_DV = 128
GDN_CONV = 4
GDN_CHUNK = 64
RWKV_HEADS = 8
RWKV_N = 64
LORA_W = 64
LORA_A = 64
LORA_G = 128
D_FF = 2816
D_PLE = 256
NORM_EPS = 1e-6
GN_EPS = 64e-5
L2_EPS = 1e-6

GDN_QK_W = GDN_HEADS * GDN_DK
GDN_W = GDN_HEADS * GDN_DV
GDN_CONV_COLS = 2 * GDN_QK_W + GDN_W
GDN_COLS = GDN_CONV_COLS + GDN_W + 2 * GDN_HEADS
RWKV_W = RWKV_HEADS * RWKV_N
RWKV_COLS = 3 * RWKV_W + LORA_W + LORA_A + LORA_G
IN_COLS = GDN_COLS + RWKV_COLS

kernel_name = 'hybrid_gdn_rwkv7_macaron_block'

def rmsnorm(x, g):
    xf = x.astype(jnp.float32)
    y = xf * lax.rsqrt(jnp.mean(xf * xf, axis=-1, keepdims=True) + NORM_EPS)
    return (y * g.astype(jnp.float32)).astype(x.dtype)

def l2norm(x):
    return x * lax.rsqrt(jnp.sum(x * x, axis=-1, keepdims=True) + L2_EPS)

def swiglu(x, w_gate, w_up, w_down):
    return (jax.nn.silu(x @ w_gate) * (x @ w_up)) @ w_down

def causal_depthwise_conv(x, w):
    k = w.shape[0]
    return lax.conv_general_dilated(
        x, w[:, None, :].astype(x.dtype), window_strides=(1,), padding=((k - 1, 0),),
        dimension_numbers=('NWC', 'WIO', 'NWC'), feature_group_count=x.shape[-1])

def to_chunks(t, n_chunks):
    b, _, h = t.shape[:3]
    t = t.reshape(b, n_chunks, GDN_CHUNK, h, *t.shape[3:])
    return jnp.moveaxis(t, 3, 1)

def gated_delta_rule_chunked(q, k, v, g, beta):
    b, t, h, dk = q.shape
    dv = v.shape[-1]
    nc = t // GDN_CHUNK
    q = to_chunks(q * dk ** -0.5, nc)
    k = to_chunks(k, nc)
    v = to_chunks(v, nc)
    g = to_chunks(g, nc)
    beta = to_chunks(beta, nc)
    gc = jnp.cumsum(g, axis=-1)
    idx = jnp.arange(GDN_CHUNK)
    causal = idx[:, None] >= idx[None, :]
    strict = idx[:, None] > idx[None, :]
    decay = jnp.where(causal, jnp.exp(jnp.where(causal, gc[..., :, None] - gc[..., None, :], 0.0)), 0.0)
    kb = k * beta[..., None]
    vb = v * beta[..., None]
    lmat = jnp.where(strict, jnp.einsum('bhnid,bhnjd->bhnij', kb, k) * decay, 0.0)
    eye = jnp.eye(GDN_CHUNK, dtype=jnp.float32)
    tinv = lax.linalg.triangular_solve(eye + lmat, jnp.broadcast_to(eye, lmat.shape),
                                       left_side=True, lower=True, unit_diagonal=True)
    u = tinv @ vb
    wk = tinv @ (kb * jnp.exp(gc)[..., None])
    a_qk = jnp.einsum('bhnid,bhnjd->bhnij', q, k) * decay
    q_dec = q * jnp.exp(gc)[..., None]
    k_dec = k * jnp.exp(gc[..., -1:] - gc)[..., None]
    g_last = jnp.exp(gc[..., -1])
    xs = tuple(jnp.moveaxis(a, 2, 0) for a in (u, wk, q_dec, a_qk, k_dec, g_last))

    def step(state, inp):
        u_n, w_n, q_n, a_n, k_n, gl_n = inp
        v_new = u_n - w_n @ state
        o_n = q_n @ state + a_n @ v_new
        state = state * gl_n[..., None, None] + jnp.swapaxes(k_n, -1, -2) @ v_new
        return state, o_n

    s0 = jnp.zeros((b, h, dk, dv), jnp.float32)
    _, o = lax.scan(step, s0, xs)
    return jnp.transpose(o, (1, 0, 3, 2, 4)).reshape(b, t, h, dv)

def rwkv7_scan(r, w, k, v, kk, a):
    b, _, h, n = r.shape
    xs = tuple(jnp.moveaxis(t, 1, 0) for t in (r, w, k, v, kk, a))

    def step(state, inp):
        r_t, w_t, k_t, v_t, kk_t, a_t = inp
        sa = jnp.einsum('bhvk,bhk->bhv', state, -kk_t)
        state = (state * w_t[:, :, None, :] + sa[..., None] * (kk_t * a_t)[:, :, None, :]
                 + v_t[..., None] * k_t[:, :, None, :])
        y = jnp.einsum('bhvk,bhk->bhv', state, r_t)
        return state, y

    s0 = jnp.zeros((b, h, n, n), jnp.float32)
    _, y = lax.scan(step, s0, xs)
    return jnp.moveaxis(y, 0, 1)

def hybrid_mixer(h, w_in, conv_w, a_log, dt_bias, gdn_norm_w, mu, w0, w2, a0, a2, g2,
                 k_k, k_a, r_k, gn_w, gn_b, w_out):
    b, t, _ = h.shape
    f32 = jnp.float32
    proj = (h @ w_in).astype(f32)

    gdn = proj[..., :GDN_COLS]
    qkv = jax.nn.silu(causal_depthwise_conv(gdn[..., :GDN_CONV_COLS], conv_w.astype(f32)))
    q = l2norm(qkv[..., :GDN_QK_W].reshape(b, t, GDN_HEADS, GDN_DK))
    k = l2norm(qkv[..., GDN_QK_W:2 * GDN_QK_W].reshape(b, t, GDN_HEADS, GDN_DK))
    v = qkv[..., 2 * GDN_QK_W:].reshape(b, t, GDN_HEADS, GDN_DV)
    z = gdn[..., GDN_CONV_COLS:GDN_CONV_COLS + GDN_W].reshape(b, t, GDN_HEADS, GDN_DV)
    off = GDN_CONV_COLS + GDN_W
    beta = jax.nn.sigmoid(gdn[..., off:off + GDN_HEADS])
    g = -jnp.exp(a_log.astype(f32)) * jax.nn.softplus(gdn[..., off + GDN_HEADS:] + dt_bias.astype(f32))
    o = gated_delta_rule_chunked(q, k, v, g, beta)
    o = rmsnorm(o, gdn_norm_w) * jax.nn.silu(z)
    y_gdn = o.reshape(b, t, GDN_W)

    rw = proj[..., GDN_COLS:]
    prev = jnp.pad(rw, ((0, 0), (1, 0), (0, 0)))[:, :-1]
    xs = rw + (prev - rw) * mu.astype(f32)
    r = xs[..., :RWKV_W]
    kr = xs[..., RWKV_W:2 * RWKV_W]
    vr = xs[..., 2 * RWKV_W:3 * RWKV_W]
    off = 3 * RWKV_W
    lw = xs[..., off:off + LORA_W]
    la = xs[..., off + LORA_W:off + LORA_W + LORA_A]
    lg = xs[..., off + LORA_W + LORA_A:]
    w_log = -jax.nn.softplus(-(w0.astype(f32) + jnp.tanh(lw) @ w2.astype(f32))) - 0.5
    decay = jnp.exp(-jnp.exp(w_log))
    a = jax.nn.sigmoid(a0.astype(f32) + la @ a2.astype(f32))
    gate = jax.nn.sigmoid(lg) @ g2.astype(f32)
    hs = (b, t, RWKV_HEADS, RWKV_N)
    r, kr, vr, a, decay = (u.reshape(hs) for u in (r, kr, vr, a, decay))
    kk = l2norm(kr * k_k.astype(f32).reshape(RWKV_HEADS, RWKV_N))
    kr = kr * (1.0 + (a - 1.0) * k_a.astype(f32).reshape(RWKV_HEADS, RWKV_N))
    y = rwkv7_scan(r, decay, kr, vr, kk, a)
    mean = jnp.mean(y, axis=-1, keepdims=True)
    var = jnp.mean(jnp.square(y - mean), axis=-1, keepdims=True)
    y = ((y - mean) * lax.rsqrt(var + GN_EPS) * gn_w.astype(f32).reshape(RWKV_HEADS, RWKV_N)
         + gn_b.astype(f32).reshape(RWKV_HEADS, RWKV_N))
    y = y + jnp.sum(r * kr * r_k.astype(f32), axis=-1, keepdims=True) * vr
    y_rwkv = y.reshape(b, t, RWKV_W) * gate

    merged = jnp.concatenate([y_gdn, y_rwkv], axis=-1).astype(h.dtype)
    return merged @ w_out

def setup_inputs(seed: int = 0) -> dict:
    key = jax.random.key(seed)
    ks = list(jax.random.split(key, 40))
    f32 = jnp.float32

    def nrm(shape, scale):
        return jax.random.normal(ks.pop(), shape, f32) * scale

    def gain(n):
        return 1.0 + 0.02 * jax.random.normal(ks.pop(), (DEPTH, n), f32)

    def unif(shape, lo, hi):
        return jax.random.uniform(ks.pop(), shape, f32, minval=lo, maxval=hi)

    dt = jnp.exp(unif((DEPTH, GDN_HEADS), float(np.log(1e-3)), float(np.log(1e-1))))
    inp = {}
    inp['x'] = nrm((BATCH, SEQ, D_MODEL), 1.0)
    inp['p'] = nrm((DEPTH, BATCH, SEQ, D_PLE), 1.0)
    inp['ffn1_norm_pre'] = gain(D_MODEL)
    inp['ffn1_w_gate'] = nrm((DEPTH, D_MODEL, D_FF), D_MODEL ** -0.5)
    inp['ffn1_w_up'] = nrm((DEPTH, D_MODEL, D_FF), D_MODEL ** -0.5)
    inp['ffn1_w_down'] = nrm((DEPTH, D_FF, D_MODEL), D_FF ** -0.5)
    inp['ffn1_norm_post'] = gain(D_MODEL)
    inp['mix_norm_pre'] = gain(D_MODEL)
    inp['w_in'] = nrm((DEPTH, D_MODEL, IN_COLS), D_MODEL ** -0.5)
    inp['gdn_conv_w'] = nrm((DEPTH, GDN_CONV, GDN_CONV_COLS), GDN_CONV ** -0.5)
    inp['gdn_a_log'] = jnp.log(unif((DEPTH, GDN_HEADS), 1.0, 16.0))
    inp['gdn_dt_bias'] = dt + jnp.log(-jnp.expm1(-dt))
    inp['gdn_norm_w'] = gain(GDN_DV)
    inp['rwkv_mu'] = unif((DEPTH, RWKV_COLS), 0.0, 1.0)
    inp['rwkv_w0'] = unif((DEPTH, RWKV_W), -6.0, 1.0)
    inp['rwkv_w2'] = nrm((DEPTH, LORA_W, RWKV_W), LORA_W ** -0.5)
    inp['rwkv_a0'] = nrm((DEPTH, RWKV_W), 0.5)
    inp['rwkv_a2'] = nrm((DEPTH, LORA_A, RWKV_W), LORA_A ** -0.5)
    inp['rwkv_g2'] = nrm((DEPTH, LORA_G, RWKV_W), LORA_G ** -0.5)
    inp['rwkv_k_k'] = 0.85 + nrm((DEPTH, RWKV_W), 0.05)
    inp['rwkv_k_a'] = 1.0 + nrm((DEPTH, RWKV_W), 0.05)
    inp['rwkv_r_k'] = nrm((DEPTH, RWKV_HEADS, RWKV_N), 0.1)
    inp['rwkv_gn_w'] = gain(RWKV_W)
    inp['rwkv_gn_b'] = nrm((DEPTH, RWKV_W), 0.01)
    inp['w_out'] = nrm((DEPTH, D_MIX, D_MODEL), D_MIX ** -0.5)
    inp['mix_norm_post'] = gain(D_MODEL)
    inp['ffn2_norm_pre'] = gain(D_MODEL)
    inp['ffn2_w_gate'] = nrm((DEPTH, D_MODEL, D_FF), D_MODEL ** -0.5)
    inp['ffn2_w_up'] = nrm((DEPTH, D_MODEL, D_FF), D_MODEL ** -0.5)
    inp['ffn2_w_down'] = nrm((DEPTH, D_FF, D_MODEL), D_FF ** -0.5)
    inp['ffn2_norm_post'] = gain(D_MODEL)
    inp['ple_norm_pre'] = gain(D_MODEL)
    inp['ple_w_gate'] = nrm((DEPTH, D_MODEL, D_MODEL), D_MODEL ** -0.5)
    inp['ple_w_proj'] = nrm((DEPTH, D_PLE, D_MODEL), D_PLE ** -0.5)
    inp['ple_norm_post'] = gain(D_MODEL)
    return inp

def reference(x, p, ffn1_norm_pre, ffn1_w_gate, ffn1_w_up, ffn1_w_down, ffn1_norm_post,
              mix_norm_pre, w_in, gdn_conv_w, gdn_a_log, gdn_dt_bias, gdn_norm_w,
              rwkv_mu, rwkv_w0, rwkv_w2, rwkv_a0, rwkv_a2, rwkv_g2, rwkv_k_k, rwkv_k_a, rwkv_r_k,
              rwkv_gn_w, rwkv_gn_b, w_out, mix_norm_post,
              ffn2_norm_pre, ffn2_w_gate, ffn2_w_up, ffn2_w_down, ffn2_norm_post,
              ple_norm_pre, ple_w_gate, ple_w_proj, ple_norm_post):
    for i in range(DEPTH):
        f = swiglu(rmsnorm(x, ffn1_norm_pre[i]), ffn1_w_gate[i], ffn1_w_up[i], ffn1_w_down[i])
        x = x + 0.5 * rmsnorm(f, ffn1_norm_post[i])
        m = hybrid_mixer(rmsnorm(x, mix_norm_pre[i]), w_in[i], gdn_conv_w[i], gdn_a_log[i],
                         gdn_dt_bias[i], gdn_norm_w[i], rwkv_mu[i], rwkv_w0[i], rwkv_w2[i],
                         rwkv_a0[i], rwkv_a2[i], rwkv_g2[i], rwkv_k_k[i], rwkv_k_a[i], rwkv_r_k[i],
                         rwkv_gn_w[i], rwkv_gn_b[i], w_out[i])
        x = x + rmsnorm(m, mix_norm_post[i])
        f = swiglu(rmsnorm(x, ffn2_norm_pre[i]), ffn2_w_gate[i], ffn2_w_up[i], ffn2_w_down[i])
        x = x + 0.5 * rmsnorm(f, ffn2_norm_post[i])
        gate = jax.nn.sigmoid(rmsnorm(x, ple_norm_pre[i]) @ ple_w_gate[i])
        x = x + rmsnorm(gate * (p[i] @ ple_w_proj[i]), ple_norm_post[i])
    return x


_drawn_inputs = setup_inputs


def setup_inputs(seed=0):
    import zlib

    import numpy as np

    out = dict(_drawn_inputs(seed))
    spreads = {}
    factors = {'ffn1_norm_pre': 3.274,
     'ffn1_norm_post': 4.8,
     'gdn_a_log': 6.582,
     'gdn_norm_w': 30.574,
     'rwkv_k_k': 3.257,
     'rwkv_k_a': 2.694,
     'rwkv_gn_w': 25.868,
     'rwkv_gn_b': 48.743,
     'mix_norm_post': 12.772,
     'ffn2_norm_pre': 21.699,
     'ffn2_norm_post': 37.146,
     'ple_norm_pre': 36.881,
     'ple_norm_post': 86.897,
     'rwkv_r_k': 3.646}
    for name, (base, spread) in spreads.items():
        noise = np.random.default_rng([zlib.crc32(name.encode()), seed]).standard_normal(out[name].shape)
        drawn = base * np.exp(spread * noise) if base else spread * noise
        out[name] = __import__('jax').numpy.asarray(drawn.astype(out[name].dtype))
    for name, factor in factors.items():
        out[name] = (out[name] * factor).astype(out[name].dtype)
    return out
```

```python
from contextlib import ExitStack

import concourse.bass as bass
from concourse import mybir

F32 = mybir.dt.float32
F32R = mybir.dt.float32r
U32 = mybir.dt.uint32
ALU = mybir.AluOpType
ACT = mybir.ActivationFunctionType

P = 128
SEQ = 1024
D = 1024
D_FF = 2816
D_PLE = 256
NT = SEQ // P
ND = D // P
HALF = 512
NH = SEQ // HALF
NORM_EPS = 1e-6


class Stage:

    def __init__(self, nc, tag):
        self.nc, self.tag, self.stack, self.sems = nc, tag, ExitStack(), []

    def __enter__(self):
        self.stack.__enter__()
        return self

    def __exit__(self, *what):
        self.stack.__exit__(*what)
        if self.sems:
            self.nc.clear_and_free_semaphores(self.sems)
            self.nc.all_engine_barrier()

    def sbuf(self, name, shape, dtype=F32):
        return self.stack.enter_context(self.nc.sbuf_tensor(f"{self.tag}_{name}", shape, dtype))

    def psum(self, name, shape, dtype=F32):
        return self.stack.enter_context(self.nc.psum_tensor(f"{self.tag}_{name}", shape, dtype))

    def sem(self, name):
        self.sems.append(self.nc.alloc_semaphore(f"{self.tag}_{name}"))
        return self.sems[-1]


def split_matmul(nc, out, weights, moving, first, last):
    (w_hi, w_lo), (m_hi, m_lo) = weights, moving
    nc.tensor.matmul(out, w_hi, m_hi, start=first, stop=False)
    nc.tensor.matmul(out, w_hi, m_lo, start=False, stop=False)
    return nc.tensor.matmul(out, w_lo, m_hi, start=False, stop=last)


def row_of(vector):
    return bass.AP(tensor=vector.tensor, offset=vector.offset, ap=[[0, P], [1, vector.shape[-1]]])


def residual_norm(nc, tag, x_in, x_out, branch, post_gain, share, pre_gain, h, identity):
    LOOPS = NT // 2
    with Stage(nc, tag) as st:
        x = st.sbuf("x", [P, 2, D])
        scratch = st.sbuf("scratch", [P, 2, D])
        normed = st.sbuf("normed", [P, 2, D])
        added = st.sbuf("added", [P, 2, D])
        stats = st.sbuf("stats", [P, 2, 8])
        post_row = st.sbuf("post_row", [P, D])
        pre_row = st.sbuf("pre_row", [P, D])
        turned = st.psum("turned", [P, 4, HALF])
        rows_in = st.sem("rows_in")
        x_loaded = [st.sem(f"x_loaded{u}") for u in range(2)]
        x_stored = [st.sem(f"x_stored{u}") for u in range(2)]
        branch_squared, branch_mean, branch_root = st.sem("branch_squared"), st.sem("branch_mean"), st.sem("branch_root")
        branch_inverse, branch_scaled, x_ready = st.sem("branch_inverse"), st.sem("branch_scaled"), st.sem("x_ready")
        x_squared, x_mean, x_root = st.sem("x_squared"), st.sem("x_mean"), st.sem("x_root")
        x_inverse, x_normed = st.sem("x_inverse"), st.sem("x_normed")
        transposed, hi_done, lo_done = st.sem("transposed"), st.sem("hi_done"), st.sem("lo_done")
        block = st.stack.enter_context(nc.Block())
        x_sem = x_ready if branch is not None else None

        @block.sync
        def _(sp):
            n = 0
            if branch is not None:
                sp.dma_start(post_row[:], row_of(post_gain)).then_inc(rows_in, 16)
                n += 16
            if pre_gain is not None:
                sp.dma_start(pre_row[:], row_of(pre_gain)).then_inc(rows_in, 16)
            for u in range(2):
                sp.dma_start(x[:, u], x_in[u * P:(u + 1) * P, :]).then_inc(x_loaded[u], 16)
            if branch is None:
                with sp.Fori(0, LOOPS - 1) as i:
                    for u in range(2):
                        sp.wait_ge(x_normed, 2 * i + u + 1)
                        sp.dma_start(x[:, u], x_in[bass.ds((2 * i + u + 2) * P, P), :]).then_inc(x_loaded[u], 16)
            else:
                def store(n, i, u):
                    sp.wait_ge(x_ready, n + 1)
                    sp.dma_start(x_out[bass.ds(n * P, P), :], added[:, u]).then_inc(x_stored[u], 16)

                with sp.Fori(0, LOOPS - 1) as i:
                    for u in range(2):
                        store(2 * i + u, i, u)
                        sp.wait_ge(x_stored[u], 16 * (i + 1))
                        sp.dma_start(x[:, u], x_in[bass.ds((2 * i + u + 2) * P, P), :]).then_inc(x_loaded[u], 16)
                for u in range(2):
                    store(NT - 2 + u, LOOPS - 1, u)
                for u in range(2):
                    sp.wait_ge(x_stored[u], 16 * LOOPS)

        @block.scalar
        def _(act):
            with act.Fori(0, LOOPS) as i:
                for u in range(2):
                    n = 2 * i + u
                    if branch is not None:
                        nc.scalar.activation(scratch[:, u], branch[:, bass.ds(n, 1), :].rearrange("p a d -> p (a d)"), ACT.Square,
                                             accum_out=stats[:, u, 0:1]).then_inc(branch_squared, 1)
                        act.wait_ge(branch_mean, n + 1)
                        nc.scalar.activation(stats[:, u, 2:3], stats[:, u, 1:2], ACT.Sqrt).then_inc(branch_root, 1)
                        act.wait_ge(x_ready, n + 1)
                        xin = added[:, u]
                    else:
                        act.wait_ge(x_loaded[u], 16 * (i + 1))
                        xin = x[:, u]
                    if pre_gain is None:
                        continue
                    nc.scalar.activation(scratch[:, u], xin, ACT.Square, accum_out=stats[:, u, 4:5]).then_inc(x_squared, 1)
                    act.wait_ge(x_mean, n + 1)
                    nc.scalar.activation(stats[:, u, 6:7], stats[:, u, 5:6], ACT.Sqrt).then_inc(x_root, 1)
                    for b in range(2):
                        act.wait_ge(transposed, 2 * n + b + 1)
                        nc.scalar.copy(h[0][:, 4 * b:4 * b + 4, bass.ds(n * P, P)],
                                       turned[:, 2 * u + b].rearrange("p (c t) -> p c t", t=P)).then_inc(hi_done, 1)

        @block.vector
        def _(dve):
            dve.wait_ge(rows_in, 16 * ((branch is not None) + (pre_gain is not None)))
            with dve.Fori(0, LOOPS) as i:
                for u in range(2):
                    n = 2 * i + u
                    if branch is not None:
                        dve.wait_ge(branch_squared, n + 1)
                        nc.vector.tensor_scalar(stats[:, u, 1:2], stats[:, u, 0:1], 1.0 / D, NORM_EPS, ALU.mult, ALU.add).then_inc(branch_mean, 1)
                        dve.wait_ge(branch_root, n + 1)
                        nc.vector.reciprocal(stats[:, u, 3:4], stats[:, u, 2:3]).then_inc(branch_inverse, 1)
                        dve.wait_ge(branch_inverse, n + 1)
                        nc.vector.scalar_tensor_tensor(normed[:, u], branch[:, bass.ds(n, 1), :].rearrange("p a d -> p (a d)"), stats[:, u, 3:4], post_row[:],
                                                       ALU.mult, ALU.mult).then_inc(branch_scaled, 1)
                        dve.wait_ge(branch_scaled, n + 1)
                        dve.wait_ge(x_loaded[u], 16 * (i + 1))
                        nc.vector.scalar_tensor_tensor(added[:, u], normed[:, u], share, x[:, u],
                                                       ALU.mult, ALU.add).then_inc(x_ready, 1)
                        xin = added[:, u]
                    else:
                        xin = x[:, u]
                    if pre_gain is None:
                        continue
                    dve.wait_ge(x_squared, n + 1)
                    nc.vector.tensor_scalar(stats[:, u, 5:6], stats[:, u, 4:5], 1.0 / D, NORM_EPS, ALU.mult, ALU.add).then_inc(x_mean, 1)
                    dve.wait_ge(x_root, n + 1)
                    nc.vector.reciprocal(stats[:, u, 7:8], stats[:, u, 6:7]).then_inc(x_inverse, 1)
                    dve.wait_ge(x_inverse, n + 1)
                    nc.vector.scalar_tensor_tensor(normed[:, u], xin, stats[:, u, 7:8], pre_row[:],
                                                   ALU.mult, ALU.mult).then_inc(x_normed, 1)
                    for b in range(2):
                        dve.wait_ge(hi_done, 2 * n + b + 1)
                        nc.vector.tensor_tensor(h[1][:, 4 * b:4 * b + 4, bass.ds(n * P, P)],
                                                turned[:, 2 * u + b].rearrange("p (c t) -> p c t", t=P),
                                                h[0][:, 4 * b:4 * b + 4, bass.ds(n * P, P)].bitcast(F32),
                                                ALU.subtract).then_inc(lo_done, 1)

        if pre_gain is not None:
            @block.tensor
            def _(pe):
                with pe.Fori(0, LOOPS) as i:
                    for u in range(2):
                        n = 2 * i + u
                        pe.wait_ge(x_normed, n + 1)
                        for b in range(2):
                            for c in range(4):
                                d = 4 * b + c
                                last = nc.tensor.transpose(turned[:, 2 * u + b, c * P:(c + 1) * P],
                                                           normed[:, u, d * P:(d + 1) * P], identity)
                            last.then_inc(transposed, 1)


def swiglu(nc, tag, h, w_gate, w_up, w_down, out):
    CH = D_FF // P
    GROUPS = CH // 2
    LOOPS = (GROUPS - 1) // 2
    START = 2 * NT + 1
    with Stage(nc, tag) as st:
        up_raw = st.sbuf("up_raw", [P, 2, 2, ND, P])
        up_hi = st.sbuf("up_hi", [P, 2, 2, ND, P], F32R)
        up_lo = st.sbuf("up_lo", [P, 2, 2, ND, P], F32R)
        down_raw = st.sbuf("down_raw", [P, 2, 2, HALF])
        down_hi = st.sbuf("down_hi", [P, 2, 2, HALF], F32R)
        down_lo = st.sbuf("down_lo", [P, 2, 2, HALF], F32R)
        a_hi = st.sbuf("a_hi", [P, 4, SEQ], F32R)
        a_lo = st.sbuf("a_lo", [P, 4, SEQ], F32R)
        product = st.sbuf("product", [P, 2, HALF])
        up_ps = st.psum("up_ps", [P, 2, 2, HALF])
        down_ps = st.psum("down_ps", [P, 4, HALF])
        up_loaded = [st.sem(f"up_loaded{u}") for u in range(2)]
        down_loaded = [st.sem(f"down_loaded{u}") for u in range(2)]
        up_rounded, up_split = st.sem("up_rounded"), st.sem("up_split")
        down_rounded, down_split = st.sem("down_rounded"), st.sem("down_split")
        up_summed, silu_done, multiplied = st.sem("up_summed"), st.sem("silu_done"), st.sem("multiplied")
        a_rounded, a_split = st.sem("a_rounded"), st.sem("a_split")
        down_summed, down_added = st.sem("down_summed"), st.sem("down_added")
        block = st.stack.enter_context(nc.Block())

        gate_cols = w_gate.rearrange("(d p) f -> p d f", p=P)
        up_cols = w_up.rearrange("(d p) f -> p d f", p=P)
        down_rows = w_down.rearrange("(c p) n -> p c n", p=P)

        def steps(engine, up, down):
            up(0, 0, 0)
            up(1, 1, 0)
            with engine.Fori(0, LOOPS) as i:
                for g in range(2):
                    up(4 * i + 2 * g + 2, (2 * g + 2) % 4, 2 * i + g + 1)
                    up(4 * i + 2 * g + 3, (2 * g + 3) % 4, 2 * i + g + 1)
                    down(2 * i + g, g)


        def is_first(c, n=1):
            return isinstance(c, int) and c < n

        @block.sync
        def _(sp):
            def load_up(c, u, free):
                if free is not None:
                    sp.wait_ge(up_split, free)
                for k, cols in enumerate((gate_cols, up_cols)):
                    sp.dma_start(up_raw[:, u, k], cols[:, :, bass.ds(c * P, P)]).then_inc(up_loaded[u], 16)

            def load_down(g, half, free):
                if free is not None:
                    sp.wait_ge(down_split, free)
                sp.dma_start(down_raw[:, half], down_rows[:, bass.ds(2 * g, 2), half * HALF:(half + 1) * HALF]).then_inc(down_loaded[half], 16)

            load_up(0, 0, None)
            load_up(1, 1, None)
            load_down(0, 0, None)
            load_down(0, 1, None)
            with sp.Fori(1, GROUPS) as g:
                load_up(2 * g, 0, 2 * g - 1)
                load_up(2 * g + 1, 1, 2 * g)
                load_down(g, 0, 2 * g - 1)
                load_down(g, 1, 2 * g)

        @block.scalar
        def _(act):
            def finish(c, q, g):
                for t in range(NH):
                    n = 2 * c + t
                    act.wait_ge(up_summed, n + 1)
                    if not is_first(c):
                        act.wait_ge(a_split, n - 1)
                    nc.scalar.activation(product[:, t], up_ps[:, t, 0], ACT.Silu).then_inc(silu_done, 1)
                    act.wait_ge(multiplied, n + 1)
                    act.wait_ge(down_added, START + 2 * NT * (g - 1))
                    nc.scalar.copy(a_hi[:, q, t * HALF:(t + 1) * HALF], product[:, t]).then_inc(a_rounded, 1)

            def round_down(g):
                for half in range(2):
                    act.wait_ge(down_loaded[half], 16 * (g + 1))
                    act.wait_ge(down_added, START + NT * (2 * g + half - 1))
                    nc.scalar.copy(down_hi[:, half], down_raw[:, half]).then_inc(down_rounded, 1)

            def up(c, q, g):
                u = q % 2
                act.wait_ge(up_loaded[u], 32 * (g + 1))
                if not is_first(c, 2):
                    act.wait_ge(up_summed, 2 * c - 2)
                nc.scalar.copy(up_hi[:, u], up_raw[:, u]).then_inc(up_rounded, 1)
                if not is_first(c):
                    finish(c - 1, (q - 1) % 4, g - (1 - u))
                if not is_first(c, 2) and u == 0:
                    round_down(g - 1)

            steps(act, up, lambda g, odd: None)
            finish(CH - 1, (CH - 1) % 4, GROUPS - 1)
            round_down(GROUPS - 1)

        @block.gpsimd
        def _(pool):
            def finish(c, q, g):
                for t in range(NH):
                    part = (slice(None), q, slice(t * HALF, (t + 1) * HALF))
                    pool.wait_ge(a_rounded, 2 * c + t + 1)
                    nc.gpsimd.tensor_tensor(a_lo[part], product[:, t], a_hi[part].bitcast(F32), ALU.subtract).then_inc(a_split, 1)

            def split_down(g):
                for half in range(2):
                    pool.wait_ge(down_rounded, 2 * g + half + 1)
                    nc.gpsimd.tensor_tensor(down_lo[:, half], down_raw[:, half], down_hi[:, half].bitcast(F32), ALU.subtract).then_inc(down_split, 1)

            def up(c, q, g):
                u = q % 2
                pool.wait_ge(up_rounded, c + 1)
                nc.gpsimd.tensor_tensor(up_lo[:, u], up_raw[:, u], up_hi[:, u].bitcast(F32), ALU.subtract).then_inc(up_split, 1)
                if not is_first(c):
                    finish(c - 1, (q - 1) % 4, g - (1 - u))
                if not is_first(c, 2) and u == 0:
                    split_down(g - 1)

            steps(pool, up, lambda g, odd: None)
            finish(CH - 1, (CH - 1) % 4, GROUPS - 1)
            split_down(GROUPS - 1)

        @block.vector
        def _(dve):
            nc.vector.nop().then_inc(down_added, 1)
            for t in range(NT):
                for half in range(2):
                    nc.vector.memset(out[:, t, half * HALF:(half + 1) * HALF], 0.0).then_inc(down_added, 1)

            def up(c, q, g):
                for t in range(NH):
                    n = 2 * c + t
                    dve.wait_ge(silu_done, n + 1)
                    nc.vector.tensor_tensor(product[:, t], product[:, t], up_ps[:, t, 1], ALU.mult).then_inc(multiplied, 1)

            def down(g, odd):
                for half in range(2):
                    for t in range(NT):
                        k = half * NT + t
                        dve.wait_ge(down_summed, 2 * NT * g + k + 1)
                        dve.wait_ge(down_added, START + 2 * NT * g + k)
                        to = out[:, t, half * HALF:(half + 1) * HALF]
                        nc.vector.tensor_tensor(to, to, down_ps[:, k % 4], ALU.add).then_inc(down_added, 1)

            steps(dve, up, down)
            down(GROUPS - 1, (GROUPS - 1) % 2)

        @block.tensor
        def _(pe):
            def up(c, q, g):
                u = q % 2
                pe.wait_ge(up_split, c + 1)
                for t in range(NH):
                    if not is_first(c):
                        pe.wait_ge(multiplied, 2 * c + t - 1)
                    for k in range(2):
                        for d in range(ND):
                            last = split_matmul(nc, up_ps[:, t, k], (up_hi[:, u, k, d], up_lo[:, u, k, d]),
                                                tuple(part[:, d, t * HALF:(t + 1) * HALF] for part in h), d == 0, d == ND - 1)
                    last.then_inc(up_summed, 1)

            def down(g, odd):
                pe.wait_ge(a_split, 4 * g + 4)
                for half in range(2):
                    pe.wait_ge(down_split, 2 * g + half + 1)
                    for t in range(NT):
                        k = half * NT + t
                        pe.wait_ge(down_added, START + 2 * NT * g + k - 3)
                        for j in range(2):
                            slot = 2 * odd + j
                            last = split_matmul(nc, down_ps[:, k % 4], (a_hi[:, slot, t * P:(t + 1) * P], a_lo[:, slot, t * P:(t + 1) * P]),
                                                (down_hi[:, half, j], down_lo[:, half, j]), j == 0, j == 1)
                        last.then_inc(down_summed, 1)

            steps(pe, up, down)
            down(GROUPS - 1, (GROUPS - 1) % 2)


GDN_HEADS, GDN_DK = 4, 128
CONV = 4
RWKV_BLOCKS = 4
GDN_QK, GDN_V, GDN_Z = 0, 1024, 1536
GDN_SMALL = 2048
RWKV_COLS = 2056
RWKV_W = 512
L2_EPS = 1e-6

S_Q, S_K, S_V, S_INCL, S_STRICT, S_RWKV = 0, 8, 16, 20, 24, 28
R_KK, R_R, R_K, R_B, R_V, R_SLOTS = 0, 1, 2, 3, 4, 5
SLOTS = S_RWKV + R_SLOTS * RWKV_BLOCKS
COLS = 16
C_GDN = SLOTS * P
TILE_W = SLOTS * P + COLS


class Steps:

    def __init__(self, sem, names):
        self.sem, self.names, self.next = sem, names.split(), 0

    def open(self, engine):
        engine.nop().then_inc(self.sem, len(self.names))

    def done(self, instruction, name):
        assert name == self.names[self.next], (name, self.names[self.next])
        self.next = (self.next + 1) % len(self.names)
        instruction.then_inc(self.sem, 1)

    def wait(self, engine, name, turn):
        engine.wait_ge(self.sem, len(self.names) * (turn + 1) + self.names.index(name) + 1)


def stream_weights(nc, pool, gate, w_raw, w_hi, w_lo, w_loaded, w_rounded, w_split, projected, blocks):
    def split(k, s, first):
        pool.wait_ge(w_loaded[s], 16 * (k // 2 + 1) if isinstance(k, int) else 16 * first)
        if not (isinstance(k, int) and k < 2):
            pool.wait_ge(projected, k - 1)
        nc.gpsimd.tensor_tensor(gate[:, 0:1], gate[:, 1:2], gate[:, 1:2], ALU.add)
        nc.gpsimd.tensor_copy(w_hi[:, s], w_raw[:, s]).then_inc(w_rounded, 1)
        pool.wait_ge(w_rounded, k + 2)
        nc.gpsimd.tensor_tensor(w_lo[:, s], w_raw[:, s], w_hi[:, s].bitcast(F32), ALU.subtract).then_inc(w_split, 1)

    nc.gpsimd.memset(gate, 0.0).then_inc(w_rounded, 1)
    pool.wait_ge(w_rounded, 1)
    split(0, 0, 1)
    split(1, 1, 1)
    with pool.Fori(1, blocks // 2) as i:
        split(2 * i, 0, i + 1)
        split(2 * i + 1, 1, i + 1)
    if blocks % 2:
        split(blocks - 1, 0, None)


def gdn_projection(nc, h, w_in, conv_w, a_log, dt_bias, masks, scratch, z_gate):
    with Stage(nc, "gp") as st:
        w_raw = st.sbuf("w_raw", [P, 2, ND, P])
        w_hi = st.sbuf("w_hi", [P, 2, ND, P], F32R)
        w_lo = st.sbuf("w_lo", [P, 2, ND, P], F32R)
        x_ext = st.sbuf("x_ext", [P, 2, 4 + SEQ])
        conv = st.sbuf("conv", [P, 2, SEQ])
        act_out = st.sbuf("act_out", [P, 2, SEQ])
        square = st.sbuf("square", [P, SEQ])
        root = st.sbuf("root", [P, SEQ])
        unit = st.sbuf("unit", [P, 2, SEQ])
        scaled = st.sbuf("scaled", [P, 2, SEQ])
        rows = st.sbuf("rows", [P, 8, SEQ])
        taps = st.sbuf("taps", [P, CONV, 12])
        scale_col = st.sbuf("scale_col", [P, 8])
        eps = st.sbuf("eps", [P, 1])
        gate = st.sbuf("gate", [P, 2])
        mask = st.sbuf("mask", [P, 4, P])
        a_row = st.sbuf("a_row", [P, GDN_HEADS])
        dt_row = st.sbuf("dt_row", [P, GDN_HEADS])
        s = st.sbuf("small", [P, 12, NT, GDN_HEADS])
        gb = st.sbuf("gb", [P, NT, 8])
        gc_rows = st.sbuf("gc_rows", [P, 4, P])
        spread = st.sbuf("spread", [P, 2, 4, P])
        diag = st.sbuf("diag", [P, 4, P])
        gaps = st.sbuf("gaps", [P, 4, P])
        decay = st.sbuf("decay", [P, 4, P])
        decays = st.sbuf("decays", [P, 8, P])
        exps = st.sbuf("exps", [P, 16])
        cols = st.sbuf("cols", [P, 16])
        proj = st.psum("proj", [P, 2, 2, HALF])
        sums = st.psum("sums", [P, 2, HALF])
        row_ps = st.psum("row_ps", [P, 2, HALF])

        setup, ready = st.sem("setup"), st.sem("ready")
        w_loaded = [st.sem(f"w_loaded{u}") for u in range(2)]
        w_rounded, w_split, projected = st.sem("w_rounded"), st.sem("w_split"), st.sem("projected")
        copied, tapped, convolved, silu_done = st.sem("copied"), st.sem("tapped"), st.sem("convolved"), st.sem("silu_done")
        squared, summed, rooted = st.sem("squared"), st.sem("summed"), st.sem("rooted")
        unit_ready, scaled_ready = st.sem("unit_ready"), st.sem("scaled_ready")
        turned, small_dve, small_act = st.sem("turned"), st.sem("small_dve"), st.sem("small_act")
        spread_ready, rows_summed, rows_copied = st.sem("spread_ready"), st.sem("rows_summed"), st.sem("rows_copied")
        col_step, gaps_ready, decayed, decays_ready = st.sem("col_step"), st.sem("gaps_ready"), st.sem("decayed"), st.sem("decays_ready")
        exps_done = st.sem("exps_done")
        act_stored, decay_stored = [st.sem(f"act_stored{u}") for u in range(2)], st.sem("decay_stored")
        unit_stored, scaled_stored = [st.sem(f"unit_stored{u}") for u in range(2)], [st.sem(f"scaled_stored{u}") for u in range(2)]
        block = st.stack.enter_context(nc.Block())

        w_cols = w_in.rearrange("(d p) f -> p d f", p=P)
        tiles = scratch.rearrange("c p w -> p c w")
        K_V, K_Z, K_QK, BLOCKS = 1, 5, 9, 17
        SETUP = 16 * 4

        def in_pairs(engine, body, n, base):
            with engine.Fori(0, n // 2) as i:
                for u in range(2):
                    body(2 * i + u, u, i)

        def lagged(engine, first, second):
            first(0, 0, 0)
            with engine.Fori(0, 3) as i:
                for u in range(2):
                    first(2 * i + u + 1, (u + 1) % 2, i + u)
                    second(2 * i + u, u, i)
            first(7, 1, 3)
            second(6, 0, 3)
            second(7, 1, 3)

        @block.sync
        def _(sp):
            for stored in act_stored + unit_stored + scaled_stored:
                sp.nop().then_inc(stored, 16)
            sp.nop().then_inc(decay_stored, 32)
            sp.dma_start(taps[:], conv_w).then_inc(setup, 16)
            sp.dma_start(mask[:], masks[:, 0:4]).then_inc(setup, 16)
            sp.dma_start(a_row[:], row_of(a_log)).then_inc(setup, 16)
            sp.dma_start(dt_row[:], row_of(dt_bias)).then_inc(setup, 16)

            def load(col, s_, split):
                if split is not None:
                    sp.wait_ge(w_split, split)
                sp.dma_start(w_raw[:, s_], w_cols[:, :, bass.ds(col, P)]).then_inc(w_loaded[s_], 16)

            load(GDN_SMALL, 0, None)
            load(GDN_V, 1, None)

            def decays_out(c):
                sp.wait_ge(decays_ready, c + 1)
                sp.dma_start(scratch[bass.ds(c, 1), :, S_INCL * P:S_RWKV * P].rearrange("a p w -> p (a w)"),
                             decays[:].rearrange("p s t -> p (s t)")).then_inc(decay_stored, 16)
                sp.dma_start(scratch[bass.ds(c, 1), :, C_GDN:C_GDN + 16].rearrange("a p w -> p (a w)"), cols[:]).then_inc(decay_stored, 16)

            def v_step(j, u, i):
                load(GDN_V + (j + 1) * P, u, j + 1)
                decays_out(j)
                sp.wait_ge(silu_done, j + 1)
                sp.dma_start(tiles[:, :, bass.ds((S_V + j) * P, P)], act_out[:, u].rearrange("p (c t) -> p c t", t=P)).then_inc(act_stored[u], 16)

            def z_step(j, u, i):
                load(((GDN_Z + (j + 1) * P) % GDN_SMALL), u, j + 5)
                decays_out(j + 4)
                sp.wait_ge(silu_done, j + 5)
                sp.dma_start(z_gate[bass.ds(j, 1)].rearrange("a p t -> p (a t)"), act_out[:, u]).then_inc(act_stored[u], 16)

            in_pairs(sp, v_step, 4, K_V)
            for j in range(4):
                z_step(j, j % 2, j // 2)

            def qk_load(b, u, i):
                load((b + 1) * P, (u + 0) % 2, b + K_QK)

            def qk_store(b, u, i):
                sp.wait_ge(unit_ready, b + 2)
                sp.dma_start(tiles[:, :, bass.ds(2 * b * P, P)], unit[:, u].rearrange("p (c t) -> p c t", t=P)).then_inc(unit_stored[u], 16)
                sp.wait_ge(scaled_ready, b + 1)
                sp.dma_start(tiles[:, :, bass.ds((2 * b + 1) * P, P)], scaled[:, u].rearrange("p (c t) -> p c t", t=P)).then_inc(scaled_stored[u], 16)

            lagged(sp, lambda b, u, i: None if isinstance(b, int) and b == 7 else qk_load(b, u, i), qk_store)
            for u in range(2):
                sp.wait_ge(act_stored[u], 16 * 5)
                sp.wait_ge(unit_stored[u], 16 * 5)
                sp.wait_ge(scaled_stored[u], 16 * 5)
            sp.wait_ge(decay_stored, 32 * (NT + 1))

        @block.gpsimd
        def _(pool):
            stream_weights(nc, pool, gate[:], w_raw, w_hi, w_lo, w_loaded, w_rounded, w_split, projected, BLOCKS)

        @block.tensor
        def _(pe):
            def project(k, s_):
                pe.wait_ge(w_split, k + 1)
                if not (isinstance(k, int) and k < 2):
                    pe.wait_ge(copied, k)
                for t in range(NH):
                    for d in range(ND):
                        last = split_matmul(nc, proj[:, s_, t], (w_hi[:, s_, d], w_lo[:, s_, d]),
                                            tuple(part[:, d, t * HALF:(t + 1) * HALF] for part in h), d == 0, d == ND - 1)
                last.then_inc(projected, 1)

            def sum_rows(c):
                pe.wait_ge(spread_ready, 2 * c + 2)
                pe.wait_ge(rows_copied, 2 * c + 1)
                for n in range(2):
                    last = nc.tensor.matmul(row_ps[:, n], mask[:, 1], spread[:, n].rearrange("p n t -> p (n t)"), start=True, stop=True)
                last.then_inc(rows_summed, 1)

            project(0, 0)
            pe.wait_ge(setup, SETUP)
            pe.wait_ge(copied, 2)
            for c in range(NT):
                last = nc.tensor.transpose(sums[:, c // 4, (c % 4) * P:(c % 4 + 1) * P], x_ext[:, 0, 4 + c * P:4 + (c + 1) * P], mask[:, 0])
            last.then_inc(turned, 1)

            def vz_step(j, u, i):
                project(j + 1, (u + 1) % 2)
                sum_rows(j)

            in_pairs(pe, vz_step, 8, K_V)

            def sum_squares(b, u, i):
                pe.wait_ge(squared, b + 1)
                for t in range(NH):
                    pe.wait_ge(rooted, 2 * b + 1)
                    last = nc.tensor.matmul(sums[:, t], mask[:, 1], square[:, t * HALF:(t + 1) * HALF], start=True, stop=True)
                last.then_inc(summed, 1)

            lagged(pe, lambda b, u, i: project(b + K_QK, (u + 1) % 2), sum_squares)

        @block.scalar
        def _(act):
            act.wait_ge(setup, SETUP)
            act.wait_ge(ready, 1)

            def copy_block(k, s_):
                act.wait_ge(projected, k + 1)
                nc.scalar.copy(x_ext[:, s_, 4:], proj[:, s_].rearrange("p n t -> p (n t)")).then_inc(copied, 1)

            copy_block(0, 0)
            act.wait_ge(small_dve, 1)
            nc.scalar.activation(s[:, 0], gb[:, :, 0:4], ACT.Sigmoid).then_inc(small_act, 1)
            nc.scalar.activation(a_row[:], a_row[:], ACT.Exp).then_inc(small_act, 1)
            act.wait_ge(small_dve, 4)
            nc.scalar.activation(s[:, 4], s[:, 3], ACT.Exp, scale=-1.0).then_inc(small_act, 1)
            act.wait_ge(small_dve, 5)
            nc.scalar.activation(s[:, 6], s[:, 5], ACT.Ln).then_inc(small_act, 1)

            def rows_of(c):
                act.wait_ge(rows_summed, c + 1)
                nc.scalar.copy(gc_rows[:], row_ps[:, 0].rearrange("p (n t) -> p n t", t=P)).then_inc(rows_copied, 1)
                nc.scalar.copy(rows[:, 4:8, bass.ds(c * P, P)], row_ps[:, 1].rearrange("p (n t) -> p n t", t=P)).then_inc(rows_copied, 1)
                act.wait_ge(rows_copied, 2 * c + 3)
                nc.scalar.activation(rows[:, 0:4, bass.ds(c * P, P)], gc_rows[:], ACT.Exp)
                act.wait_ge(gaps_ready, c + 1)
                nc.scalar.activation(decay[:], gaps[:], ACT.Exp).then_inc(decayed, 1)
                nc.scalar.activation(exps[:, 0:12], exps[:, 0:12], ACT.Exp).then_inc(exps_done, 1)

            def tap_last(b, s_, blk, used):
                nc.scalar.activation(conv[:, s_], x_ext[:, s_, 4:], ACT.Copy, scale=taps[:, CONV - 1, bass.ds(blk, 1)]).then_inc(tapped, 1)

            def v_step(j, u, i):
                s_ = (u + 1) % 2
                copy_block(j + K_V, s_)
                act.wait_ge(copied, j + K_V + 2)
                tap_last(j, s_, j + 8, None)
                rows_of(j)
                act.wait_ge(convolved, 3 * j + 3)
                act.wait_ge(act_stored[u], 16 * (i + 1))
                nc.scalar.activation(act_out[:, u], conv[:, s_], ACT.Silu).then_inc(silu_done, 1)

            def z_step(j, u, i):
                s_ = (u + 1) % 2
                copy_block(j + K_Z, s_)
                rows_of(j + 4)
                act.wait_ge(copied, j + K_Z + 2)
                act.wait_ge(act_stored[u], 16 * (i + 3))
                nc.scalar.activation(act_out[:, u], x_ext[:, s_, 4:], ACT.Silu).then_inc(silu_done, 1)

            in_pairs(act, v_step, 4, K_V)
            in_pairs(act, z_step, 4, K_Z)

            def qk_first(b, u, i):
                s_ = (u + 1) % 2
                copy_block(b + K_QK, s_)
                act.wait_ge(copied, b + K_QK + 2)
                tap_last(b, s_, b, None)
                act.wait_ge(convolved, 3 * (b + 4) + 3)
                act.wait_ge(act_stored[u], 16 * 5)
                if not (isinstance(b, int) and b < 1):
                    act.wait_ge(unit_ready, b)
                nc.scalar.activation(act_out[:, u], conv[:, s_], ACT.Silu).then_inc(silu_done, 1)
                act.wait_ge(silu_done, b + 9)
                if not (isinstance(b, int) and b < 1):
                    act.wait_ge(summed, b)
                nc.scalar.activation(square[:], act_out[:, u], ACT.Square).then_inc(squared, 1)

            def qk_second(b, u, i):
                act.wait_ge(summed, b + 1)
                act.wait_ge(unit_ready, b + 1)
                nc.scalar.activation(root[:], sums[:].rearrange("p n t -> p (n t)"), ACT.Ln, bias=eps[:]).then_inc(rooted, 1)
                act.wait_ge(rooted, 2 * b + 2)
                nc.scalar.activation(root[:], root[:], ACT.Exp, scale=-0.5).then_inc(rooted, 1)

            lagged(act, qk_first, qk_second)

        @block.vector
        def _(dve):
            nc.vector.memset(eps[:], L2_EPS)
            nc.vector.memset(scale_col[:, 0:4], GDN_DK ** -0.5)
            nc.vector.memset(scale_col[:, 4:8], 1.0)
            nc.vector.memset(x_ext[:, :, 0:4], 0.0).then_inc(ready, 1)
            for free in (rows_copied, copied, rooted, unit_ready):
                nc.vector.nop().then_inc(free, 1)
            dve.wait_ge(setup, SETUP)
            dve.wait_ge(ready, 1)
            step = [0]

            def small(ins):
                ins.then_inc(small_dve, 1)
                step[0] += 1
                dve.wait_ge(small_dve, step[0])

            dt = dt_row[:].rearrange("p (a n) -> p a n", a=1).broadcast_to([P, NT, GDN_HEADS])
            ea = a_row[:].rearrange("p (a n) -> p a n", a=1).broadcast_to([P, NT, GDN_HEADS])
            dve.wait_ge(turned, 1)
            small(nc.vector.tensor_copy(gb[:], sums[:].rearrange("p n (c t) -> p (n c) t", t=P)[:, :, 0:8]))
            small(nc.vector.tensor_tensor(s[:, 1], gb[:, :, 4:8], dt, ALU.add))
            small(nc.vector.tensor_scalar(s[:, 2], s[:, 1], -1.0, None, ALU.mult))
            small(nc.vector.tensor_tensor(s[:, 3], s[:, 1], s[:, 2], ALU.max))
            dve.wait_ge(small_act, 3)
            small(nc.vector.tensor_scalar(s[:, 5], s[:, 4], 1.0, None, ALU.add))
            small(nc.vector.tensor_scalar(s[:, 7], s[:, 5], 1.0, None, ALU.is_equal))
            small(nc.vector.scalar_tensor_tensor(s[:, 8], s[:, 5], -1.0, s[:, 7], ALU.add, ALU.add))
            small(nc.vector.reciprocal(s[:, 9], s[:, 8]))
            dve.wait_ge(small_act, 4)
            small(nc.vector.tensor_tensor(s[:, 8], s[:, 6], s[:, 7], ALU.add))
            small(nc.vector.tensor_tensor(s[:, 8], s[:, 8], s[:, 9], ALU.mult))
            small(nc.vector.tensor_tensor(s[:, 8], s[:, 8], s[:, 4], ALU.mult))
            small(nc.vector.scalar_tensor_tensor(s[:, 10], s[:, 1], 0.0, s[:, 8], ALU.max, ALU.add))
            small(nc.vector.scalar_tensor_tensor(s[:, 10], s[:, 10], -1.0, ea, ALU.mult, ALU.mult))
            small(nc.vector.tensor_scalar(s[:, 11], s[:, 0], -1.0, None, ALU.mult))

            def over_heads(n):
                return mask[:, n:n + 1].broadcast_to([P, GDN_HEADS, P])

            def spread_rows(c):
                for n, (m, of) in enumerate(((2, 10), (0, 11))):
                    nc.vector.tensor_tensor(spread[:, n], over_heads(m), per_head(s[:, of, bass.ds(c, 1), :]), ALU.mult).then_inc(spread_ready, 1)

            def per_head(ap):
                return ap.rearrange("p a n -> p n a").broadcast_to([P, GDN_HEADS, P])

            def decays_of(c):
                g_rows = gc_rows[:]
                dve.wait_ge(rows_copied, 2 * c + 2)
                nc.vector.tensor_tensor(diag[:], g_rows, over_heads(0), ALU.mult).then_inc(col_step, 1)
                dve.wait_ge(col_step, 6 * c + 1)
                nc.vector.tensor_reduce(exps[:, 0:4], diag[:], mybir.AxisListType.X, ALU.add).then_inc(col_step, 1)
                nc.vector.tensor_copy(exps[:, 8:12], g_rows[:, :, P - 1]).then_inc(col_step, 1)
                dve.wait_ge(col_step, 6 * c + 3)
                nc.vector.tensor_tensor(gaps[:], g_rows, exps[:, 0:4].rearrange("p (n a) -> p n a", a=1).broadcast_to([P, GDN_HEADS, P]), ALU.subtract).then_inc(col_step, 1)
                nc.vector.tensor_tensor(exps[:, 4:8], exps[:, 8:12], exps[:, 0:4], ALU.subtract).then_inc(col_step, 1)
                dve.wait_ge(col_step, 6 * c + 5)
                nc.vector.tensor_scalar(exps[:, 4:8], exps[:, 4:8], 0.0, None, ALU.min).then_inc(col_step, 1)
                nc.vector.tensor_scalar(gaps[:], gaps[:], 0.0, None, ALU.min).then_inc(gaps_ready, 1)
                dve.wait_ge(exps_done, c + 1)
                dve.wait_ge(decay_stored, 32 * (c + 1))
                beta = s[:, 0, bass.ds(c, 1), :].rearrange("p a n -> p (a n)")
                minus_beta = s[:, 11, bass.ds(c, 1), :].rearrange("p a n -> p (a n)")
                nc.vector.tensor_copy(cols[:, 0:4], beta)
                nc.vector.tensor_tensor(cols[:, 4:8], exps[:, 0:4], minus_beta, ALU.mult)
                nc.vector.tensor_copy(cols[:, 8:16], exps[:, 4:12])
                nc.vector.tensor_tensor(decays[:, 0:4], decay[:], over_heads(2), ALU.mult)
                nc.vector.tensor_tensor(decays[:, 4:8], decay[:], over_heads(3), ALU.mult).then_inc(decays_ready, 1)

            def convolve(n, s_, blk):
                dve.wait_ge(tapped, n + 1)
                for j in range(CONV - 1):
                    if j:
                        dve.wait_ge(convolved, 3 * n + j)
                    nc.vector.scalar_tensor_tensor(conv[:, s_], x_ext[:, s_, j + 1:j + 1 + SEQ], taps[:, j, bass.ds(blk, 1)], conv[:, s_],
                                                   ALU.mult, ALU.add).then_inc(convolved, 1)

            def v_step(j, u, i):
                spread_rows(j)
                convolve(j, (u + 1) % 2, j + 8)
                decays_of(j)

            def z_step(j, u, i):
                spread_rows(j + 4)
                decays_of(j + 4)

            in_pairs(dve, v_step, 4, K_V)
            in_pairs(dve, z_step, 4, K_Z)

            def qk_first(b, u, i):
                convolve(b + 4, (u + 1) % 2, b)

            def qk_second(b, u, i):
                dve.wait_ge(rooted, 2 * b + 3)
                dve.wait_ge(unit_stored[u], 16 * (i + 1))
                dve.wait_ge(scaled_stored[u], 16 * (i + 1))
                nc.vector.scalar_tensor_tensor(unit[:, u], act_out[:, u], scale_col[:, bass.ds(b, 1)], root[:], ALU.mult, ALU.mult).then_inc(unit_ready, 1)
                dve.wait_ge(unit_ready, b + 2)
                nc.vector.tensor_tensor(scaled[:, u], unit[:, u], rows[:, bass.ds(b, 1), :].rearrange("p a t -> p (a t)"), ALU.mult).then_inc(scaled_ready, 1)

            lagged(dve, qk_first, qk_second)


EXP_HALF = 0.6065306597126334
M_MU, M_W0, M_A0, M_KK, M_KA, M_RK, M_GNW, M_GNB, M_COLS = 0, 14, 18, 22, 26, 30, 34, 38, 42
LORA_WA, LORA_G = 12, 13


def rwkv_projection(nc, h, w_in, w2, a2, g2, params, masks, scratch, gate_out, bonus_out, carry):
    with Stage(nc, "rp") as st:
        w_raw = st.sbuf("w_raw", [P, 2, ND, P])
        w_hi = st.sbuf("w_hi", [P, 2, ND, P], F32R)
        w_lo = st.sbuf("w_lo", [P, 2, ND, P], F32R)
        gate = st.sbuf("gate", [P, 2])
        wa2 = st.sbuf("wa2", [P, RWKV_W])
        g2_sb = st.sbuf("g2", [P, RWKV_W])
        col = st.sbuf("col", [P, M_COLS])
        one_less_ka = st.sbuf("one_less_ka", [P, 4])
        head_ones = st.sbuf("head_ones", [P, P])
        eps = st.sbuf("eps", [P, 1])
        reset = st.sbuf("reset", [P, NT, P])
        sig = st.sbuf("sig", [P, 4, SEQ])
        rate = st.sbuf("rate", [P, 4, SEQ])
        kr_x, r_x, v_x = (st.sbuf(n, [P, 4 + SEQ]) for n in ("kr_x", "r_x", "v_x"))
        k = st.sbuf("k", [P, SEQ])
        kk = st.sbuf("kk", [P, SEQ])
        r = st.sbuf("r", [P, SEQ])
        sq = st.sbuf("sq", [P, SEQ])
        cs = st.sbuf("cs", [P, NT, P])
        cm = st.sbuf("cm", [P, NT, P])
        before = st.sbuf("before", [P, NT, P])
        grow = st.sbuf("grow", [P, NT, P])
        shrink = st.sbuf("shrink", [P, NT, P])
        out = st.sbuf("out", [P, NT, R_SLOTS, P])
        bonus = st.sbuf("bonus", [P, SEQ])
        ends = st.sbuf("ends", [P, NT])
        proj = st.psum("proj", [P, 2, 2, HALF])
        sums = st.psum("sums", [P, 4, HALF])

        setup, ready, setup_v, lora_g = st.sem("setup"), st.sem("ready"), st.sem("setup_v"), st.sem("lora_g")
        w_loaded = [st.sem(f"w_loaded{u}") for u in range(2)]
        w_rounded, w_split, projected, copied = st.sem("w_rounded"), st.sem("w_split"), st.sem("projected"), st.sem("copied")
        lora_in, lora_summed, lora_read = st.sem("lora_in"), st.sem("lora_summed"), st.sem("lora_read")
        gate_ready, gate_stored = st.sem("gate_ready"), st.sem("gate_stored")
        out_stored, bonus_stored = st.sem("out_stored"), st.sem("bonus_stored")
        dve_steps = Steps(st.sem("dve_steps"), "kr_diff kr kk_raw cs cm before k_factor k r_diff r rk kk "
                          "kk_out r_out k_out b_pre b_out v_diff v_out bonus ends ends_next")
        act_steps = Steps(st.sem("act_steps"), "kr_copied kk_squared r_copied shrink grow before log_norm norm v_copied carry")
        pe_steps = Steps(st.sem("pe_steps"), "norm_summed bonus_summed")
        block = st.stack.enter_context(nc.Block())
        w_cols = w_in.rearrange("(d p) f -> p d f", p=P)
        tiles = scratch.rearrange("c p w -> p c w")
        BLOCKS = 14
        kr_lora, g_lora = k, kk

        @block.sync
        def _(sp):
            sp.nop().then_inc(out_stored, 16)
            sp.nop().then_inc(bonus_stored, 16)
            sp.nop().then_inc(gate_stored, 16)
            sp.dma_start(col[:], params).then_inc(setup, 16)
            sp.dma_start(wa2[0:64], w2).then_inc(setup, 16)
            sp.dma_start(wa2[64:128], a2).then_inc(setup, 16)
            sp.dma_start(g2_sb[:], g2).then_inc(setup, 16)
            sp.dma_start(head_ones[:], masks[:, 4]).then_inc(setup, 16)

            def load(kk_, s, start):
                if not (isinstance(kk_, int) and kk_ < 2):
                    sp.wait_ge(w_split, kk_ - 1)
                sp.dma_start(w_raw[:, s], w_cols[:, :, bass.ds(start, P)]).then_inc(w_loaded[s], 16)

            load(0, 0, RWKV_COLS + LORA_WA * P)
            load(1, 1, RWKV_COLS + LORA_G * P)
            load(2, 0, RWKV_COLS + RWKV_W)
            load(3, 1, RWKV_COLS)
            for b in range(4):
                sp.wait_ge(gate_ready, b + 1)
                sp.dma_start(gate_out[b], sq[:]).then_inc(gate_stored, 16)

            def store(b):
                dve_steps.wait(sp, "v_out", b)
                sp.dma_start(tiles[:, :, bass.ds((S_RWKV + R_SLOTS * b) * P, R_SLOTS * P)],
                             out[:].rearrange("p c s t -> p c (s t)")).then_inc(out_stored, 16)
                dve_steps.wait(sp, "bonus", b)
                sp.dma_start(bonus_out[bass.ds(b, 1)].rearrange("a p t -> p (a t)"), bonus[:]).then_inc(bonus_stored, 16)

            for b in range(4):
                n = 3 * b + 4
                load(n, n % 2, RWKV_COLS + 2 * RWKV_W + b * P)
                if b < 3:
                    load(n + 1, (n + 1) % 2, RWKV_COLS + RWKV_W + (b + 1) * P)
                    load(n + 2, n % 2, RWKV_COLS + (b + 1) * P)
                store(b)
            sp.wait_ge(out_stored, 16 * 5)
            sp.wait_ge(bonus_stored, 16 * 5)
            sp.wait_ge(gate_stored, 16 * 5)

        @block.gpsimd
        def _(pool):
            stream_weights(nc, pool, gate[:], w_raw, w_hi, w_lo, w_loaded, w_rounded, w_split, projected, BLOCKS)

        @block.tensor
        def _(pe):
            pe_steps.open(pe)

            def project(n, s):
                pe.wait_ge(w_split, n + 1)
                if not (isinstance(n, int) and n < 2):
                    pe.wait_ge(copied, n)
                for t in range(NH):
                    for d in range(ND):
                        last = split_matmul(nc, proj[:, s, t], (w_hi[:, s, d], w_lo[:, s, d]),
                                            tuple(part[:, d, t * HALF:(t + 1) * HALF] for part in h), d == 0, d == ND - 1)
                last.then_inc(projected, 1)

            project(0, 0)
            project(1, 1)
            pe.wait_ge(setup, 16 * 5)
            for b in range(4):
                cols = slice(b * P, (b + 1) * P)
                pe.wait_ge(lora_in, 2)
                if b:
                    pe.wait_ge(lora_read, 3 * b)
                for t in range(NH):
                    tok = slice(t * HALF, (t + 1) * HALF)
                    nc.tensor.matmul(sums[:, t], wa2[0:64, cols], kr_lora[0:64, tok], start=True, stop=True)
                    last = nc.tensor.matmul(sums[:, 2 + t], wa2[64:128, cols], kr_lora[64:128, tok], start=True, stop=True)
                last.then_inc(lora_summed, 1)
                pe.wait_ge(lora_in, 3)
                pe.wait_ge(lora_read, 3 * b + 1)
                for t in range(NH):
                    last = nc.tensor.matmul(sums[:, t], g2_sb[:, cols], g_lora[:, t * HALF:(t + 1) * HALF], start=True, stop=True)
                last.then_inc(lora_summed, 1)

            def over_heads(what, b, bank, prev):
                for t in range(NH):
                    last = nc.tensor.matmul(sums[:, bank + t], head_ones[:], sq[:, t * HALF:(t + 1) * HALF], start=True, stop=True)
                pe_steps.done(last, what)

            def heads(b, s, n):
                project(n, s)
                project(n + 1, 1 - s)
                act_steps.wait(pe, "kk_squared", b)
                act_steps.wait(pe, "log_norm", b - 1)
                over_heads("norm_summed", b, 0, None)
                project(n + 2, s)
                dve_steps.wait(pe, "rk", b)
                dve_steps.wait(pe, "bonus", b - 1)
                over_heads("bonus_summed", b, 2, None)

            with pe.Fori(0, 2) as i:
                heads(2 * i, 0, 6 * i + 2)
                heads(2 * i + 1, 1, 6 * i + 5)

        @block.scalar
        def _(act):
            act_steps.open(act)
            act.wait_ge(setup, 16 * 5)
            act.wait_ge(ready, 1)

            def copy_block(n, to, s):
                act.wait_ge(projected, n + 1)
                return nc.scalar.copy(to[:, 4:], proj[:, s].rearrange("p n t -> p (n t)"))

            copy_block(0, kr_x, 0).then_inc(copied, 1)
            copy_block(1, r_x, 1).then_inc(copied, 1)
            act.wait_ge(lora_in, 1)
            nc.scalar.activation(kr_lora[0:64], k[0:64], ACT.Tanh).then_inc(lora_in, 1)
            act.wait_ge(lora_in, 2)
            act.wait_ge(lora_g, 1)
            nc.scalar.activation(g_lora[:], kk[:], ACT.Sigmoid).then_inc(lora_in, 1)
            for b in range(4):
                act.wait_ge(lora_summed, 2 * b + 1)
                nc.scalar.activation(sig[:, b], sums[:, 0:2].rearrange("p n t -> p (n t)"), ACT.Sigmoid, bias=col[:, M_W0 + b:M_W0 + b + 1]).then_inc(lora_read, 1)
                nc.scalar.activation(rate[:, b], sums[:, 2:4].rearrange("p n t -> p (n t)"), ACT.Sigmoid, bias=col[:, M_A0 + b:M_A0 + b + 1]).then_inc(lora_read, 1)
                act.wait_ge(lora_summed, 2 * b + 2)
                act.wait_ge(gate_stored, 16 * (b + 1))
                nc.scalar.copy(sq[:], sums[:, 0:2].rearrange("p n t -> p (n t)")).then_inc(lora_read, 1)
                act.wait_ge(lora_read, 3 * b + 3)
                nc.scalar.nop().then_inc(gate_ready, 1)
            act.wait_ge(gate_stored, 16 * 5)

            def heads(b, s, n):
                dve_steps.wait(act, "kr", b - 1)
                ins = copy_block(n, kr_x, s)
                act_steps.done(ins, "kr_copied")
                act_steps.wait(act, "kr_copied", b)
                nc.scalar.nop().then_inc(copied, 1)
                dve_steps.wait(act, "kk_raw", b)
                pe_steps.wait(act, "bonus_summed", b - 1)
                act_steps.done(nc.scalar.activation(sq[:], kk[:], ACT.Square), "kk_squared")
                dve_steps.wait(act, "r", b - 1)
                ins = copy_block(n + 1, r_x, 1 - s)
                act_steps.done(ins, "r_copied")
                act_steps.wait(act, "r_copied", b)
                nc.scalar.nop().then_inc(copied, 1)
                dve_steps.wait(act, "cm", b)
                act_steps.done(nc.scalar.activation(shrink[:], cm[:], ACT.Exp, scale=-EXP_HALF), "shrink")
                act_steps.done(nc.scalar.activation(grow[:], cm[:], ACT.Exp, scale=EXP_HALF), "grow")
                dve_steps.wait(act, "before", b)
                act_steps.done(nc.scalar.activation(before[:], before[:], ACT.Exp, scale=-EXP_HALF), "before")
                pe_steps.wait(act, "norm_summed", b)
                act.wait_ge(bonus_stored, 16 * (b + 1))
                act_steps.done(nc.scalar.activation(bonus[:], sums[:, 0:2].rearrange("p n t -> p (n t)"), ACT.Ln, bias=eps[:]), "log_norm")
                act_steps.wait(act, "log_norm", b)
                act_steps.done(nc.scalar.activation(bonus[:], bonus[:], ACT.Exp, scale=-0.5), "norm")
                dve_steps.wait(act, "v_out", b - 1)
                ins = copy_block(n + 2, v_x, s)
                act_steps.done(ins, "v_copied")
                act_steps.wait(act, "v_copied", b)
                nc.scalar.nop().then_inc(copied, 1)
                dve_steps.wait(act, "ends_next", b)
                act_steps.done(nc.scalar.activation(carry[:, :, bass.ds(b, 1)].rearrange("p c a -> p (c a)"), ends[:], ACT.Exp, scale=-EXP_HALF), "carry")

            with act.Fori(0, 2) as i:
                heads(2 * i, 0, 6 * i + 2)
                heads(2 * i + 1, 1, 6 * i + 5)

        @block.vector
        def _(dve):
            dve_steps.open(dve)
            nc.vector.nop().then_inc(copied, 1)
            nc.vector.memset(eps[:], L2_EPS)
            nc.vector.memset(reset[:], 1.0).then_inc(setup_v, 1)
            dve.wait_ge(setup_v, 1)
            nc.vector.memset(reset[:, :, 0:1], 0.0).then_inc(setup_v, 1)
            dve.wait_ge(setup, 16 * 5)
            nc.vector.tensor_scalar(one_less_ka[:], col[:, M_KA:M_KA + 4], -1.0, 1.0, ALU.mult, ALU.add).then_inc(setup_v, 1)
            for x in (r_x, v_x, kr_x):
                last = nc.vector.memset(x[:, 0:4], 0.0)
            last.then_inc(ready, 1)
            dve.wait_ge(setup_v, 3)
            dve.wait_ge(ready, 1)

            def mu(blk):
                return col[:, bass.ds(M_MU + blk, 1)]

            def shift(x, blk, diff, to, name_diff, name, b):
                ins = nc.vector.tensor_tensor(diff, x[:, 3:3 + SEQ], x[:, 4:], ALU.subtract)
                dve_steps.done(ins, name_diff)
                dve_steps.wait(dve, name_diff, b)
                dve_steps.done(nc.vector.scalar_tensor_tensor(to, diff, mu(blk), x[:, 4:], ALU.mult, ALU.add), name)

            for n, (x, to, sem) in enumerate(((kr_x, k, lora_in), (r_x, kk, lora_g))):
                dve.wait_ge(copied, n + 2)
                nc.vector.tensor_tensor(to[:], x[:, 3:3 + SEQ], x[:, 4:], ALU.subtract).then_inc(setup_v, 1)
                dve.wait_ge(setup_v, 4 + n)
                nc.vector.scalar_tensor_tensor(to[:], to[:], mu(LORA_WA + n), x[:, 4:], ALU.mult, ALU.add).then_inc(sem, 1)
            dve.wait_ge(lora_read, 12)
            dve.wait_ge(gate_stored, 16 * 5)

            def heads(b):
                one = lambda base: col[:, bass.ds(base + b, 1)]
                flat = lambda x: x[:].rearrange("p c t -> p (c t)")
                at_head = lambda x: x[:, bass.ds(b, 1)].rearrange("p a t -> p (a t)")
                slot = lambda j: out[:, :, j]
                act_steps.wait(dve, "kr_copied", b)
                shift(kr_x, b + 4, k[:], k[:], "kr_diff", "kr", b)
                dve_steps.wait(dve, "kr", b)
                dve_steps.done(nc.vector.tensor_scalar(kk[:], k[:], one(M_KK), None, ALU.mult), "kk_raw")
                dve_steps.done(nc.vector.tensor_tensor_scan(flat(cs), flat(reset), at_head(sig), 0.0, ALU.mult, ALU.add), "cs")
                dve_steps.wait(dve, "cs", b)
                dve_steps.done(nc.vector.tensor_tensor(cm[:], cs[:], cs[:, :, P // 2 - 1:P // 2].broadcast_to([P, NT, P]), ALU.subtract), "cm")
                dve_steps.wait(dve, "cm", b)
                dve_steps.done(nc.vector.tensor_tensor(flat(before), flat(cm), at_head(sig), ALU.subtract), "before")
                dve_steps.done(nc.vector.tensor_scalar(r[:], at_head(rate), one(M_KA), one_less_ka[:, bass.ds(b, 1)], ALU.mult, ALU.add), "k_factor")
                dve_steps.wait(dve, "k_factor", b)
                dve_steps.done(nc.vector.tensor_tensor(k[:], k[:], r[:], ALU.mult), "k")
                act_steps.wait(dve, "r_copied", b)
                dve_steps.wait(dve, "k", b)
                shift(r_x, b, r[:], r[:], "r_diff", "r", b)
                dve_steps.wait(dve, "r", b)
                pe_steps.wait(dve, "norm_summed", b)
                dve_steps.done(nc.vector.scalar_tensor_tensor(sq[:], r[:], one(M_RK), k[:], ALU.mult, ALU.mult), "rk")
                act_steps.wait(dve, "norm", b)
                dve_steps.done(nc.vector.tensor_tensor(kk[:], kk[:], bonus[:], ALU.mult), "kk")
                dve_steps.wait(dve, "kk", b)
                dve.wait_ge(out_stored, 16 * (b + 1))
                by_tile = lambda x: x[:].rearrange("p (c t) -> p c t", t=P)
                dve_steps.done(nc.vector.tensor_tensor(slot(R_KK), by_tile(kk), before[:], ALU.mult), "kk_out")
                dve_steps.done(nc.vector.tensor_tensor(slot(R_R), by_tile(r), shrink[:], ALU.mult), "r_out")
                dve_steps.done(nc.vector.tensor_tensor(slot(R_K), by_tile(k), grow[:], ALU.mult), "k_out")
                dve_steps.done(nc.vector.scalar_tensor_tensor(kk[:], kk[:], -1.0, at_head(rate), ALU.mult, ALU.mult), "b_pre")
                dve_steps.wait(dve, "b_pre", b)
                dve_steps.done(nc.vector.tensor_tensor(slot(R_B), by_tile(kk), grow[:], ALU.mult), "b_out")
                act_steps.wait(dve, "v_copied", b)
                dve_steps.done(nc.vector.tensor_tensor(cm[:], v_x[:, 3:3 + SEQ].rearrange("p (c t) -> p c t", t=P),
                                                       v_x[:, 4:].rearrange("p (c t) -> p c t", t=P), ALU.subtract), "v_diff")
                dve_steps.wait(dve, "v_diff", b)
                dve_steps.done(nc.vector.scalar_tensor_tensor(slot(R_V), cm[:], mu(b + 8), v_x[:, 4:].rearrange("p (c t) -> p c t", t=P),
                                                              ALU.mult, ALU.add), "v_out")
                pe_steps.wait(dve, "bonus_summed", b)
                dve_steps.wait(dve, "v_out", b)
                dve.wait_ge(bonus_stored, 16 * (b + 1))
                dve_steps.done(nc.vector.tensor_tensor(by_tile(bonus), slot(R_V), sums[:, 2:4].rearrange("p n (c t) -> p (n c) t", t=P), ALU.mult), "bonus")
                dve_steps.done(nc.vector.tensor_tensor(ends[:], cs[:, :, P - 1], cs[:, :, P // 2 - 1], ALU.subtract), "ends")
                dve_steps.wait(dve, "ends", b)
                dve_steps.done(nc.vector.tensor_tensor(ends[:, 0:NT - 1], ends[:, 0:NT - 1], cs[:, 1:NT, P // 2 - 1], ALU.add), "ends_next")

            with dve.Fori(0, 4) as b:
                heads(b)


LEVELS = (2, 4, 8, 16, 32, 64)
HEADS = 4
MASKS = 5 + 7


def recurrences(nc, masks, scratch, carry, merged):
    with Stage(nc, "rc") as st:
        CH = "GAB"
        mask = st.sbuf("mask", [P, MASKS, P])
        tile = st.sbuf("tile", [P, 2, TILE_W])
        n_t = {ch: None for ch in CH}
        att = {ch: st.sbuf(f"att_{ch}", [P, 2 if ch == "G" else 4, HEADS, P]) for ch in CH}
        level = {ch: st.sbuf(f"level_{ch}", [P, 2, HEADS, P]) for ch in CH}
        T = {ch: st.sbuf(f"T_{ch}", [P, HEADS, P]) for ch in CH}
        TT = {ch: st.sbuf(f"TT_{ch}", [P, HEADS, P]) for ch in CH}
        X = {ch: st.sbuf(f"X_{ch}", [P, HEADS, P]) for ch in CH}
        tok = {ch: st.sbuf(f"tok_{ch}", [P, 8 if ch == "G" else 6, P]) for ch in CH}
        new = {ch: st.sbuf(f"new_{ch}", [P, HEADS if ch == "G" else 2, P]) for ch in CH}
        delta = {ch: st.sbuf(f"delta_{ch}", [P, HEADS if ch == "G" else 2, P]) for ch in CH}
        state = {ch: st.sbuf(f"state_{ch}", [P, HEADS if ch == "G" else 2, P]) for ch in CH}
        gate = st.sbuf("gate", [P, 2])
        ps = st.psum("ps", [P, 8, HALF])
        bank = {"G": 0, "A": 2, "B": 4}
        NT_, OUT_NEW, IN_V, OUT_V = 0, 1, 2, 3

        levels = [f"{ch}_{{}}{b}" for b in LEVELS for ch in CH]
        setup, ready = st.sem("setup"), st.sem("ready")
        loaded = [st.sem(f"loaded{u}") for u in range(2)]

        def level_names(kinds):
            return " ".join(f"{ch}_{k}{b}" for b in LEVELS for ks in kinds for ch in CH for k in ks if not (b == 64 and k in ("tx", "t")))

        pe_steps = Steps(st.sem("pe_steps"), "G_products A_products G_tokens G_turn B_products A_tokens A_turn B_tokens B_turn "
                         + level_names((("x",), ("tx", "xt"))) + " G_ks A_x B_x G_v A_p B_p G_s A_d B_d G_o A_y B_y")
        act_steps = Steps(st.sem("act_steps"), "G_T A_tokens A_tokens2 A_T B_tokens B_tokens2 B_T " + level_names((("xc",),))
                          + " A_x B_x G_v G_o A_y A_y2 B_y B_y2")
        dve_steps = Steps(st.sem("dve_steps"), "G_n G_att A_n A_att2 A_att3 A_att G_kd G_vb B_n B_att2 B_att3 B_att "
                          + level_names((("t", "tt"),))
                          + " G_xb G_x A_p1 A_p B_p1 B_p G_sg A_d B_d G_s A_m A_s0 A_s B_m B_s0 B_s")
        pool_steps = Steps(st.sem("pool_steps"), "G_m1 G_tt A_m1 A_tt B_m1 B_tt " + level_names((("m",),)))
        block = st.stack.enter_context(nc.Block())

        def slot(u, n, count=1):
            return tile[:, u, n * P:(n + count) * P]

        def slots(u, n, count, step=1):
            v = tile[:, u, 0:SLOTS * P].rearrange("p (s t) -> p s t", t=P)
            return v[:, n:n + step * (count - 1) + 1:step]

        def rwkv(ch, pair, j):
            return S_RWKV + R_SLOTS * (2 * "AB".index(ch) + pair) + j

        def columns(u, n):
            return tile[:, u, C_GDN + 4 * n:C_GDN + 4 * n + 4].rearrange("p (n a) -> p n a", a=1).broadcast_to([P, HEADS, P])

        def over_heads(n):
            return mask[:, n:n + 1].broadcast_to([P, HEADS, P])

        def banks(n, count=1):
            return ps[:, n:n + count].rearrange("p b w -> p (b w)").rearrange("p (n t) -> p n t", t=P)

        def chosen(n):
            return mask[:, n:n + 1].bitcast(U32).broadcast_to([P, HEADS, P])

        @block.sync
        def _(sp):
            sp.dma_start(mask[:], masks).then_inc(setup, 16)
            for u in range(2):
                sp.dma_start(tile[:, u], scratch[u]).then_inc(loaded[u], 16)
            with sp.Fori(0, NT // 2 - 1) as i:
                for u in range(2):
                    pe_steps.wait(sp, "B_y", 2 * i + u)
                    dve_steps.wait(sp, "B_s", 2 * i + u)
                    sp.dma_start(tile[:, u], scratch[bass.ds(2 * i + u + 2, 1)].rearrange("a p w -> p (a w)")).then_inc(loaded[u], 16)

        @block.tensor
        def _(pe):
            pe_steps.open(pe)
            mm = nc.tensor.matmul
            pe.wait_ge(setup, 16)
            pe.wait_ge(ready, 1)

            def turn(out, sources):
                for n, src in enumerate(sources):
                    last = nc.tensor.transpose(out[:, n], src, mask[:, 0])
                return last

            def products(ch, u):
                for n in range(HEADS):
                    if ch == "G":
                        last = mm(ps[:, n // 2, n % 2 * 2 * P:(n % 2 + 1) * 2 * P], slot(u, S_K + 2 * n),
                                  slots(u, 2 * n, 2, S_K + 1), start=True, stop=True)
                    else:
                        rows = slice(64 * (n % 2), 64 * (n % 2) + 64)
                        kk_r = slot(u, rwkv(ch, n // 2, R_KK), 2)[rows]
                        for j, kind in enumerate((R_B, R_K)):
                            last = mm(ps[:, 4 + n, 2 * j * P:2 * (j + 1) * P], slot(u, rwkv(ch, n // 2, kind))[rows], kk_r, start=True, stop=True)
                pe_steps.done(last, f"{ch}_products")

            def tile_of(c, u, i):
                pe.wait_ge(loaded[u], 16 * (i + 1))
                act_steps.wait(pe, "G_o", c - 1)
                dve_steps.wait(pe, "G_s", c - 1)
                products("G", u)
                act_steps.wait(pe, "B_y2", c - 1)
                dve_steps.wait(pe, "B_d", c - 1)
                products("A", u)
                act_steps.wait(pe, "A_y2", c - 1)
                dve_steps.wait(pe, "A_d", c - 1)
                turn(banks(2), [slot(u, S_K + 2 * n) for n in range(HEADS)])
                pe_steps.done(turn(banks(3), [slot(u, S_V + n) for n in range(HEADS)]), "G_tokens")
                pool_steps.wait(pe, "G_tt", c)
                dve_steps.wait(pe, "G_att", c)
                pe_steps.done(turn(banks(0), [TT["G"][:, n] for n in range(HEADS)]), "G_turn")
                dve_steps.wait(pe, "A_att", c)
                products("B", u)
                dve_steps.wait(pe, "G_vb", c)

                def tokens(ch):
                    kinds = [(pair, j) for j in (R_V, R_K, R_B) for pair in range(2)]
                    srcs = [slot(u, rwkv(ch, pair, j)) for pair, j in kinds]
                    turn(banks(bank[ch]), srcs[0:4])
                    pe_steps.done(turn(banks(bank[ch] + 1), srcs[4:6]), f"{ch}_tokens")

                tokens("A")
                act_steps.wait(pe, "A_tokens2", c)
                pool_steps.wait(pe, "A_tt", c)
                pe_steps.done(turn(banks(2), [TT["A"][:, n] for n in range(HEADS)]), "A_turn")
                dve_steps.wait(pe, "B_att", c)
                tokens("B")
                act_steps.wait(pe, "B_tokens2", c)
                pool_steps.wait(pe, "B_tt", c)
                pe_steps.done(turn(banks(4), [TT["B"][:, n] for n in range(HEADS)]), "B_turn")

                for k, b in enumerate(LEVELS):
                    for ch in CH:
                        pool_steps.wait(pe, f"{ch}_m{b}", c)
                        act_steps.wait(pe, f"{ch}_T", c)
                        if k:
                            dve_steps.wait(pe, f"{ch}_t{LEVELS[k - 1]}", c)
                        for n in range(HEADS):
                            last = mm(banks(bank[ch])[:, n], level[ch][:, k % 2, n], T[ch][:, n], start=True, stop=True)
                        pe_steps.done(last, f"{ch}_x{b}")
                    for ch in CH:
                        act_steps.wait(pe, f"{ch}_xc{b}", c)
                        if k:
                            dve_steps.wait(pe, f"{ch}_tt{LEVELS[k - 1]}", c)
                        if b < 64:
                            for n in range(HEADS):
                                last = mm(banks(bank[ch])[:, n], TT[ch][:, n], X[ch][:, n], start=True, stop=True)
                            pe_steps.done(last, f"{ch}_tx{b}")
                        for n in range(HEADS):
                            last = mm(banks(bank[ch] + 1)[:, n], X[ch][:, n], TT[ch][:, n], start=True, stop=True)
                        pe_steps.done(last, f"{ch}_xt{b}")

                dve_steps.wait(pe, "G_s", c - 1)
                for n in range(HEADS):
                    last = mm(banks(0)[:, n], slot(u, S_K + 2 * n), state["G"][:, n], start=True, stop=True)
                pe_steps.done(last, "G_ks")
                for ch in "AB":
                    dve_steps.wait(pe, f"{ch}_s", c - 1)
                    for n in range(HEADS):
                        o = banks(bank[ch])[:, n]
                        mm(o, slot(u, rwkv(ch, n // 2, R_KK)), state[ch][:, n // 2], start=True, stop=False)
                        last = mm(o, att[ch][:, IN_V, n], tok[ch][:, n // 2], start=False, stop=True)
                    pe_steps.done(last, f"{ch}_x")
                for ch, name in (("G", "G_v"), ("A", "A_p"), ("B", "B_p")):
                    dve_steps.wait(pe, f"{ch}_tt64", c)
                    if ch == "G":
                        dve_steps.wait(pe, "G_x", c)
                    else:
                        act_steps.wait(pe, f"{ch}_x", c)
                    for n in range(HEADS):
                        last = mm(banks(bank[ch] + 1)[:, n], TT[ch][:, n], X[ch][:, n], start=True, stop=True)
                    pe_steps.done(last, name)
                act_steps.wait(pe, "G_v", c)
                for n in range(HEADS):
                    last = mm(banks(1)[:, n], tok["G"][:, n], new["G"][:, n], start=True, stop=True)
                pe_steps.done(last, "G_s")
                for ch in "AB":
                    dve_steps.wait(pe, f"{ch}_p", c)
                    for pair in range(2):
                        o = banks(bank[ch])[:, pair]
                        mm(o, tok[ch][:, 2 + pair], tok[ch][:, pair], start=True, stop=False)
                        last = mm(o, tok[ch][:, 4 + pair], new[ch][:, pair], start=False, stop=True)
                    pe_steps.done(last, f"{ch}_d")
                for n in range(HEADS):
                    mm(banks(0)[:, n], state["G"][:, n], slot(u, S_Q + 2 * n + 1), start=True, stop=False)
                    last = mm(banks(0)[:, n], new["G"][:, n], att["G"][:, OUT_NEW, n], start=False, stop=True)
                pe_steps.done(last, "G_o")
                for ch in "AB":
                    for n in range(HEADS):
                        o = banks(bank[ch] + 1)[:, n]
                        mm(o, state[ch][:, n // 2], slot(u, rwkv(ch, n // 2, R_R)), start=True, stop=False)
                        mm(o, tok[ch][:, n // 2], att[ch][:, OUT_V, n], start=False, stop=False)
                        last = mm(o, new[ch][:, n // 2], att[ch][:, OUT_NEW, n], start=False, stop=True)
                    pe_steps.done(last, f"{ch}_y")

            with pe.Fori(0, NT // 2) as i:
                for u in range(2):
                    tile_of(2 * i + u, u, i)

        @block.scalar
        def _(act):
            act_steps.open(act)

            def copy(name, out, src):
                act_steps.done(nc.scalar.copy(out, src), name)

            def tile_of(c):
                def tokens(ch):
                    pe_steps.wait(act, f"{ch}_tokens", c)
                    copy(f"{ch}_tokens", tok[ch][:, 0:4], banks(bank[ch]))
                    copy(f"{ch}_tokens2", tok[ch][:, 4:6], banks(bank[ch] + 1)[:, 0:2])

                pe_steps.wait(act, "G_turn", c)
                copy("G_T", T["G"][:], banks(0))
                tokens("A")
                pe_steps.wait(act, "A_turn", c)
                copy("A_T", T["A"][:], banks(2))
                tokens("B")
                pe_steps.wait(act, "B_turn", c)
                copy("B_T", T["B"][:], banks(4))
                for b in LEVELS:
                    for ch in CH:
                        pe_steps.wait(act, f"{ch}_x{b}", c)
                        copy(f"{ch}_xc{b}", X[ch][:], banks(bank[ch]))
                for ch in "AB":
                    pe_steps.wait(act, f"{ch}_x", c)
                    copy(f"{ch}_x", X[ch][:], banks(bank[ch]))
                pe_steps.wait(act, "G_v", c)
                copy("G_v", new["G"][:], banks(1))
                pe_steps.wait(act, "G_o", c)
                copy("G_o", merged[:, 0:4, bass.ds(c * P, P)], banks(0))
                for ch in "AB":
                    pe_steps.wait(act, f"{ch}_y", c)
                    first = 4 + 2 * "AB".index(ch)
                    for e, name in enumerate((f"{ch}_y", f"{ch}_y2")):
                        rows = slice(64 * e, 64 * e + 64)
                        copy(name, merged[rows, first:first + 2, bass.ds(c * P, P)],
                             banks(bank[ch] + 1)[rows, e:e + 3:2])

            with act.Fori(0, NT // 2) as i:
                for u in range(2):
                    tile_of(2 * i + u)

        @block.gpsimd
        def _(pool):
            pool_steps.open(pool)
            pool.wait_ge(setup, 16)
            tt = nc.gpsimd.tensor_tensor

            def tile_of(c):
                for ch in CH:
                    dve_steps.wait(pool, f"{ch}_n", c)
                    pe_steps.wait(pool, f"{ch}_p" if ch != "G" else "G_v", c - 1)
                    pool_steps.done(tt(X[ch][:], att[ch][:, NT_], over_heads(5), ALU.mult), f"{ch}_m1")
                    pool_steps.wait(pool, f"{ch}_m1", c)
                    pool_steps.done(tt(TT[ch][:], X[ch][:], over_heads(0), ALU.add), f"{ch}_tt")
                for k, b in enumerate(LEVELS):
                    for ch in CH:
                        if k >= 2:
                            pe_steps.wait(pool, f"{ch}_x{LEVELS[k - 2]}", c)
                        pool_steps.done(tt(level[ch][:, k % 2], att[ch][:, NT_], over_heads(6 + k), ALU.mult), f"{ch}_m{b}")

            with pool.Fori(0, NT // 2) as i:
                for u in range(2):
                    tile_of(2 * i + u)

        @block.vector
        def _(dve):
            dve_steps.open(dve)
            for ch in CH:
                nc.vector.memset(state[ch][:], 0.0)
                nc.vector.memset(att[ch][:], 0.0)
            nc.vector.memset(gate[:], 0.0).then_inc(ready, 1)
            dve.wait_ge(setup, 16)
            dve.wait_ge(ready, 1)
            tt = nc.vector.tensor_tensor

            def masked(ch, c):
                pe_steps.wait(dve, f"{ch}_products", c)
                pe_steps.wait(dve, f"{ch}_y", c - 1)
                pool_steps.wait(dve, f"{ch}_m64", c - 1)
                nc.vector.tensor_copy(gate[:, 0:1], gate[:, 1:2])
                for name, j, kind, which in ((f"{ch}_n", 0, NT_, 3), (f"{ch}_att2", 1, OUT_NEW, 2),
                                             (f"{ch}_att3", 2, IN_V, 3), (f"{ch}_att", 3, OUT_V, 2)):
                    dve_steps.done(nc.vector.copy_predicated(att[ch][:, kind], chosen(which), ps[:, 4:8, j * P:(j + 1) * P]), name)

            def tile_of(c, u, i):
                both = ps[:, 0:2].rearrange("p b w -> p (b w)").rearrange("p (n k t) -> p n k t", k=2, t=P)
                dve.wait_ge(loaded[u], 16 * (i + 1))
                pe_steps.wait(dve, "G_products", c)
                pool_steps.wait(dve, "G_m64", c - 1)
                dve_steps.done(tt(att["G"][:, NT_], both[:, :, 1], slots(u, S_STRICT, 4), ALU.mult), "G_n")
                dve_steps.done(tt(att["G"][:, OUT_NEW], both[:, :, 0], slots(u, S_INCL, 4), ALU.mult), "G_att")
                masked("A", c)
                pe_steps.wait(dve, "G_tokens", c)
                dve_steps.done(tt(tok["G"][:, 0:4], banks(2), columns(u, 2), ALU.mult), "G_kd")
                dve_steps.done(tt(tok["G"][:, 4:8], banks(3), columns(u, 0), ALU.mult), "G_vb")
                masked("B", c)
                for b in LEVELS:
                    for ch in CH:
                        if b < 64:
                            pe_steps.wait(dve, f"{ch}_tx{b}", c)
                            dve_steps.done(tt(T[ch][:], T[ch][:], banks(bank[ch]), ALU.add), f"{ch}_t{b}")
                        pe_steps.wait(dve, f"{ch}_xt{b}", c)
                        dve_steps.done(tt(TT[ch][:], TT[ch][:], banks(bank[ch] + 1), ALU.add), f"{ch}_tt{b}")
                pe_steps.wait(dve, "G_ks", c)
                dve_steps.done(tt(delta["G"][:], banks(0), columns(u, 1), ALU.mult), "G_xb")
                dve_steps.wait(dve, "G_xb", c)
                dve_steps.done(tt(X["G"][:], delta["G"][:], tok["G"][:, 4:8], ALU.add), "G_x")
                for ch in "AB":
                    pe_steps.wait(dve, f"{ch}_p", c)
                    for e, name in enumerate((f"{ch}_p1", f"{ch}_p")):
                        half = slice(64 * e, 64 * e + 64)
                        dve_steps.done(nc.vector.tensor_copy(new[ch][:, :, half], banks(bank[ch] + 1)[:, e:e + 3:2, half]), name)
                pe_steps.wait(dve, "G_s", c)
                dve_steps.done(tt(delta["G"][:], state["G"][:], columns(u, 3), ALU.mult), "G_sg")
                for ch in "AB":
                    pe_steps.wait(dve, f"{ch}_d", c)
                    dve_steps.done(tt(delta[ch][:], banks(bank[ch])[:, 0:2], mask[:, 4:5].broadcast_to([P, 2, P]), ALU.mult), f"{ch}_d")
                dve_steps.wait(dve, "G_sg", c)
                pe_steps.wait(dve, "G_o", c)
                dve_steps.done(tt(state["G"][:], delta["G"][:], banks(1), ALU.add), "G_s")
                for ch in "AB":
                    dve_steps.wait(dve, f"{ch}_d", c)
                    pe_steps.wait(dve, f"{ch}_y", c)
                    dve_steps.done(tt(delta[ch][:], delta[ch][:], state[ch][:], ALU.add), f"{ch}_m")
                    dve_steps.wait(dve, f"{ch}_m", c)
                    for pair, name in enumerate((f"{ch}_s0", f"{ch}_s")):
                        n = 2 * "AB".index(ch) + pair
                        dve_steps.done(nc.vector.tensor_scalar(state[ch][:, pair], delta[ch][:, pair],
                                                               carry[:, bass.ds(c, 1), n], None, ALU.mult), name)

            with dve.Fori(0, NT // 2) as i:
                for u in range(2):
                    tile_of(2 * i + u, u, i)


GN_EPS = 64e-5
HEAD_N = 64


def mixer_output(nc, merged, z_gate, rwkv_gate, rwkv_bonus, norm_w, gn_w, gn_b, masks, w_out, out):
    with Stage(nc, "mo") as st:
        w_raw = st.sbuf("w_raw", [P, 2, D])
        w_hi = st.sbuf("w_hi", [P, 8, D], F32R)
        w_lo = st.sbuf("w_lo", [P, 8, D], F32R)
        m_hi = merged[:].bitcast(F32R)
        m_lo = st.sbuf("m_lo", [P, 8, SEQ], F32R)
        z, gate, bonus = st.sbuf("z", [P, SEQ]), st.sbuf("gate", [P, SEQ]), st.sbuf("bonus", [P, SEQ])
        g_root, r_root = st.sbuf("g_root", [P, SEQ]), st.sbuf("r_root", [P, SEQ])
        g_value, r_value = st.sbuf("g_value", [P, SEQ]), st.sbuf("r_value", [P, SEQ])
        mask = st.sbuf("mask", [P, 2, P])
        cols = st.sbuf("cols", [P, 12])
        eps = st.sbuf("eps", [P, 2])
        pass_gate = st.sbuf("pass_gate", [P, 2])
        ps = st.psum("ps", [P, 8, HALF])
        setup, ready = st.sem("setup"), st.sem("ready")
        w_loaded = [st.sem(f"w_loaded{u}") for u in range(2)]
        w_rounded, w_split = st.sem("w_rounded"), st.sem("w_split")
        z_loaded, gates_loaded = st.sem("z_loaded"), st.sem("gates_loaded")
        summed, copied_act, copied_dve = st.sem("summed"), st.sem("copied_act"), st.sem("copied_dve")
        pe_steps = Steps(st.sem("pe_steps"), "R_mean G_sum R_sum")
        act_steps = Steps(st.sem("act_steps"), "R_sq G_sq G_ln G_root R_ln R_root")
        dve_steps = Steps(st.sem("dve_steps"), "R_centred G_scaled G_value G_hi R_scaled R_offset R_value R_hi")
        pool_steps = Steps(st.sem("pool_steps"), "G_lo R_lo")
        block = st.stack.enter_context(nc.Block())
        BLOCKS = 4
        MEAN, G_SUM, R_SUM = 0, 2, 4

        def bank(n):
            return ps[:, n:n + 2].rearrange("p n t -> p (n t)")

        def at(x, n):
            return x[:, bass.ds(n, 1)].rearrange("p a t -> p (a t)")

        @block.sync
        def _(sp):
            sp.dma_start(mask[:, 0], masks[:, 1]).then_inc(setup, 16)
            sp.dma_start(mask[:, 1], masks[:, 4]).then_inc(setup, 16)
            for j, v in enumerate((norm_w, gn_w, gn_b)):
                sp.dma_start(cols[:, 4 * j:4 * j + 4], v).then_inc(setup, 16)
            with sp.Fori(0, BLOCKS) as n:
                dve_steps.wait(sp, "G_value", n - 1)
                sp.dma_start(z[:], z_gate[bass.ds(n, 1)].rearrange("a p t -> p (a t)")).then_inc(z_loaded, 16)
                dve_steps.wait(sp, "R_value", n - 1)
                sp.dma_start(bonus[:], rwkv_bonus[bass.ds(n, 1)].rearrange("a p t -> p (a t)")).then_inc(gates_loaded, 16)
                sp.dma_start(gate[:], rwkv_gate[bass.ds(n, 1)].rearrange("a p t -> p (a t)")).then_inc(gates_loaded, 16)

        @block.gpsimd
        def _(pool):
            pool_steps.open(pool)
            nc.gpsimd.memset(pass_gate[:], 0.0).then_inc(w_rounded, 1)
            pool.wait_ge(w_rounded, 1)
            for u in range(2):
                pool.dma_start(w_raw[:, u], w_out[u * P:(u + 1) * P, :]).then_inc(w_loaded[u], 16)

            def split(k, u, i):
                pool.wait_ge(w_loaded[u], 16 * (i + 1))
                nc.gpsimd.tensor_tensor(pass_gate[:, 0:1], pass_gate[:, 1:2], pass_gate[:, 1:2], ALU.add)
                nc.gpsimd.tensor_copy(at(w_hi, k), w_raw[:, u]).then_inc(w_rounded, 1)
                pool.wait_ge(w_rounded, k + 2)
                nc.gpsimd.tensor_tensor(at(w_lo, k), w_raw[:, u], at(w_hi, k).bitcast(F32), ALU.subtract).then_inc(w_split, 1)

            def lower(n, i):
                dve_steps.wait(pool, "G_hi", n)
                pool_steps.done(nc.gpsimd.tensor_tensor(at(m_lo, n), g_value[:], at(m_hi, n).bitcast(F32), ALU.subtract), "G_lo")
                dve_steps.wait(pool, "R_hi", n)
                pool_steps.done(nc.gpsimd.tensor_tensor(at(m_lo, n + 4), r_value[:], at(m_hi, n + 4).bitcast(F32), ALU.subtract), "R_lo")

            with pool.Fori(0, BLOCKS - 1) as i:
                for u in range(2):
                    split(2 * i + u, u, i)
                for u in range(2):
                    pool.wait_ge(w_split, 2 * i + u + 1)
                    pool.dma_start(w_raw[:, u], w_out[bass.ds((2 * i + u + 2) * P, P), :]).then_inc(w_loaded[u], 16)
                lower(i, i)
            for u in range(2):
                split(NT - 2 + u, u, BLOCKS - 1)
            lower(BLOCKS - 1, BLOCKS - 1)

        @block.scalar
        def _(act):
            act_steps.open(act)
            act.wait_ge(ready, 1)

            def inverse_root(out, n_bank, n_eps, scale, ln, root, n):
                act_steps.done(nc.scalar.activation(out, bank(n_bank), ACT.Ln, bias=eps[:, n_eps:n_eps + 1], scale=scale), ln)
                act_steps.wait(act, ln, n)
                act_steps.done(nc.scalar.activation(out, out, ACT.Exp, scale=-0.5), root)

            with act.Fori(0, BLOCKS) as n:
                dve_steps.wait(act, "R_centred", n)
                act_steps.done(nc.scalar.activation(r_root[:], r_value[:], ACT.Square), "R_sq")
                act_steps.done(nc.scalar.activation(g_root[:], at(merged, n), ACT.Square), "G_sq")
                pe_steps.wait(act, "G_sum", n)
                inverse_root(g_root[:], G_SUM, 0, 1.0 / P, "G_ln", "G_root", n)
                pe_steps.wait(act, "R_sum", n)
                inverse_root(r_root[:], R_SUM, 1, 1.0 / HEAD_N, "R_ln", "R_root", n)
            for t in range(NT):
                act.wait_ge(summed, 2 * t + 1)
                nc.scalar.copy(out[:, t, 0:HALF], ps[:, 2 * t % 8]).then_inc(copied_act, 1)

        @block.vector
        def _(dve):
            dve_steps.open(dve)
            nc.vector.memset(eps[:, 0:1], NORM_EPS)
            nc.vector.memset(eps[:, 1:2], GN_EPS).then_inc(ready, 1)
            dve.wait_ge(setup, 16 * 5)
            stt = nc.vector.scalar_tensor_tensor

            with dve.Fori(0, BLOCKS) as n:
                pe_steps.wait(dve, "R_mean", n)
                pool_steps.wait(dve, "R_lo", n - 1)
                dve_steps.done(stt(r_value[:], bank(MEAN), -1.0 / HEAD_N, at(merged, n + 4), ALU.mult, ALU.add), "R_centred")
                act_steps.wait(dve, "G_root", n)
                pool_steps.wait(dve, "G_lo", n - 1)
                dve_steps.done(stt(g_value[:], at(merged, n), cols[:, bass.ds(n, 1)], g_root[:], ALU.mult, ALU.mult), "G_scaled")
                dve_steps.wait(dve, "G_scaled", n)
                dve.wait_ge(z_loaded, 16 * (n + 1))
                dve_steps.done(nc.vector.tensor_tensor(g_value[:], g_value[:], z[:], ALU.mult), "G_value")
                dve_steps.wait(dve, "G_value", n)
                dve_steps.done(nc.vector.tensor_scalar(at(m_hi, n), g_value[:], 1.0, None, ALU.mult), "G_hi")
                act_steps.wait(dve, "R_root", n)
                dve_steps.done(stt(r_value[:], r_value[:], cols[:, bass.ds(n + 4, 1)], r_root[:], ALU.mult, ALU.mult), "R_scaled")
                dve_steps.wait(dve, "R_scaled", n)
                dve.wait_ge(gates_loaded, 32 * (n + 1))
                dve_steps.done(stt(r_value[:], r_value[:], cols[:, bass.ds(n + 8, 1)], bonus[:], ALU.add, ALU.add), "R_offset")
                dve_steps.wait(dve, "R_offset", n)
                dve_steps.done(nc.vector.tensor_tensor(r_value[:], r_value[:], gate[:], ALU.mult), "R_value")
                dve_steps.wait(dve, "R_value", n)
                dve_steps.done(nc.vector.tensor_scalar(at(m_hi, n + 4), r_value[:], 1.0, None, ALU.mult), "R_hi")
            for t in range(NT):
                dve.wait_ge(summed, 2 * t + 2)
                nc.vector.tensor_copy(out[:, t, HALF:D], ps[:, (2 * t + 1) % 8]).then_inc(copied_dve, 1)

        @block.tensor
        def _(pe):
            pe_steps.open(pe)
            pe.wait_ge(setup, 16 * 5)

            def over_channels(which, first_bank, src, name):
                for t in range(NH):
                    last = nc.tensor.matmul(ps[:, first_bank + t], mask[:, which], src[:, t * HALF:(t + 1) * HALF], start=True, stop=True)
                pe_steps.done(last, name)

            with pe.Fori(0, BLOCKS) as n:
                dve_steps.wait(pe, "R_centred", n - 1)
                over_channels(1, MEAN, at(merged, n + 4), "R_mean")
                act_steps.wait(pe, "G_sq", n)
                over_channels(0, G_SUM, g_root, "G_sum")
                over_channels(1, R_SUM, r_root, "R_sum")
            pool_steps.wait(pe, "R_lo", BLOCKS - 1)
            pe.wait_ge(w_split, 8)
            for t in range(NT):
                tok = slice(t * P, (t + 1) * P)
                for half in range(2):
                    if t >= 4:
                        pe.wait_ge(copied_act if half == 0 else copied_dve, t - 3)
                    cols_ = slice(half * HALF, (half + 1) * HALF)
                    for c in range(8):
                        last = split_matmul(nc, ps[:, (2 * t + half) % 8], (m_hi[:, c, tok], m_lo[:, c, tok]),
                                            (w_hi[:, c, cols_], w_lo[:, c, cols_]), c == 0, c == 7)
                    last.then_inc(summed, 1)


def layer_embedding(nc, h, p, w_gate, w_proj, masks, out):
    with Stage(nc, "le") as st:
        NE = D_PLE // P
        ROWS = NE + ND
        w_raw = st.sbuf("w_raw", [P, 2, D])
        w_hi = st.sbuf("w_hi", [P, ROWS, D], F32R)
        w_lo = st.sbuf("w_lo", [P, ROWS, D], F32R)
        p_raw = st.sbuf("p_raw", [P, 2, D_PLE])
        p_hi = st.sbuf("p_hi", [P, NE, SEQ], F32R)
        p_lo = st.sbuf("p_lo", [P, NE, SEQ], F32R)
        identity = st.sbuf("identity", [P, P])
        ps = st.psum("ps", [P, 8, HALF])
        setup = st.sem("setup")
        w_loaded = [st.sem(f"w_loaded{u}") for u in range(2)]
        p_loaded = [st.sem(f"p_loaded{u}") for u in range(2)]
        w_rounded, w_split = st.sem("w_rounded"), st.sem("w_split")
        p_turned, p_rounded, p_split = st.sem("p_turned"), st.sem("p_rounded"), st.sem("p_split")
        gate_summed, proj_summed, sigmoid_done, multiplied = st.sem("gate_summed"), st.sem("proj_summed"), st.sem("sigmoid_done"), st.sem("multiplied")
        block = st.stack.enter_context(nc.Block())

        @block.sync
        def _(sp):
            sp.dma_start(identity[:], masks[:, 0]).then_inc(setup, 16)
            for t in range(NT):
                if t >= 2:
                    sp.wait_ge(p_turned, t - 1)
                sp.dma_start(p_raw[:, t % 2], p[t * P:(t + 1) * P, :]).then_inc(p_loaded[t % 2], 16)

        @block.gpsimd
        def _(pool):
            for k in range(ROWS):
                if k >= 2:
                    pool.wait_ge(w_split, k - 1)
                src = w_proj[k * P:(k + 1) * P, :] if k < NE else w_gate[(k - NE) * P:(k - NE + 1) * P, :]
                pool.dma_start(w_raw[:, k % 2], src).then_inc(w_loaded[k % 2], 16)

        @block.scalar
        def _(act):
            for k in range(ROWS):
                act.wait_ge(w_loaded[k % 2], 16 * (k // 2 + 1))
                nc.scalar.copy(w_hi[:, k], w_raw[:, k % 2]).then_inc(w_rounded, 1)
                if k < NT:
                    act.wait_ge(p_turned, k + 1)
                    nc.scalar.copy(p_hi[:, :, k * P:(k + 1) * P], ps[:, k % 2, 0:D_PLE].rearrange("p (e t) -> p e t", t=P)).then_inc(p_rounded, 1)
            for t in range(NT):
                for half in range(2):
                    n = 2 * t + half
                    act.wait_ge(gate_summed, n + 1)
                    nc.scalar.activation(out[:, t, half * HALF:(half + 1) * HALF], ps[:, n % 4], ACT.Sigmoid).then_inc(sigmoid_done, 1)

        @block.vector
        def _(dve):
            for k in range(ROWS):
                dve.wait_ge(w_rounded, k + 1)
                nc.vector.tensor_tensor(w_lo[:, k], w_raw[:, k % 2], w_hi[:, k].bitcast(F32), ALU.subtract).then_inc(w_split, 1)
                if k < NT:
                    dve.wait_ge(p_rounded, k + 1)
                    part = (slice(None), slice(None), slice(k * P, (k + 1) * P))
                    nc.vector.tensor_tensor(p_lo[part], ps[:, k % 2, 0:D_PLE].rearrange("p (e t) -> p e t", t=P),
                                            p_hi[part].bitcast(F32), ALU.subtract).then_inc(p_split, 1)
            for t in range(NT):
                for half in range(2):
                    n = 2 * t + half
                    to = out[:, t, half * HALF:(half + 1) * HALF]
                    dve.wait_ge(sigmoid_done, n + 1)
                    dve.wait_ge(proj_summed, n + 1)
                    nc.vector.tensor_tensor(to, to, ps[:, 4 + n % 4], ALU.mult).then_inc(multiplied, 1)

        @block.tensor
        def _(pe):
            pe.wait_ge(setup, 16)
            for t in range(NT):
                pe.wait_ge(p_loaded[t % 2], 16 * (t // 2 + 1))
                if t >= 2:
                    pe.wait_ge(p_split, t - 1)
                for e in range(NE):
                    last = nc.tensor.transpose(ps[:, t % 2, e * P:(e + 1) * P], p_raw[:, t % 2, e * P:(e + 1) * P], identity[:])
                last.then_inc(p_turned, 1)
            pe.wait_ge(p_split, NT)
            pe.wait_ge(w_split, NE)
            for t in range(NT):
                tok = slice(t * P, (t + 1) * P)
                for half in range(2):
                    n = 2 * t + half
                    cols = slice(half * HALF, (half + 1) * HALF)
                    if n >= 4:
                        pe.wait_ge(multiplied, n - 3)
                    for e in range(NE):
                        last = split_matmul(nc, ps[:, 4 + n % 4], (p_hi[:, e, tok], p_lo[:, e, tok]),
                                            (w_hi[:, e, cols], w_lo[:, e, cols]), e == 0, e == NE - 1)
                    last.then_inc(proj_summed, 1)
                    for d in range(ND):
                        if n == 0:
                            pe.wait_ge(w_split, NE + d + 1)
                        last = split_matmul(nc, ps[:, n % 4], (h[0][:, d, tok], h[1][:, d, tok]),
                                            (w_hi[:, NE + d, cols], w_lo[:, NE + d, cols]), d == 0, d == ND - 1)
                    last.then_inc(gate_summed, 1)


def layer(nc, x, p, ffn1_norm_pre, ffn1_w_gate, ffn1_w_up, ffn1_w_down, ffn1_norm_post, mix_norm_pre, w_in, conv_w,
          a_log, dt_bias, norm_w, rwkv_params, w2, a2, g2, w_out, mix_norm_post, ffn2_norm_pre,
          ffn2_w_gate, ffn2_w_up, ffn2_w_down, ffn2_norm_post, ple_norm_pre, ple_w_gate, ple_w_proj, ple_norm_post,
          masks, out):
    def internal(name, shape):
        return nc.dram_tensor(name, shape, F32, kind="Internal").ap()

    x1, x2, x3 = (internal(f"x{n}", [SEQ, D]) for n in (1, 2, 3))
    scratch = internal("tiles", [NT, P, TILE_W])
    z_gate, rwkv_gate, rwkv_bonus = (internal(name, [4, P, SEQ]) for name in ("z_gate", "rwkv_gate", "rwkv_bonus"))

    def h_parts(st):
        return st.sbuf("h_hi", [P, ND, SEQ], F32R), st.sbuf("h_lo", [P, ND, SEQ], F32R)

    with Stage(nc, "layer") as whole:
        identity = whole.sbuf("identity", [P, P])
        carry = whole.sbuf("carry", [P, NT, 4])
        loaded = whole.sem("loaded")
        with nc.Block() as block:
            @block.sync
            def _(sp):
                sp.dma_start(identity[:], masks[:, 0]).then_inc(loaded, 16)
                sp.wait_ge(loaded, 16)

        with Stage(nc, "first") as st:
            h = h_parts(st)
            with Stage(nc, "first_branch") as inner:
                branch = inner.sbuf("branch", [P, NT, D])
                residual_norm(nc, "n1", x, None, None, None, None, ffn1_norm_pre, h, identity[:])
                swiglu(nc, "f1", h, ffn1_w_gate, ffn1_w_up, ffn1_w_down, branch)
                residual_norm(nc, "n2", x, x1, branch, ffn1_norm_post, 0.5, mix_norm_pre, h, identity[:])
            gdn_projection(nc, h, w_in, conv_w, a_log, dt_bias, masks, scratch, z_gate)
            rwkv_projection(nc, h, w_in, w2, a2, g2, rwkv_params, masks, scratch, rwkv_gate, rwkv_bonus, carry)

        with Stage(nc, "second") as st:
            branch = st.sbuf("branch", [P, NT, D])
            with Stage(nc, "second_merged") as inner:
                merged = inner.sbuf("merged", [P, 8, SEQ])
                recurrences(nc, masks, scratch, carry, merged)
                mixer_output(nc, merged, z_gate, rwkv_gate, rwkv_bonus, norm_w, rwkv_params[:, M_GNW:M_GNW + 4],
                             rwkv_params[:, M_GNB:M_GNB + 4], masks, w_out, branch)
            h = h_parts(st)
            residual_norm(nc, "n3", x1, x2, branch, mix_norm_post, 1.0, ffn2_norm_pre, h, identity[:])
            swiglu(nc, "f2", h, ffn2_w_gate, ffn2_w_up, ffn2_w_down, branch)
            residual_norm(nc, "n4", x2, x3, branch, ffn2_norm_post, 0.5, ple_norm_pre, h, identity[:])
            layer_embedding(nc, h, p, ple_w_gate, ple_w_proj, masks, branch)
            residual_norm(nc, "n5", x3, out, branch, ple_norm_post, 1.0, None, None, identity[:])


def kernel(**inputs):
    import numpy as np
    import concourse.bacc as bacc
    from concourse.bass_utils import run_bass_kernel_spmd

    def rows(*names):
        return np.concatenate([np.asarray(inputs[name]).reshape(-1, P) for name in names]).T

    given = {name: np.asarray(a)[0] for name, a in inputs.items()}
    given["p"] = given["p"][0]
    position = np.arange(P)
    j, i = position[:, None], position[None, :]
    masks = np.zeros((P, MASKS, P), np.float32)
    for n, mask in enumerate([j == i, j >= 0, j <= i, j < i, j // HEAD_N == i // HEAD_N]):
        masks[:, n] = mask
    for level in range(7):
        size = 2 ** level
        masks[:, 5 + level] = (j // (2 * size) == i // (2 * size)) & (j // size < i // size)
    arrays = dict(
        x=given["x"], p=given["p"], ffn1_norm_pre=given["ffn1_norm_pre"], ffn1_w_gate=given["ffn1_w_gate"],
        ffn1_w_up=given["ffn1_w_up"], ffn1_w_down=given["ffn1_w_down"], ffn1_norm_post=given["ffn1_norm_post"],
        mix_norm_pre=given["mix_norm_pre"], w_in=given["w_in"],
        conv_w=given["gdn_conv_w"].reshape(CONV, 12, P).transpose(2, 0, 1),
        a_log=given["gdn_a_log"], dt_bias=given["gdn_dt_bias"],
        norm_w=np.repeat(given["gdn_norm_w"][:, None], 4, axis=1),
        rwkv_params=rows("rwkv_mu", "rwkv_w0", "rwkv_a0", "rwkv_k_k", "rwkv_k_a", "rwkv_r_k", "rwkv_gn_w", "rwkv_gn_b"),
        w2=given["rwkv_w2"], a2=given["rwkv_a2"], g2=given["rwkv_g2"], w_out=given["w_out"],
        mix_norm_post=given["mix_norm_post"], ffn2_norm_pre=given["ffn2_norm_pre"],
        ffn2_w_gate=given["ffn2_w_gate"], ffn2_w_up=given["ffn2_w_up"], ffn2_w_down=given["ffn2_w_down"],
        ffn2_norm_post=given["ffn2_norm_post"], ple_norm_pre=given["ple_norm_pre"], ple_w_gate=given["ple_w_gate"],
        ple_w_proj=given["ple_w_proj"], ple_norm_post=given["ple_norm_post"], masks=masks)
    nc = bacc.Bacc("TRN2", target_bir_lowering=False, num_devices=1)
    launched, args = {}, {}
    for name, a in arrays.items():
        launched[f"in_{name}"] = np.ascontiguousarray(a)
        args[name] = nc.dram_tensor(f"in_{name}", a.shape, mybir.dt.from_np(a.dtype), kind="ExternalInput").ap()
    args["out"] = nc.dram_tensor("out_x", (SEQ, D), F32, kind="ExternalOutput").ap()
    layer(nc, **args)
    result = run_bass_kernel_spmd(nc, [launched], core_ids=[0])
    return result.results[0]["out_x"].reshape(1, SEQ, D)
```

```python
from contextlib import ExitStack

import concourse.bass as bass
from concourse import mybir

F32 = mybir.dt.float32
F32R = mybir.dt.float32r
U32 = mybir.dt.uint32
ALU = mybir.AluOpType
ACT = mybir.ActivationFunctionType

P = 128
SEQ = 1024
D = 1024
D_FF = 2816
D_PLE = 256
NT = SEQ // P
ND = D // P
HALF = 512
NH = SEQ // HALF
NORM_EPS = 1e-6


class Stage:

    def __init__(self, nc, tag):
        self.nc, self.tag, self.stack, self.sems = nc, tag, ExitStack(), []

    def __enter__(self):
        self.stack.__enter__()
        return self

    def __exit__(self, *what):
        self.stack.__exit__(*what)
        if self.sems:
            self.nc.clear_and_free_semaphores(self.sems)
            self.nc.all_engine_barrier()

    def sbuf(self, name, shape, dtype=F32):
        return self.stack.enter_context(self.nc.sbuf_tensor(f"{self.tag}_{name}", shape, dtype))

    def psum(self, name, shape, dtype=F32):
        return self.stack.enter_context(self.nc.psum_tensor(f"{self.tag}_{name}", shape, dtype))

    def sem(self, name):
        self.sems.append(self.nc.alloc_semaphore(f"{self.tag}_{name}"))
        return self.sems[-1]


def split_matmul(nc, out, weights, moving, first, last):
    (w_hi, w_lo), (m_hi, m_lo) = weights, moving
    nc.tensor.matmul(out, w_hi, m_hi, start=first, stop=False)
    nc.tensor.matmul(out, w_hi, m_lo, start=False, stop=False)
    return nc.tensor.matmul(out, w_lo, m_hi, start=False, stop=last)


def row_of(vector):
    return bass.AP(tensor=vector.tensor, offset=vector.offset, ap=[[0, P], [1, vector.shape[-1]]])


def residual_norm(nc, tag, x_in, x_out, branch, post_gain, share, pre_gain, h, identity):
    QUARTER = 0.25
    has_branch, has_h = branch is not None, pre_gain is not None
    with Stage(nc, tag) as st:
        x = st.sbuf("x", [P, 2, D])
        squares = st.sbuf("squares", [P, 2, D])
        normed = st.sbuf("normed", [P, 2, D])
        added = st.sbuf("added", [P, 2, D])
        stats = st.sbuf("stats", [P, 2, 8])
        post_row = st.sbuf("post_row", [P, D])
        pre_row = st.sbuf("pre_row", [P, D])
        turned = st.psum("turned", [P, 4, HALF])
        rows_in, row_shared = st.sem("rows_in"), st.sem("row_shared")
        x_loaded = [st.sem(f"x_loaded{u}") for u in range(2)]
        x_stored = [st.sem(f"x_stored{u}") for u in range(2)]
        branch_squared, branch_mean, branch_root = st.sem("branch_squared"), st.sem("branch_mean"), st.sem("branch_root")
        branch_inverse, branch_scaled, x_ready = st.sem("branch_inverse"), st.sem("branch_scaled"), st.sem("x_ready")
        x_squared, x_mean, x_root = st.sem("x_squared"), st.sem("x_mean"), st.sem("x_root")
        x_inverse, x_normed = st.sem("x_inverse"), st.sem("x_normed")
        transposed, hi_done, lo_done = st.sem("transposed"), st.sem("hi_done"), st.sem("lo_done")
        block = st.stack.enter_context(nc.Block())

        def at(u):
            return added[:, u] if has_branch else x[:, u]

        def branch_tile(n):
            return branch[:, bass.ds(n, 1), :].rearrange("p a d -> p (a d)")

        def h_part(part, n, b):
            return h[part][:, 4 * b:4 * b + 4, bass.ds(n * P, P)]

        def staggered(engine, step):
            step(-1, 1, 1, has_branch, False, False)
            step(0, 0, 1, has_branch, has_h, False)
            with engine.Fori(0, NT // 2 - 1) as i:
                step(2 * i + 1, 1, i + 2, has_branch, has_h, has_h)
                step(2 * i + 2, 0, i + 2, has_branch, has_h, has_h)
            step(NT - 1, 1, NT // 2 + 1, False, has_h, has_h)
            step(NT, 0, NT // 2 + 1, False, False, has_h)

        def early(n, count):
            return isinstance(n, int) and n < count

        @block.sync
        def _(sp):
            if has_branch:
                sp.dma_start(post_row[:], row_of(post_gain)).then_inc(rows_in, 16)
            if has_h:
                sp.dma_start(pre_row[:], row_of(pre_gain)).then_inc(rows_in, 16)
            for u in range(2):
                sp.dma_start(x[:, u], x_in[u * P:(u + 1) * P, :]).then_inc(x_loaded[u], 16)

            def store(n, u):
                sp.wait_ge(x_ready, n + 1)
                sp.dma_start(x_out[bass.ds(n * P, P), :], added[:, u]).then_inc(x_stored[u], 16)

            with sp.Fori(0, NT // 2 - 1) as i:
                for u in range(2):
                    n = 2 * i + u
                    if has_branch:
                        store(n, u)
                    else:
                        sp.wait_ge(x_normed, n + 1)
                    sp.dma_start(x[:, u], x_in[bass.ds((n + 2) * P, P), :]).then_inc(x_loaded[u], 16)
            if has_branch:
                for u in range(2):
                    store(NT - 2 + u, u)
                for u in range(2):
                    sp.wait_ge(x_stored[u], 16 * (NT // 2))

        @block.scalar
        def _(act):
            def step(k, v, pair, adds, norms, turns):
                if adds:
                    if not early(k + 1, 1):
                        act.wait_ge(branch_mean, k + 1)
                    nc.scalar.activation(squares[:, 0], branch_tile(k + 1), ACT.Square,
                                         accum_out=stats[:, 1 - v, 0:1]).then_inc(branch_squared, 1)
                if norms:
                    if has_branch:
                        act.wait_ge(x_ready, k + 1)
                    else:
                        act.wait_ge(x_loaded[v], 16 * (pair - v))
                    if not early(k, 1):
                        act.wait_ge(x_mean, k)
                    nc.scalar.activation(squares[:, 1], at(v), ACT.Square, accum_out=stats[:, v, 4:5]).then_inc(x_squared, 1)
                if adds:
                    act.wait_ge(branch_mean, k + 2)
                    nc.scalar.activation(stats[:, 1 - v, 2:3], stats[:, 1 - v, 1:2], ACT.Sqrt).then_inc(branch_root, 1)
                if norms:
                    act.wait_ge(x_mean, k + 1)
                    nc.scalar.activation(stats[:, v, 6:7], stats[:, v, 5:6], ACT.Sqrt).then_inc(x_root, 1)
                if turns:
                    for b in range(2):
                        act.wait_ge(transposed, 2 * k + b - 1)
                        nc.scalar.copy(h_part(0, k - 1, b), turned[:, 2 * (1 - v) + b].rearrange("p (c t) -> p c t", t=P)).then_inc(hi_done, 1)

            staggered(act, step)

        if has_branch:
            @block.gpsimd
            def _(pool):
                def step(k, v, pair, adds, norms, turns):
                    if adds:
                        pool.wait_ge(branch_scaled, k + 2)
                        pool.wait_ge(x_loaded[1 - v], 16 * pair)
                        nc.gpsimd.tensor_tensor(added[:, 1 - v], added[:, 1 - v], x[:, 1 - v], ALU.add).then_inc(x_ready, 1)

                staggered(pool, step)

        @block.vector
        def _(dve):
            dve.wait_ge(rows_in, 16 * (has_branch + has_h))
            if has_branch:
                nc.vector.tensor_scalar(post_row[:], post_row[:], share, None, ALU.mult).then_inc(row_shared, 1)
                dve.wait_ge(row_shared, 1)

            def inverse_root(s, done, n):
                nc.vector.reciprocal(s[:, 3:4], s[:, 2:3]).then_inc(done, 1)
                dve.wait_ge(done, 3 * n + 1)
                nc.vector.scalar_tensor_tensor(s[:, 0:1], s[:, 1:2], s[:, 3:4], s[:, 2:3], ALU.mult, ALU.add).then_inc(done, 1)
                dve.wait_ge(done, 3 * n + 2)
                nc.vector.reciprocal(s[:, 3:4], s[:, 0:1]).then_inc(done, 1)
                dve.wait_ge(done, 3 * n + 3)

            def step(k, v, pair, adds, norms, turns):
                n, u = k + 1, 1 - v
                if adds:
                    dve.wait_ge(branch_squared, n + 1)
                    nc.vector.tensor_scalar(stats[:, u, 1:2], stats[:, u, 0:1], QUARTER / D, QUARTER * NORM_EPS, ALU.mult, ALU.add).then_inc(branch_mean, 1)
                if norms:
                    dve.wait_ge(x_squared, k + 1)
                    nc.vector.tensor_scalar(stats[:, v, 5:6], stats[:, v, 4:5], QUARTER / D, QUARTER * NORM_EPS, ALU.mult, ALU.add).then_inc(x_mean, 1)
                if adds:
                    dve.wait_ge(branch_root, n + 1)
                    inverse_root(stats[:, u, 0:4], branch_inverse, n)
                    if not early(n, 2):
                        dve.wait_ge(x_stored[u], 16 * (pair - 1))
                    nc.vector.scalar_tensor_tensor(added[:, u], branch_tile(n), stats[:, u, 3:4], post_row[:],
                                                   ALU.mult, ALU.mult).then_inc(branch_scaled, 1)
                if norms:
                    dve.wait_ge(x_root, k + 1)
                    inverse_root(stats[:, v, 4:8], x_inverse, k)
                    nc.vector.scalar_tensor_tensor(normed[:, v], at(v), stats[:, v, 7:8], pre_row[:],
                                                   ALU.mult, ALU.mult).then_inc(x_normed, 1)
                if turns:
                    for b in range(2):
                        dve.wait_ge(hi_done, 2 * k + b - 1)
                        nc.vector.tensor_tensor(h_part(1, k - 1, b), turned[:, 2 * u + b].rearrange("p (c t) -> p c t", t=P),
                                                h_part(0, k - 1, b).bitcast(F32), ALU.subtract).then_inc(lo_done, 1)

            staggered(dve, step)

        if has_h:
            @block.tensor
            def _(pe):
                with pe.Fori(0, NT // 2) as i:
                    for u in range(2):
                        n = 2 * i + u
                        pe.wait_ge(x_normed, n + 1)
                        for b in range(2):
                            for c in range(4):
                                d = 4 * b + c
                                last = nc.tensor.transpose(turned[:, 2 * u + b, c * P:(c + 1) * P],
                                                           normed[:, u, d * P:(d + 1) * P], identity)
                            last.then_inc(transposed, 1)


def swiglu(nc, tag, h, w_gate, w_up, w_down, out):
    CH = D_FF // P
    GROUPS = CH // 2
    LOOPS = (GROUPS - 1) // 2
    START = 2 * NT + 1
    with Stage(nc, tag) as st:
        up_raw = st.sbuf("up_raw", [P, 2, 2, ND, P])
        up_hi = st.sbuf("up_hi", [P, 2, 2, ND, P], F32R)
        up_lo = st.sbuf("up_lo", [P, 2, 2, ND, P], F32R)
        down_raw = st.sbuf("down_raw", [P, 2, 2, HALF])
        down_hi = st.sbuf("down_hi", [P, 2, 2, HALF], F32R)
        down_lo = st.sbuf("down_lo", [P, 2, 2, HALF], F32R)
        a_hi = st.sbuf("a_hi", [P, 4, SEQ], F32R)
        a_lo = st.sbuf("a_lo", [P, 4, SEQ], F32R)
        product = st.sbuf("product", [P, 2, HALF])
        up_ps = st.psum("up_ps", [P, 2, 2, HALF])
        down_ps = st.psum("down_ps", [P, 4, HALF])
        up_loaded = [st.sem(f"up_loaded{u}") for u in range(2)]
        down_loaded = [st.sem(f"down_loaded{u}") for u in range(2)]
        up_rounded, up_split = st.sem("up_rounded"), st.sem("up_split")
        down_rounded, down_split = st.sem("down_rounded"), st.sem("down_split")
        up_summed, silu_done, multiplied = st.sem("up_summed"), st.sem("silu_done"), st.sem("multiplied")
        a_rounded, a_split = st.sem("a_rounded"), st.sem("a_split")
        down_summed, down_added = st.sem("down_summed"), st.sem("down_added")
        block = st.stack.enter_context(nc.Block())

        gate_cols = w_gate.rearrange("(d p) f -> p d f", p=P)
        up_cols = w_up.rearrange("(d p) f -> p d f", p=P)
        down_rows = w_down.rearrange("(c p) n -> p c n", p=P)

        def steps(engine, up, down):
            up(0, 0, 0)
            up(1, 1, 0)
            with engine.Fori(0, LOOPS) as i:
                for g in range(2):
                    up(4 * i + 2 * g + 2, (2 * g + 2) % 4, 2 * i + g + 1)
                    up(4 * i + 2 * g + 3, (2 * g + 3) % 4, 2 * i + g + 1)
                    down(2 * i + g, g)


        def is_first(c, n=1):
            return isinstance(c, int) and c < n

        @block.sync
        def _(sp):
            def load_up(c, u, free):
                if free is not None:
                    sp.wait_ge(up_split, free)
                for k, cols in enumerate((gate_cols, up_cols)):
                    sp.dma_start(up_raw[:, u, k], cols[:, :, bass.ds(c * P, P)]).then_inc(up_loaded[u], 16)

            def load_down(g, half, free):
                if free is not None:
                    sp.wait_ge(down_split, free)
                sp.dma_start(down_raw[:, half], down_rows[:, bass.ds(2 * g, 2), half * HALF:(half + 1) * HALF]).then_inc(down_loaded[half], 16)

            load_up(0, 0, None)
            load_up(1, 1, None)
            load_down(0, 0, None)
            load_down(0, 1, None)
            with sp.Fori(1, GROUPS) as g:
                load_up(2 * g, 0, 2 * g - 1)
                load_up(2 * g + 1, 1, 2 * g)
                load_down(g, 0, 2 * g - 1)
                load_down(g, 1, 2 * g)

        @block.scalar
        def _(act):
            def finish(c, q, g):
                for t in range(NH):
                    n = 2 * c + t
                    act.wait_ge(up_summed, n + 1)
                    if not is_first(c):
                        act.wait_ge(a_split, n - 1)
                    nc.scalar.activation(product[:, t], up_ps[:, t, 0], ACT.Silu).then_inc(silu_done, 1)
                    act.wait_ge(multiplied, n + 1)
                    act.wait_ge(down_added, START + 2 * NT * (g - 1))
                    nc.scalar.copy(a_hi[:, q, t * HALF:(t + 1) * HALF], product[:, t]).then_inc(a_rounded, 1)

            def round_down(g):
                for half in range(2):
                    act.wait_ge(down_loaded[half], 16 * (g + 1))
                    act.wait_ge(down_added, START + NT * (2 * g + half - 1))
                    nc.scalar.copy(down_hi[:, half], down_raw[:, half]).then_inc(down_rounded, 1)

            def up(c, q, g):
                u = q % 2
                act.wait_ge(up_loaded[u], 32 * (g + 1))
                if not is_first(c, 2):
                    act.wait_ge(up_summed, 2 * c - 2)
                nc.scalar.copy(up_hi[:, u], up_raw[:, u]).then_inc(up_rounded, 1)
                if not is_first(c):
                    finish(c - 1, (q - 1) % 4, g - (1 - u))
                if not is_first(c, 2) and u == 0:
                    round_down(g - 1)

            steps(act, up, lambda g, odd: None)
            finish(CH - 1, (CH - 1) % 4, GROUPS - 1)
            round_down(GROUPS - 1)

        @block.gpsimd
        def _(pool):
            def finish(c, q, g):
                for t in range(NH):
                    part = (slice(None), q, slice(t * HALF, (t + 1) * HALF))
                    pool.wait_ge(a_rounded, 2 * c + t + 1)
                    nc.gpsimd.tensor_tensor(a_lo[part], product[:, t], a_hi[part].bitcast(F32), ALU.subtract).then_inc(a_split, 1)

            def split_down(g):
                for half in range(2):
                    pool.wait_ge(down_rounded, 2 * g + half + 1)
                    nc.gpsimd.tensor_tensor(down_lo[:, half], down_raw[:, half], down_hi[:, half].bitcast(F32), ALU.subtract).then_inc(down_split, 1)

            def up(c, q, g):
                u = q % 2
                pool.wait_ge(up_rounded, c + 1)
                nc.gpsimd.tensor_tensor(up_lo[:, u], up_raw[:, u], up_hi[:, u].bitcast(F32), ALU.subtract).then_inc(up_split, 1)
                if not is_first(c):
                    finish(c - 1, (q - 1) % 4, g - (1 - u))
                if not is_first(c, 2) and u == 0:
                    split_down(g - 1)

            steps(pool, up, lambda g, odd: None)
            finish(CH - 1, (CH - 1) % 4, GROUPS - 1)
            split_down(GROUPS - 1)

        @block.vector
        def _(dve):
            nc.vector.nop().then_inc(down_added, 1)
            for t in range(NT):
                for half in range(2):
                    nc.vector.memset(out[:, t, half * HALF:(half + 1) * HALF], 0.0).then_inc(down_added, 1)

            def up(c, q, g):
                for t in range(NH):
                    n = 2 * c + t
                    dve.wait_ge(silu_done, n + 1)
                    nc.vector.tensor_tensor(product[:, t], product[:, t], up_ps[:, t, 1], ALU.mult).then_inc(multiplied, 1)

            def down(g, odd):
                for half in range(2):
                    for t in range(NT):
                        k = half * NT + t
                        dve.wait_ge(down_summed, 2 * NT * g + k + 1)
                        dve.wait_ge(down_added, START + 2 * NT * g + k)
                        to = out[:, t, half * HALF:(half + 1) * HALF]
                        nc.vector.tensor_tensor(to, to, down_ps[:, k % 4], ALU.add).then_inc(down_added, 1)

            steps(dve, up, down)
            down(GROUPS - 1, (GROUPS - 1) % 2)

        @block.tensor
        def _(pe):
            def up(c, q, g):
                u = q % 2
                pe.wait_ge(up_split, c + 1)
                for t in range(NH):
                    if not is_first(c):
                        pe.wait_ge(multiplied, 2 * c + t - 1)
                    for k in range(2):
                        for d in range(ND):
                            last = split_matmul(nc, up_ps[:, t, k], (up_hi[:, u, k, d], up_lo[:, u, k, d]),
                                                tuple(part[:, d, t * HALF:(t + 1) * HALF] for part in h), d == 0, d == ND - 1)
                    last.then_inc(up_summed, 1)

            def down(g, odd):
                pe.wait_ge(a_split, 4 * g + 4)
                for half in range(2):
                    pe.wait_ge(down_split, 2 * g + half + 1)
                    for t in range(NT):
                        k = half * NT + t
                        pe.wait_ge(down_added, START + 2 * NT * g + k - 3)
                        for j in range(2):
                            slot = 2 * odd + j
                            last = split_matmul(nc, down_ps[:, k % 4], (a_hi[:, slot, t * P:(t + 1) * P], a_lo[:, slot, t * P:(t + 1) * P]),
                                                (down_hi[:, half, j], down_lo[:, half, j]), j == 0, j == 1)
                        last.then_inc(down_summed, 1)

            steps(pe, up, down)
            down(GROUPS - 1, (GROUPS - 1) % 2)


GDN_HEADS, GDN_DK = 4, 128
CONV = 4
RWKV_BLOCKS = 4
GDN_QK, GDN_V, GDN_Z = 0, 1024, 1536
GDN_SMALL = 2048
RWKV_COLS = 2056
RWKV_W = 512
L2_EPS = 1e-6

S_Q, S_K, S_V, S_INCL, S_STRICT, S_RWKV = 0, 8, 16, 20, 24, 28
R_KK, R_R, R_K, R_B, R_V, R_SLOTS = 0, 1, 2, 3, 4, 5
SLOTS = S_RWKV + R_SLOTS * RWKV_BLOCKS
COLS = 16
C_GDN = SLOTS * P
TILE_W = SLOTS * P + COLS


class Steps:

    def __init__(self, sem, names):
        self.sem, self.names, self.next = sem, names.split(), 0

    def open(self, engine):
        engine.nop().then_inc(self.sem, len(self.names))

    def done(self, instruction, name):
        assert name == self.names[self.next], (name, self.names[self.next])
        self.next = (self.next + 1) % len(self.names)
        instruction.then_inc(self.sem, 1)

    def wait(self, engine, name, turn):
        engine.wait_ge(self.sem, len(self.names) * (turn + 1) + self.names.index(name) + 1)


def stream_weights(nc, pool, gate, w_raw, w_hi, w_lo, w_loaded, w_rounded, w_split, projected, blocks):
    def split(k, s, first):
        pool.wait_ge(w_loaded[s], 16 * (k // 2 + 1) if isinstance(k, int) else 16 * first)
        if not (isinstance(k, int) and k < 2):
            pool.wait_ge(projected, k - 1)
        nc.gpsimd.tensor_tensor(gate[:, 0:1], gate[:, 1:2], gate[:, 1:2], ALU.add)
        nc.gpsimd.tensor_copy(w_hi[:, s], w_raw[:, s]).then_inc(w_rounded, 1)
        pool.wait_ge(w_rounded, k + 2)
        nc.gpsimd.tensor_tensor(w_lo[:, s], w_raw[:, s], w_hi[:, s].bitcast(F32), ALU.subtract).then_inc(w_split, 1)

    nc.gpsimd.memset(gate, 0.0).then_inc(w_rounded, 1)
    pool.wait_ge(w_rounded, 1)
    split(0, 0, 1)
    split(1, 1, 1)
    with pool.Fori(1, blocks // 2) as i:
        split(2 * i, 0, i + 1)
        split(2 * i + 1, 1, i + 1)
    if blocks % 2:
        split(blocks - 1, 0, None)


def gdn_projection(nc, h, w_in, conv_w, a_log, dt_bias, masks, scratch, z_gate):
    with Stage(nc, "gp") as st:
        w_raw = st.sbuf("w_raw", [P, 2, ND, P])
        w_hi = st.sbuf("w_hi", [P, 2, ND, P], F32R)
        w_lo = st.sbuf("w_lo", [P, 2, ND, P], F32R)
        x_ext = st.sbuf("x_ext", [P, 2, 4 + SEQ])
        conv = st.sbuf("conv", [P, 2, SEQ])
        act_out = st.sbuf("act_out", [P, 2, SEQ])
        square = st.sbuf("square", [P, SEQ])
        root = st.sbuf("root", [P, SEQ])
        unit = st.sbuf("unit", [P, 2, SEQ])
        scaled = st.sbuf("scaled", [P, 2, SEQ])
        rows = st.sbuf("rows", [P, 8, SEQ])
        taps = st.sbuf("taps", [P, CONV, 12])
        scale_col = st.sbuf("scale_col", [P, 8])
        eps = st.sbuf("eps", [P, 1])
        gate = st.sbuf("gate", [P, 2])
        mask = st.sbuf("mask", [P, 4, P])
        a_row = st.sbuf("a_row", [P, GDN_HEADS])
        dt_row = st.sbuf("dt_row", [P, GDN_HEADS])
        s = st.sbuf("small", [P, 12, NT, GDN_HEADS])
        gb = st.sbuf("gb", [P, NT, 8])
        gc_rows = st.sbuf("gc_rows", [P, 4, P])
        spread = st.sbuf("spread", [P, 2, 4, P])
        diag = st.sbuf("diag", [P, 4, P])
        gaps = st.sbuf("gaps", [P, 4, P])
        decay = st.sbuf("decay", [P, 4, P])
        decays = st.sbuf("decays", [P, 8, P])
        exps = st.sbuf("exps", [P, 16])
        cols = st.sbuf("cols", [P, 16])
        proj = st.psum("proj", [P, 2, 2, HALF])
        sums = st.psum("sums", [P, 2, HALF])
        row_ps = st.psum("row_ps", [P, 2, HALF])

        setup, ready = st.sem("setup"), st.sem("ready")
        w_loaded = [st.sem(f"w_loaded{u}") for u in range(2)]
        w_rounded, w_split, projected = st.sem("w_rounded"), st.sem("w_split"), st.sem("projected")
        copied, tapped, convolved, silu_done = st.sem("copied"), st.sem("tapped"), st.sem("convolved"), st.sem("silu_done")
        squared, summed, rooted = st.sem("squared"), st.sem("summed"), st.sem("rooted")
        unit_ready, scaled_ready = st.sem("unit_ready"), st.sem("scaled_ready")
        turned, small_dve, small_act = st.sem("turned"), st.sem("small_dve"), st.sem("small_act")
        spread_ready, rows_summed, rows_copied = st.sem("spread_ready"), st.sem("rows_summed"), st.sem("rows_copied")
        col_step, gaps_ready, decayed, decays_ready = st.sem("col_step"), st.sem("gaps_ready"), st.sem("decayed"), st.sem("decays_ready")
        exps_done = st.sem("exps_done")
        act_stored, decay_stored = [st.sem(f"act_stored{u}") for u in range(2)], st.sem("decay_stored")
        unit_stored, scaled_stored = [st.sem(f"unit_stored{u}") for u in range(2)], [st.sem(f"scaled_stored{u}") for u in range(2)]
        block = st.stack.enter_context(nc.Block())

        w_cols = w_in.rearrange("(d p) f -> p d f", p=P)
        tiles = scratch.rearrange("c p w -> p c w")
        K_V, K_Z, K_QK, BLOCKS = 1, 5, 9, 17
        SETUP = 16 * 4

        def in_pairs(engine, body, n, base):
            with engine.Fori(0, n // 2) as i:
                for u in range(2):
                    body(2 * i + u, u, i)

        def lagged(engine, first, second):
            first(0, 0, 0)
            with engine.Fori(0, 3) as i:
                for u in range(2):
                    first(2 * i + u + 1, (u + 1) % 2, i + u)
                    second(2 * i + u, u, i)
            first(7, 1, 3)
            second(6, 0, 3)
            second(7, 1, 3)

        @block.sync
        def _(sp):
            for stored in act_stored + unit_stored + scaled_stored:
                sp.nop().then_inc(stored, 16)
            sp.nop().then_inc(decay_stored, 32)
            sp.dma_start(taps[:], conv_w).then_inc(setup, 16)
            sp.dma_start(mask[:], masks[:, 0:4]).then_inc(setup, 16)
            sp.dma_start(a_row[:], row_of(a_log)).then_inc(setup, 16)
            sp.dma_start(dt_row[:], row_of(dt_bias)).then_inc(setup, 16)

            def load(col, s_, split):
                if split is not None:
                    sp.wait_ge(w_split, split)
                sp.dma_start(w_raw[:, s_], w_cols[:, :, bass.ds(col, P)]).then_inc(w_loaded[s_], 16)

            load(GDN_SMALL, 0, None)
            load(GDN_V, 1, None)

            def decays_out(c):
                sp.wait_ge(decays_ready, c + 1)
                sp.dma_start(scratch[bass.ds(c, 1), :, S_INCL * P:S_RWKV * P].rearrange("a p w -> p (a w)"),
                             decays[:].rearrange("p s t -> p (s t)")).then_inc(decay_stored, 16)
                sp.dma_start(scratch[bass.ds(c, 1), :, C_GDN:C_GDN + 16].rearrange("a p w -> p (a w)"), cols[:]).then_inc(decay_stored, 16)

            def v_step(j, u, i):
                load(GDN_V + (j + 1) * P, u, j + 1)
                decays_out(j)
                sp.wait_ge(silu_done, j + 1)
                sp.dma_start(tiles[:, :, bass.ds((S_V + j) * P, P)], act_out[:, u].rearrange("p (c t) -> p c t", t=P)).then_inc(act_stored[u], 16)

            def z_step(j, u, i):
                load(((GDN_Z + (j + 1) * P) % GDN_SMALL), u, j + 5)
                decays_out(j + 4)
                sp.wait_ge(silu_done, j + 5)
                sp.dma_start(z_gate[bass.ds(j, 1)].rearrange("a p t -> p (a t)"), act_out[:, u]).then_inc(act_stored[u], 16)

            in_pairs(sp, v_step, 4, K_V)
            for j in range(4):
                z_step(j, j % 2, j // 2)

            def qk_load(b, u, i):
                load((b + 1) * P, (u + 0) % 2, b + K_QK)

            def qk_store(b, u, i):
                sp.wait_ge(unit_ready, b + 2)
                sp.dma_start(tiles[:, :, bass.ds(2 * b * P, P)], unit[:, u].rearrange("p (c t) -> p c t", t=P)).then_inc(unit_stored[u], 16)
                sp.wait_ge(scaled_ready, b + 1)
                sp.dma_start(tiles[:, :, bass.ds((2 * b + 1) * P, P)], scaled[:, u].rearrange("p (c t) -> p c t", t=P)).then_inc(scaled_stored[u], 16)

            lagged(sp, lambda b, u, i: None if isinstance(b, int) and b == 7 else qk_load(b, u, i), qk_store)
            for u in range(2):
                sp.wait_ge(act_stored[u], 16 * 5)
                sp.wait_ge(unit_stored[u], 16 * 5)
                sp.wait_ge(scaled_stored[u], 16 * 5)
            sp.wait_ge(decay_stored, 32 * (NT + 1))

        @block.gpsimd
        def _(pool):
            stream_weights(nc, pool, gate[:], w_raw, w_hi, w_lo, w_loaded, w_rounded, w_split, projected, BLOCKS)

        @block.tensor
        def _(pe):
            def project(k, s_):
                pe.wait_ge(w_split, k + 1)
                if not (isinstance(k, int) and k < 2):
                    pe.wait_ge(copied, k)
                for t in range(NH):
                    for d in range(ND):
                        last = split_matmul(nc, proj[:, s_, t], (w_hi[:, s_, d], w_lo[:, s_, d]),
                                            tuple(part[:, d, t * HALF:(t + 1) * HALF] for part in h), d == 0, d == ND - 1)
                last.then_inc(projected, 1)

            def sum_rows(c):
                pe.wait_ge(spread_ready, 2 * c + 2)
                pe.wait_ge(rows_copied, 2 * c + 1)
                for n in range(2):
                    last = nc.tensor.matmul(row_ps[:, n], mask[:, 1], spread[:, n].rearrange("p n t -> p (n t)"), start=True, stop=True)
                last.then_inc(rows_summed, 1)

            project(0, 0)
            pe.wait_ge(setup, SETUP)
            pe.wait_ge(copied, 2)
            for c in range(NT):
                last = nc.tensor.transpose(sums[:, c // 4, (c % 4) * P:(c % 4 + 1) * P], x_ext[:, 0, 4 + c * P:4 + (c + 1) * P], mask[:, 0])
            last.then_inc(turned, 1)

            def vz_step(j, u, i):
                project(j + 1, (u + 1) % 2)
                sum_rows(j)

            in_pairs(pe, vz_step, 8, K_V)

            def sum_squares(b, u, i):
                pe.wait_ge(squared, b + 1)
                for t in range(NH):
                    pe.wait_ge(rooted, 2 * b + 1)
                    last = nc.tensor.matmul(sums[:, t], mask[:, 1], square[:, t * HALF:(t + 1) * HALF], start=True, stop=True)
                last.then_inc(summed, 1)

            lagged(pe, lambda b, u, i: project(b + K_QK, (u + 1) % 2), sum_squares)

        @block.scalar
        def _(act):
            act.wait_ge(setup, SETUP)
            act.wait_ge(ready, 1)

            def copy_block(k, s_):
                act.wait_ge(projected, k + 1)
                nc.scalar.copy(x_ext[:, s_, 4:], proj[:, s_].rearrange("p n t -> p (n t)")).then_inc(copied, 1)

            copy_block(0, 0)
            act.wait_ge(small_dve, 1)
            nc.scalar.activation(s[:, 0], gb[:, :, 0:4], ACT.Sigmoid).then_inc(small_act, 1)
            nc.scalar.activation(a_row[:], a_row[:], ACT.Exp).then_inc(small_act, 1)
            act.wait_ge(small_dve, 4)
            nc.scalar.activation(s[:, 4], s[:, 3], ACT.Exp, scale=-1.0).then_inc(small_act, 1)
            act.wait_ge(small_dve, 5)
            nc.scalar.activation(s[:, 6], s[:, 5], ACT.Ln).then_inc(small_act, 1)

            def rows_of(c):
                act.wait_ge(rows_summed, c + 1)
                nc.scalar.copy(gc_rows[:], row_ps[:, 0].rearrange("p (n t) -> p n t", t=P)).then_inc(rows_copied, 1)
                nc.scalar.copy(rows[:, 4:8, bass.ds(c * P, P)], row_ps[:, 1].rearrange("p (n t) -> p n t", t=P)).then_inc(rows_copied, 1)
                act.wait_ge(rows_copied, 2 * c + 3)
                nc.scalar.activation(rows[:, 0:4, bass.ds(c * P, P)], gc_rows[:], ACT.Exp)
                act.wait_ge(gaps_ready, c + 1)
                nc.scalar.activation(decay[:], gaps[:], ACT.Exp).then_inc(decayed, 1)
                nc.scalar.activation(exps[:, 0:12], exps[:, 0:12], ACT.Exp).then_inc(exps_done, 1)

            def tap_last(b, s_, blk, used):
                nc.scalar.activation(conv[:, s_], x_ext[:, s_, 4:], ACT.Copy, scale=taps[:, CONV - 1, bass.ds(blk, 1)]).then_inc(tapped, 1)

            def v_step(j, u, i):
                s_ = (u + 1) % 2
                copy_block(j + K_V, s_)
                act.wait_ge(copied, j + K_V + 2)
                tap_last(j, s_, j + 8, None)
                rows_of(j)
                act.wait_ge(convolved, 3 * j + 3)
                act.wait_ge(act_stored[u], 16 * (i + 1))
                nc.scalar.activation(act_out[:, u], conv[:, s_], ACT.Silu).then_inc(silu_done, 1)

            def z_step(j, u, i):
                s_ = (u + 1) % 2
                copy_block(j + K_Z, s_)
                rows_of(j + 4)
                act.wait_ge(copied, j + K_Z + 2)
                act.wait_ge(act_stored[u], 16 * (i + 3))
                nc.scalar.activation(act_out[:, u], x_ext[:, s_, 4:], ACT.Silu).then_inc(silu_done, 1)

            in_pairs(act, v_step, 4, K_V)
            in_pairs(act, z_step, 4, K_Z)

            def qk_first(b, u, i):
                s_ = (u + 1) % 2
                copy_block(b + K_QK, s_)
                act.wait_ge(copied, b + K_QK + 2)
                tap_last(b, s_, b, None)
                act.wait_ge(convolved, 3 * (b + 4) + 3)
                act.wait_ge(act_stored[u], 16 * 5)
                if not (isinstance(b, int) and b < 1):
                    act.wait_ge(unit_ready, b)
                nc.scalar.activation(act_out[:, u], conv[:, s_], ACT.Silu).then_inc(silu_done, 1)
                act.wait_ge(silu_done, b + 9)
                if not (isinstance(b, int) and b < 1):
                    act.wait_ge(summed, b)
                nc.scalar.activation(square[:], act_out[:, u], ACT.Square).then_inc(squared, 1)

            def qk_second(b, u, i):
                act.wait_ge(summed, b + 1)
                act.wait_ge(unit_ready, b + 1)
                nc.scalar.activation(root[:], sums[:].rearrange("p n t -> p (n t)"), ACT.Ln, bias=eps[:]).then_inc(rooted, 1)
                act.wait_ge(rooted, 2 * b + 2)
                nc.scalar.activation(root[:], root[:], ACT.Exp, scale=-0.5).then_inc(rooted, 1)

            lagged(act, qk_first, qk_second)

        @block.vector
        def _(dve):
            nc.vector.memset(eps[:], L2_EPS)
            nc.vector.memset(scale_col[:, 0:4], GDN_DK ** -0.5)
            nc.vector.memset(scale_col[:, 4:8], 1.0)
            nc.vector.memset(x_ext[:, :, 0:4], 0.0).then_inc(ready, 1)
            for free in (rows_copied, copied, rooted, unit_ready):
                nc.vector.nop().then_inc(free, 1)
            dve.wait_ge(setup, SETUP)
            dve.wait_ge(ready, 1)
            step = [0]

            def small(ins):
                ins.then_inc(small_dve, 1)
                step[0] += 1
                dve.wait_ge(small_dve, step[0])

            dt = dt_row[:].rearrange("p (a n) -> p a n", a=1).broadcast_to([P, NT, GDN_HEADS])
            ea = a_row[:].rearrange("p (a n) -> p a n", a=1).broadcast_to([P, NT, GDN_HEADS])
            dve.wait_ge(turned, 1)
            small(nc.vector.tensor_copy(gb[:], sums[:].rearrange("p n (c t) -> p (n c) t", t=P)[:, :, 0:8]))
            small(nc.vector.tensor_tensor(s[:, 1], gb[:, :, 4:8], dt, ALU.add))
            small(nc.vector.tensor_scalar(s[:, 2], s[:, 1], -1.0, None, ALU.mult))
            small(nc.vector.tensor_tensor(s[:, 3], s[:, 1], s[:, 2], ALU.max))
            dve.wait_ge(small_act, 3)
            small(nc.vector.tensor_scalar(s[:, 5], s[:, 4], 1.0, None, ALU.add))
            small(nc.vector.tensor_scalar(s[:, 7], s[:, 5], 1.0, None, ALU.is_equal))
            small(nc.vector.scalar_tensor_tensor(s[:, 8], s[:, 5], -1.0, s[:, 7], ALU.add, ALU.add))
            small(nc.vector.reciprocal(s[:, 9], s[:, 8]))
            dve.wait_ge(small_act, 4)
            small(nc.vector.tensor_tensor(s[:, 8], s[:, 6], s[:, 7], ALU.add))
            small(nc.vector.tensor_tensor(s[:, 8], s[:, 8], s[:, 9], ALU.mult))
            small(nc.vector.tensor_tensor(s[:, 8], s[:, 8], s[:, 4], ALU.mult))
            small(nc.vector.scalar_tensor_tensor(s[:, 10], s[:, 1], 0.0, s[:, 8], ALU.max, ALU.add))
            small(nc.vector.scalar_tensor_tensor(s[:, 10], s[:, 10], -1.0, ea, ALU.mult, ALU.mult))
            small(nc.vector.tensor_scalar(s[:, 11], s[:, 0], -1.0, None, ALU.mult))

            def over_heads(n):
                return mask[:, n:n + 1].broadcast_to([P, GDN_HEADS, P])

            def spread_rows(c):
                for n, (m, of) in enumerate(((2, 10), (0, 11))):
                    nc.vector.tensor_tensor(spread[:, n], over_heads(m), per_head(s[:, of, bass.ds(c, 1), :]), ALU.mult).then_inc(spread_ready, 1)

            def per_head(ap):
                return ap.rearrange("p a n -> p n a").broadcast_to([P, GDN_HEADS, P])

            def decays_of(c):
                g_rows = gc_rows[:]
                dve.wait_ge(rows_copied, 2 * c + 2)
                nc.vector.tensor_tensor(diag[:], g_rows, over_heads(0), ALU.mult).then_inc(col_step, 1)
                dve.wait_ge(col_step, 6 * c + 1)
                nc.vector.tensor_reduce(exps[:, 0:4], diag[:], mybir.AxisListType.X, ALU.add).then_inc(col_step, 1)
                nc.vector.tensor_copy(exps[:, 8:12], g_rows[:, :, P - 1]).then_inc(col_step, 1)
                dve.wait_ge(col_step, 6 * c + 3)
                nc.vector.tensor_tensor(gaps[:], g_rows, exps[:, 0:4].rearrange("p (n a) -> p n a", a=1).broadcast_to([P, GDN_HEADS, P]), ALU.subtract).then_inc(col_step, 1)
                nc.vector.tensor_tensor(exps[:, 4:8], exps[:, 8:12], exps[:, 0:4], ALU.subtract).then_inc(col_step, 1)
                dve.wait_ge(col_step, 6 * c + 5)
                nc.vector.tensor_scalar(exps[:, 4:8], exps[:, 4:8], 0.0, None, ALU.min).then_inc(col_step, 1)
                nc.vector.tensor_scalar(gaps[:], gaps[:], 0.0, None, ALU.min).then_inc(gaps_ready, 1)
                dve.wait_ge(exps_done, c + 1)
                dve.wait_ge(decay_stored, 32 * (c + 1))
                beta = s[:, 0, bass.ds(c, 1), :].rearrange("p a n -> p (a n)")
                minus_beta = s[:, 11, bass.ds(c, 1), :].rearrange("p a n -> p (a n)")
                nc.vector.tensor_copy(cols[:, 0:4], beta)
                nc.vector.tensor_tensor(cols[:, 4:8], exps[:, 0:4], minus_beta, ALU.mult)
                nc.vector.tensor_copy(cols[:, 8:16], exps[:, 4:12])
                nc.vector.tensor_tensor(decays[:, 0:4], decay[:], over_heads(2), ALU.mult)
                nc.vector.tensor_tensor(decays[:, 4:8], decay[:], over_heads(3), ALU.mult).then_inc(decays_ready, 1)

            def convolve(n, s_, blk):
                dve.wait_ge(tapped, n + 1)
                for j in range(CONV - 1):
                    if j:
                        dve.wait_ge(convolved, 3 * n + j)
                    nc.vector.scalar_tensor_tensor(conv[:, s_], x_ext[:, s_, j + 1:j + 1 + SEQ], taps[:, j, bass.ds(blk, 1)], conv[:, s_],
                                                   ALU.mult, ALU.add).then_inc(convolved, 1)

            def v_step(j, u, i):
                spread_rows(j)
                convolve(j, (u + 1) % 2, j + 8)
                decays_of(j)

            def z_step(j, u, i):
                spread_rows(j + 4)
                decays_of(j + 4)

            in_pairs(dve, v_step, 4, K_V)
            in_pairs(dve, z_step, 4, K_Z)

            def qk_first(b, u, i):
                convolve(b + 4, (u + 1) % 2, b)

            def qk_second(b, u, i):
                dve.wait_ge(rooted, 2 * b + 3)
                dve.wait_ge(unit_stored[u], 16 * (i + 1))
                dve.wait_ge(scaled_stored[u], 16 * (i + 1))
                nc.vector.scalar_tensor_tensor(unit[:, u], act_out[:, u], scale_col[:, bass.ds(b, 1)], root[:], ALU.mult, ALU.mult).then_inc(unit_ready, 1)
                dve.wait_ge(unit_ready, b + 2)
                nc.vector.tensor_tensor(scaled[:, u], unit[:, u], rows[:, bass.ds(b, 1), :].rearrange("p a t -> p (a t)"), ALU.mult).then_inc(scaled_ready, 1)

            lagged(dve, qk_first, qk_second)


EXP_HALF = 0.6065306597126334
M_MU, M_W0, M_A0, M_KK, M_KA, M_RK, M_GNW, M_GNB, M_COLS = 0, 14, 18, 22, 26, 30, 34, 38, 42
LORA_WA, LORA_G = 12, 13


def rwkv_projection(nc, h, w_in, w2, a2, g2, params, masks, scratch, gate_out, bonus_out, carry):
    with Stage(nc, "rp") as st:
        w_raw = st.sbuf("w_raw", [P, 2, ND, P])
        w_hi = st.sbuf("w_hi", [P, 2, ND, P], F32R)
        w_lo = st.sbuf("w_lo", [P, 2, ND, P], F32R)
        gate = st.sbuf("gate", [P, 2])
        wa2 = st.sbuf("wa2", [P, RWKV_W])
        g2_sb = st.sbuf("g2", [P, RWKV_W])
        col = st.sbuf("col", [P, M_COLS])
        one_less_ka = st.sbuf("one_less_ka", [P, 4])
        head_ones = st.sbuf("head_ones", [P, P])
        eps = st.sbuf("eps", [P, 1])
        reset = st.sbuf("reset", [P, NT, P])
        sig = st.sbuf("sig", [P, 4, SEQ])
        rate = st.sbuf("rate", [P, 4, SEQ])
        kr_x, r_x, v_x = (st.sbuf(n, [P, 4 + SEQ]) for n in ("kr_x", "r_x", "v_x"))
        k = st.sbuf("k", [P, SEQ])
        kk = st.sbuf("kk", [P, SEQ])
        r = st.sbuf("r", [P, SEQ])
        sq = st.sbuf("sq", [P, SEQ])
        cs = st.sbuf("cs", [P, NT, P])
        cm = st.sbuf("cm", [P, NT, P])
        before = st.sbuf("before", [P, NT, P])
        grow = st.sbuf("grow", [P, NT, P])
        shrink = st.sbuf("shrink", [P, NT, P])
        out = st.sbuf("out", [P, NT, R_SLOTS, P])
        bonus = st.sbuf("bonus", [P, SEQ])
        ends = st.sbuf("ends", [P, NT])
        proj = st.psum("proj", [P, 2, 2, HALF])
        sums = st.psum("sums", [P, 4, HALF])

        setup, ready, setup_v, lora_g = st.sem("setup"), st.sem("ready"), st.sem("setup_v"), st.sem("lora_g")
        w_loaded = [st.sem(f"w_loaded{u}") for u in range(2)]
        w_rounded, w_split, projected, copied = st.sem("w_rounded"), st.sem("w_split"), st.sem("projected"), st.sem("copied")
        lora_in, lora_summed, lora_read = st.sem("lora_in"), st.sem("lora_summed"), st.sem("lora_read")
        gate_ready, gate_stored = st.sem("gate_ready"), st.sem("gate_stored")
        out_stored, bonus_stored = st.sem("out_stored"), st.sem("bonus_stored")
        dve_steps = Steps(st.sem("dve_steps"), "kr_diff kr kk_raw cs cm before k_factor k r_diff r rk kk "
                          "kk_out r_out k_out b_pre b_out v_diff v_out bonus ends ends_next")
        act_steps = Steps(st.sem("act_steps"), "kr_copied kk_squared r_copied shrink grow before log_norm norm v_copied carry")
        pe_steps = Steps(st.sem("pe_steps"), "norm_summed bonus_summed")
        block = st.stack.enter_context(nc.Block())
        w_cols = w_in.rearrange("(d p) f -> p d f", p=P)
        tiles = scratch.rearrange("c p w -> p c w")
        BLOCKS = 14
        kr_lora, g_lora = k, kk

        @block.sync
        def _(sp):
            sp.nop().then_inc(out_stored, 16)
            sp.nop().then_inc(bonus_stored, 16)
            sp.nop().then_inc(gate_stored, 16)
            sp.dma_start(col[:], params).then_inc(setup, 16)
            sp.dma_start(wa2[0:64], w2).then_inc(setup, 16)
            sp.dma_start(wa2[64:128], a2).then_inc(setup, 16)
            sp.dma_start(g2_sb[:], g2).then_inc(setup, 16)
            sp.dma_start(head_ones[:], masks[:, 4]).then_inc(setup, 16)

            def load(kk_, s, start):
                if not (isinstance(kk_, int) and kk_ < 2):
                    sp.wait_ge(w_split, kk_ - 1)
                sp.dma_start(w_raw[:, s], w_cols[:, :, bass.ds(start, P)]).then_inc(w_loaded[s], 16)

            load(0, 0, RWKV_COLS + LORA_WA * P)
            load(1, 1, RWKV_COLS + LORA_G * P)
            load(2, 0, RWKV_COLS + RWKV_W)
            load(3, 1, RWKV_COLS)
            for b in range(4):
                sp.wait_ge(gate_ready, b + 1)
                sp.dma_start(gate_out[b], sq[:]).then_inc(gate_stored, 16)

            def store(b):
                dve_steps.wait(sp, "v_out", b)
                sp.dma_start(tiles[:, :, bass.ds((S_RWKV + R_SLOTS * b) * P, R_SLOTS * P)],
                             out[:].rearrange("p c s t -> p c (s t)")).then_inc(out_stored, 16)
                dve_steps.wait(sp, "bonus", b)
                sp.dma_start(bonus_out[bass.ds(b, 1)].rearrange("a p t -> p (a t)"), bonus[:]).then_inc(bonus_stored, 16)

            for b in range(4):
                n = 3 * b + 4
                load(n, n % 2, RWKV_COLS + 2 * RWKV_W + b * P)
                if b < 3:
                    load(n + 1, (n + 1) % 2, RWKV_COLS + RWKV_W + (b + 1) * P)
                    load(n + 2, n % 2, RWKV_COLS + (b + 1) * P)
                store(b)
            sp.wait_ge(out_stored, 16 * 5)
            sp.wait_ge(bonus_stored, 16 * 5)
            sp.wait_ge(gate_stored, 16 * 5)

        @block.gpsimd
        def _(pool):
            stream_weights(nc, pool, gate[:], w_raw, w_hi, w_lo, w_loaded, w_rounded, w_split, projected, BLOCKS)

        @block.tensor
        def _(pe):
            pe_steps.open(pe)

            def project(n, s):
                pe.wait_ge(w_split, n + 1)
                if not (isinstance(n, int) and n < 2):
                    pe.wait_ge(copied, n)
                for t in range(NH):
                    for d in range(ND):
                        last = split_matmul(nc, proj[:, s, t], (w_hi[:, s, d], w_lo[:, s, d]),
                                            tuple(part[:, d, t * HALF:(t + 1) * HALF] for part in h), d == 0, d == ND - 1)
                last.then_inc(projected, 1)

            project(0, 0)
            project(1, 1)
            pe.wait_ge(setup, 16 * 5)
            for b in range(4):
                cols = slice(b * P, (b + 1) * P)
                pe.wait_ge(lora_in, 2)
                if b:
                    pe.wait_ge(lora_read, 3 * b)
                for t in range(NH):
                    tok = slice(t * HALF, (t + 1) * HALF)
                    nc.tensor.matmul(sums[:, t], wa2[0:64, cols], kr_lora[0:64, tok], start=True, stop=True)
                    last = nc.tensor.matmul(sums[:, 2 + t], wa2[64:128, cols], kr_lora[64:128, tok], start=True, stop=True)
                last.then_inc(lora_summed, 1)
                pe.wait_ge(lora_in, 3)
                pe.wait_ge(lora_read, 3 * b + 1)
                for t in range(NH):
                    last = nc.tensor.matmul(sums[:, t], g2_sb[:, cols], g_lora[:, t * HALF:(t + 1) * HALF], start=True, stop=True)
                last.then_inc(lora_summed, 1)

            def over_heads(what, b, bank, prev):
                for t in range(NH):
                    last = nc.tensor.matmul(sums[:, bank + t], head_ones[:], sq[:, t * HALF:(t + 1) * HALF], start=True, stop=True)
                pe_steps.done(last, what)

            def heads(b, s, n):
                project(n, s)
                project(n + 1, 1 - s)
                act_steps.wait(pe, "kk_squared", b)
                act_steps.wait(pe, "log_norm", b - 1)
                over_heads("norm_summed", b, 0, None)
                project(n + 2, s)
                dve_steps.wait(pe, "rk", b)
                dve_steps.wait(pe, "bonus", b - 1)
                over_heads("bonus_summed", b, 2, None)

            with pe.Fori(0, 2) as i:
                heads(2 * i, 0, 6 * i + 2)
                heads(2 * i + 1, 1, 6 * i + 5)

        @block.scalar
        def _(act):
            act_steps.open(act)
            act.wait_ge(setup, 16 * 5)
            act.wait_ge(ready, 1)

            def copy_block(n, to, s):
                act.wait_ge(projected, n + 1)
                return nc.scalar.copy(to[:, 4:], proj[:, s].rearrange("p n t -> p (n t)"))

            copy_block(0, kr_x, 0).then_inc(copied, 1)
            copy_block(1, r_x, 1).then_inc(copied, 1)
            act.wait_ge(lora_in, 1)
            nc.scalar.activation(kr_lora[0:64], k[0:64], ACT.Tanh).then_inc(lora_in, 1)
            act.wait_ge(lora_in, 2)
            act.wait_ge(lora_g, 1)
            nc.scalar.activation(g_lora[:], kk[:], ACT.Sigmoid).then_inc(lora_in, 1)
            for b in range(4):
                act.wait_ge(lora_summed, 2 * b + 1)
                nc.scalar.activation(sig[:, b], sums[:, 0:2].rearrange("p n t -> p (n t)"), ACT.Sigmoid, bias=col[:, M_W0 + b:M_W0 + b + 1]).then_inc(lora_read, 1)
                nc.scalar.activation(rate[:, b], sums[:, 2:4].rearrange("p n t -> p (n t)"), ACT.Sigmoid, bias=col[:, M_A0 + b:M_A0 + b + 1]).then_inc(lora_read, 1)
                act.wait_ge(lora_summed, 2 * b + 2)
                act.wait_ge(gate_stored, 16 * (b + 1))
                nc.scalar.copy(sq[:], sums[:, 0:2].rearrange("p n t -> p (n t)")).then_inc(lora_read, 1)
                act.wait_ge(lora_read, 3 * b + 3)
                nc.scalar.nop().then_inc(gate_ready, 1)
            act.wait_ge(gate_stored, 16 * 5)

            def heads(b, s, n):
                dve_steps.wait(act, "kr", b - 1)
                ins = copy_block(n, kr_x, s)
                act_steps.done(ins, "kr_copied")
                act_steps.wait(act, "kr_copied", b)
                nc.scalar.nop().then_inc(copied, 1)
                dve_steps.wait(act, "kk_raw", b)
                pe_steps.wait(act, "bonus_summed", b - 1)
                act_steps.done(nc.scalar.activation(sq[:], kk[:], ACT.Square), "kk_squared")
                dve_steps.wait(act, "r", b - 1)
                ins = copy_block(n + 1, r_x, 1 - s)
                act_steps.done(ins, "r_copied")
                act_steps.wait(act, "r_copied", b)
                nc.scalar.nop().then_inc(copied, 1)
                dve_steps.wait(act, "cm", b)
                act_steps.done(nc.scalar.activation(shrink[:], cm[:], ACT.Exp, scale=-EXP_HALF), "shrink")
                act_steps.done(nc.scalar.activation(grow[:], cm[:], ACT.Exp, scale=EXP_HALF), "grow")
                dve_steps.wait(act, "before", b)
                act_steps.done(nc.scalar.activation(before[:], before[:], ACT.Exp, scale=-EXP_HALF), "before")
                pe_steps.wait(act, "norm_summed", b)
                act.wait_ge(bonus_stored, 16 * (b + 1))
                act_steps.done(nc.scalar.activation(bonus[:], sums[:, 0:2].rearrange("p n t -> p (n t)"), ACT.Ln, bias=eps[:]), "log_norm")
                act_steps.wait(act, "log_norm", b)
                act_steps.done(nc.scalar.activation(bonus[:], bonus[:], ACT.Exp, scale=-0.5), "norm")
                dve_steps.wait(act, "v_out", b - 1)
                ins = copy_block(n + 2, v_x, s)
                act_steps.done(ins, "v_copied")
                act_steps.wait(act, "v_copied", b)
                nc.scalar.nop().then_inc(copied, 1)
                dve_steps.wait(act, "ends_next", b)
                act_steps.done(nc.scalar.activation(carry[:, :, bass.ds(b, 1)].rearrange("p c a -> p (c a)"), ends[:], ACT.Exp, scale=-EXP_HALF), "carry")

            with act.Fori(0, 2) as i:
                heads(2 * i, 0, 6 * i + 2)
                heads(2 * i + 1, 1, 6 * i + 5)

        @block.vector
        def _(dve):
            dve_steps.open(dve)
            nc.vector.nop().then_inc(copied, 1)
            nc.vector.memset(eps[:], L2_EPS)
            nc.vector.memset(reset[:], 1.0).then_inc(setup_v, 1)
            dve.wait_ge(setup_v, 1)
            nc.vector.memset(reset[:, :, 0:1], 0.0).then_inc(setup_v, 1)
            dve.wait_ge(setup, 16 * 5)
            nc.vector.tensor_scalar(one_less_ka[:], col[:, M_KA:M_KA + 4], -1.0, 1.0, ALU.mult, ALU.add).then_inc(setup_v, 1)
            for x in (r_x, v_x, kr_x):
                last = nc.vector.memset(x[:, 0:4], 0.0)
            last.then_inc(ready, 1)
            dve.wait_ge(setup_v, 3)
            dve.wait_ge(ready, 1)

            def mu(blk):
                return col[:, bass.ds(M_MU + blk, 1)]

            def shift(x, blk, diff, to, name_diff, name, b):
                ins = nc.vector.tensor_tensor(diff, x[:, 3:3 + SEQ], x[:, 4:], ALU.subtract)
                dve_steps.done(ins, name_diff)
                dve_steps.wait(dve, name_diff, b)
                dve_steps.done(nc.vector.scalar_tensor_tensor(to, diff, mu(blk), x[:, 4:], ALU.mult, ALU.add), name)

            for n, (x, to, sem) in enumerate(((kr_x, k, lora_in), (r_x, kk, lora_g))):
                dve.wait_ge(copied, n + 2)
                nc.vector.tensor_tensor(to[:], x[:, 3:3 + SEQ], x[:, 4:], ALU.subtract).then_inc(setup_v, 1)
                dve.wait_ge(setup_v, 4 + n)
                nc.vector.scalar_tensor_tensor(to[:], to[:], mu(LORA_WA + n), x[:, 4:], ALU.mult, ALU.add).then_inc(sem, 1)
            dve.wait_ge(lora_read, 12)
            dve.wait_ge(gate_stored, 16 * 5)

            def heads(b):
                one = lambda base: col[:, bass.ds(base + b, 1)]
                flat = lambda x: x[:].rearrange("p c t -> p (c t)")
                at_head = lambda x: x[:, bass.ds(b, 1)].rearrange("p a t -> p (a t)")
                slot = lambda j: out[:, :, j]
                act_steps.wait(dve, "kr_copied", b)
                shift(kr_x, b + 4, k[:], k[:], "kr_diff", "kr", b)
                dve_steps.wait(dve, "kr", b)
                dve_steps.done(nc.vector.tensor_scalar(kk[:], k[:], one(M_KK), None, ALU.mult), "kk_raw")
                dve_steps.done(nc.vector.tensor_tensor_scan(flat(cs), flat(reset), at_head(sig), 0.0, ALU.mult, ALU.add), "cs")
                dve_steps.wait(dve, "cs", b)
                dve_steps.done(nc.vector.tensor_tensor(cm[:], cs[:], cs[:, :, P // 2 - 1:P // 2].broadcast_to([P, NT, P]), ALU.subtract), "cm")
                dve_steps.wait(dve, "cm", b)
                dve_steps.done(nc.vector.tensor_tensor(flat(before), flat(cm), at_head(sig), ALU.subtract), "before")
                dve_steps.done(nc.vector.tensor_scalar(r[:], at_head(rate), one(M_KA), one_less_ka[:, bass.ds(b, 1)], ALU.mult, ALU.add), "k_factor")
                dve_steps.wait(dve, "k_factor", b)
                dve_steps.done(nc.vector.tensor_tensor(k[:], k[:], r[:], ALU.mult), "k")
                act_steps.wait(dve, "r_copied", b)
                dve_steps.wait(dve, "k", b)
                shift(r_x, b, r[:], r[:], "r_diff", "r", b)
                dve_steps.wait(dve, "r", b)
                pe_steps.wait(dve, "norm_summed", b)
                dve_steps.done(nc.vector.scalar_tensor_tensor(sq[:], r[:], one(M_RK), k[:], ALU.mult, ALU.mult), "rk")
                act_steps.wait(dve, "norm", b)
                dve_steps.done(nc.vector.tensor_tensor(kk[:], kk[:], bonus[:], ALU.mult), "kk")
                dve_steps.wait(dve, "kk", b)
                dve.wait_ge(out_stored, 16 * (b + 1))
                by_tile = lambda x: x[:].rearrange("p (c t) -> p c t", t=P)
                dve_steps.done(nc.vector.tensor_tensor(slot(R_KK), by_tile(kk), before[:], ALU.mult), "kk_out")
                dve_steps.done(nc.vector.tensor_tensor(slot(R_R), by_tile(r), shrink[:], ALU.mult), "r_out")
                dve_steps.done(nc.vector.tensor_tensor(slot(R_K), by_tile(k), grow[:], ALU.mult), "k_out")
                dve_steps.done(nc.vector.scalar_tensor_tensor(kk[:], kk[:], -1.0, at_head(rate), ALU.mult, ALU.mult), "b_pre")
                dve_steps.wait(dve, "b_pre", b)
                dve_steps.done(nc.vector.tensor_tensor(slot(R_B), by_tile(kk), grow[:], ALU.mult), "b_out")
                act_steps.wait(dve, "v_copied", b)
                dve_steps.done(nc.vector.tensor_tensor(cm[:], v_x[:, 3:3 + SEQ].rearrange("p (c t) -> p c t", t=P),
                                                       v_x[:, 4:].rearrange("p (c t) -> p c t", t=P), ALU.subtract), "v_diff")
                dve_steps.wait(dve, "v_diff", b)
                dve_steps.done(nc.vector.scalar_tensor_tensor(slot(R_V), cm[:], mu(b + 8), v_x[:, 4:].rearrange("p (c t) -> p c t", t=P),
                                                              ALU.mult, ALU.add), "v_out")
                pe_steps.wait(dve, "bonus_summed", b)
                dve_steps.wait(dve, "v_out", b)
                dve.wait_ge(bonus_stored, 16 * (b + 1))
                dve_steps.done(nc.vector.tensor_tensor(by_tile(bonus), slot(R_V), sums[:, 2:4].rearrange("p n (c t) -> p (n c) t", t=P), ALU.mult), "bonus")
                dve_steps.done(nc.vector.tensor_tensor(ends[:], cs[:, :, P - 1], cs[:, :, P // 2 - 1], ALU.subtract), "ends")
                dve_steps.wait(dve, "ends", b)
                dve_steps.done(nc.vector.tensor_tensor(ends[:, 0:NT - 1], ends[:, 0:NT - 1], cs[:, 1:NT, P // 2 - 1], ALU.add), "ends_next")

            with dve.Fori(0, 4) as b:
                heads(b)


LEVELS = (2, 4, 8, 16, 32, 64)
HEADS = 4
MASKS = 5 + 7


def recurrences(nc, masks, scratch, carry, merged):
    with Stage(nc, "rc") as st:
        CH = "GAB"
        mask = st.sbuf("mask", [P, MASKS, P])
        tile = st.sbuf("tile", [P, 2, TILE_W])
        n_t = {ch: None for ch in CH}
        att = {ch: st.sbuf(f"att_{ch}", [P, 2 if ch == "G" else 4, HEADS, P]) for ch in CH}
        level = {ch: st.sbuf(f"level_{ch}", [P, 2, HEADS, P]) for ch in CH}
        T = {ch: st.sbuf(f"T_{ch}", [P, HEADS, P]) for ch in CH}
        TT = {ch: st.sbuf(f"TT_{ch}", [P, HEADS, P]) for ch in CH}
        X = {ch: st.sbuf(f"X_{ch}", [P, HEADS, P]) for ch in CH}
        tok = {ch: st.sbuf(f"tok_{ch}", [P, 8 if ch == "G" else 6, P]) for ch in CH}
        new = {ch: st.sbuf(f"new_{ch}", [P, HEADS if ch == "G" else 2, P]) for ch in CH}
        delta = {ch: st.sbuf(f"delta_{ch}", [P, HEADS if ch == "G" else 2, P]) for ch in CH}
        state = {ch: st.sbuf(f"state_{ch}", [P, HEADS if ch == "G" else 2, P]) for ch in CH}
        headed = {ch: st.sbuf(f"headed_{ch}", [P, 2, 2, 2, P]) for ch in "AB"}
        gate = st.sbuf("gate", [P, 2])
        ps = st.psum("ps", [P, 8, HALF])
        bank = {"G": 6, "A": 0, "B": 2}
        first_bank = {"G": 4, "A": 0, "B": 2}
        token_bank = {"A": 0, "B": 4}
        NT_, OUT_NEW, IN_V, OUT_V = 0, 1, 2, 3

        levels = [f"{ch}_{{}}{b}" for b in LEVELS for ch in CH]
        setup, ready = st.sem("setup"), st.sem("ready")
        heads_apart = st.sem("heads_apart")
        loaded = [st.sem(f"loaded{u}") for u in range(2)]

        def level_names(kinds):
            return " ".join(f"{ch}_{k}{b}" for b in LEVELS for ch in CH for k in kinds if not (b == 64 and k == "t"))

        grown = [("products", "G", 0), ("tokens", "G", 0), ("products", "A", 0), ("early", "B", 0), ("x", "G", 2),
                 ("products", "B", 0), ("tokens", "A", 0), ("xt", "G", 2), ("x", "A", 2), ("tokens", "B", 0), ("x", "B", 2), ("xt", "A", 2)]
        for before, b in zip(LEVELS, LEVELS[1:]):
            grown += [("x", "G", b), ("xt", "B", before), ("x", "A", b), ("xt", "G", b), ("x", "B", b), ("xt", "A", b)]
        grown += [("xt", "B", LEVELS[-1])]
        pe_steps = Steps(st.sem("pe_steps"), " ".join((f"{ch}_tx{b} " if (kind, b) == ("xt", 32) else "") + f"{ch}_{kind}{b or ''}"
                                                      for kind, ch, b in grown)
                         + " G_ks A_x B_x G_v A_p B_p G_s A_d B_d G_o A_y B_y")
        act_steps = Steps(st.sem("act_steps"), level_names(("xc",)).replace("A_xc2", "A_tokens A_tokens2 A_xc2").replace("B_xc2", "B_tokens B_tokens2 B_xc2")
                          + " A_x B_x G_v G_o A_y A_y2 B_y B_y2")
        dve_steps = Steps(st.sem("dve_steps"), "G_n G_att G_kd G_vb G_t1 A_n A_att2 A_att3 A_att A_t1 B_n B_att2 B_att3 B_att B_t1 "
                          + level_names(("tt", "t"))
                          + " G_xb G_x A_p1 A_p B_p1 B_p G_sg A_d B_d G_s A_m A_s0 A_s B_m B_s0 B_s")
        pool_steps = Steps(st.sem("pool_steps"), "G_m1 G_tt G_m2 A_m1 A_tt A_m2 B_m1 B_tt B_m2 "
                           + level_names(("m",)).replace("G_m2 A_m2 B_m2 ", ""))
        block = st.stack.enter_context(nc.Block())

        def slot(u, n, count=1):
            return tile[:, u, n * P:(n + count) * P]

        def slots(u, n, count, step=1):
            v = tile[:, u, 0:SLOTS * P].rearrange("p (s t) -> p s t", t=P)
            return v[:, n:n + step * (count - 1) + 1:step]

        def rwkv(ch, pair, j):
            return S_RWKV + R_SLOTS * (2 * "AB".index(ch) + pair) + j

        def columns(u, n):
            return tile[:, u, C_GDN + 4 * n:C_GDN + 4 * n + 4].rearrange("p (n a) -> p n a", a=1).broadcast_to([P, HEADS, P])

        def over_heads(n):
            return mask[:, n:n + 1].broadcast_to([P, HEADS, P])

        def banks(n, count=1):
            return ps[:, n:n + count].rearrange("p b w -> p (b w)").rearrange("p (n t) -> p n t", t=P)

        def chosen(n):
            return mask[:, n:n + 1].bitcast(U32).broadcast_to([P, HEADS, P])

        @block.sync
        def _(sp):
            sp.dma_start(mask[:], masks).then_inc(setup, 16)
            for u in range(2):
                sp.dma_start(tile[:, u], scratch[u]).then_inc(loaded[u], 16)
            with sp.Fori(0, NT // 2 - 1) as i:
                for u in range(2):
                    pe_steps.wait(sp, "B_y", 2 * i + u)
                    dve_steps.wait(sp, "B_s", 2 * i + u)
                    sp.dma_start(tile[:, u], scratch[bass.ds(2 * i + u + 2, 1)].rearrange("a p w -> p (a w)")).then_inc(loaded[u], 16)

        @block.tensor
        def _(pe):
            pe_steps.open(pe)
            mm = nc.tensor.matmul
            pe.wait_ge(setup, 16)
            pe.wait_ge(ready, 1)

            def turn(out, sources):
                for n, src in enumerate(sources):
                    last = nc.tensor.transpose(out[:, n], src, mask[:, 0])
                return last

            def products(ch, u, name, heads):
                for n in heads:
                    if ch == "G":
                        last = mm(ps[:, first_bank[ch] + n // 2, n % 2 * 2 * P:(n % 2 + 1) * 2 * P], slot(u, S_K + 2 * n),
                                  slots(u, 2 * n, 2, S_K + 1), start=True, stop=True)
                    else:
                        for j, kind in enumerate((R_B, R_K)):
                            last = mm(ps[:, first_bank[ch] + n, 2 * j * P:2 * (j + 1) * P], slot(u, rwkv(ch, n // 2, kind)),
                                      headed[ch][:, n % 2, n // 2].rearrange("p k t -> p (k t)"), start=True, stop=True)
                pe_steps.done(last, name)

            def tile_of(c, u, i):
                pe.wait_ge(loaded[u], 16 * (i + 1))
                for kind, ch, b in grown:
                    if kind == "products" and ch == "G":
                        products("G", u, "G_products", range(HEADS))
                    elif kind == "products" and ch == "A":
                        pe.wait_ge(heads_apart, 4 * c + 2)
                        act_steps.wait(pe, "B_y2", c - 1)
                        dve_steps.wait(pe, "B_d", c - 1)
                        products("A", u, "A_products", range(HEADS))
                    elif kind == "early":
                        pe.wait_ge(heads_apart, 4 * c + 4)
                        dve_steps.wait(pe, "G_att", c)
                        products("B", u, "B_early", (2, 3))
                    elif kind == "products":
                        dve_steps.wait(pe, "A_att", c)
                        products("B", u, "B_products", (0, 1))
                    elif kind == "tokens" and ch == "G":
                        act_steps.wait(pe, "G_o", c - 1)
                        dve_steps.wait(pe, "G_s", c - 1)
                        turn(banks(bank["G"]), [slot(u, S_K + 2 * n) for n in range(HEADS)])
                        pe_steps.done(turn(banks(bank["G"] + 1), [slot(u, S_V + n) for n in range(HEADS)]), "G_tokens")
                    elif kind == "tokens":
                        dve_steps.wait(pe, f"{ch}_att", c)
                        srcs = [slot(u, rwkv(ch, pair, j)) for j in (R_V, R_K, R_B) for pair in range(2)]
                        turn(banks(token_bank[ch]), srcs[0:4])
                        pe_steps.done(turn(banks(token_bank[ch] + 1), srcs[4:6]), f"{ch}_tokens")
                    elif kind == "x":
                        pool_steps.wait(pe, f"{ch}_m{b}", c)
                        if b == LEVELS[0]:
                            if ch == "A":
                                act_steps.wait(pe, "A_tokens2", c)
                            else:
                                dve_steps.wait(pe, f"{ch}_{'vb' if ch == 'G' else 'att'}", c)
                        dve_steps.wait(pe, f"{ch}_t{b // 2}", c)
                        for n in range(HEADS):
                            last = mm(banks(bank[ch])[:, n], level[ch][:, LEVELS.index(b) % 2, n], T[ch][:, n], start=True, stop=True)
                    else:
                        act_steps.wait(pe, f"{ch}_xc{b}", c)
                        if b == 32:
                            for n in range(HEADS):
                                last = mm(banks(bank[ch])[:, n], TT[ch][:, n], X[ch][:, n], start=True, stop=True)
                            pe_steps.done(last, f"{ch}_tx{b}")
                        for n in range(HEADS):
                            last = mm(banks(bank[ch] + 1)[:, n], X[ch][:, n], TT[ch][:, n], start=True, stop=True)
                    if kind in ("x", "xt"):
                        pe_steps.done(last, f"{ch}_{kind}{b}")

                dve_steps.wait(pe, "G_s", c - 1)
                for n in range(HEADS):
                    last = mm(banks(bank["G"])[:, n], slot(u, S_K + 2 * n), state["G"][:, n], start=True, stop=True)
                pe_steps.done(last, "G_ks")
                for ch in "AB":
                    dve_steps.wait(pe, f"{ch}_s", c - 1)
                    for n in range(HEADS):
                        o = banks(bank[ch])[:, n]
                        mm(o, slot(u, rwkv(ch, n // 2, R_KK)), state[ch][:, n // 2], start=True, stop=False)
                        last = mm(o, att[ch][:, IN_V, n], tok[ch][:, n // 2], start=False, stop=True)
                    pe_steps.done(last, f"{ch}_x")
                for ch, name in (("G", "G_v"), ("A", "A_p"), ("B", "B_p")):
                    dve_steps.wait(pe, f"{ch}_tt64", c)
                    if ch == "G":
                        dve_steps.wait(pe, "G_x", c)
                    else:
                        act_steps.wait(pe, f"{ch}_x", c)
                    for n in range(HEADS):
                        last = mm(banks(bank[ch] + 1)[:, n], TT[ch][:, n], X[ch][:, n], start=True, stop=True)
                    pe_steps.done(last, name)
                act_steps.wait(pe, "G_v", c)
                for n in range(HEADS):
                    last = mm(banks(bank["G"] + 1)[:, n], tok["G"][:, n], new["G"][:, n], start=True, stop=True)
                pe_steps.done(last, "G_s")
                for ch in "AB":
                    dve_steps.wait(pe, f"{ch}_p", c)
                    for pair in range(2):
                        o = banks(bank[ch])[:, pair]
                        mm(o, tok[ch][:, 2 + pair], tok[ch][:, pair], start=True, stop=False)
                        last = mm(o, tok[ch][:, 4 + pair], new[ch][:, pair], start=False, stop=True)
                    pe_steps.done(last, f"{ch}_d")
                for n in range(HEADS):
                    mm(banks(bank["G"])[:, n], state["G"][:, n], slot(u, S_Q + 2 * n + 1), start=True, stop=False)
                    last = mm(banks(bank["G"])[:, n], new["G"][:, n], att["G"][:, OUT_NEW, n], start=False, stop=True)
                pe_steps.done(last, "G_o")
                for ch in "AB":
                    for n in range(HEADS):
                        o = banks(bank[ch] + 1)[:, n]
                        mm(o, state[ch][:, n // 2], slot(u, rwkv(ch, n // 2, R_R)), start=True, stop=False)
                        mm(o, tok[ch][:, n // 2], att[ch][:, OUT_V, n], start=False, stop=False)
                        last = mm(o, new[ch][:, n // 2], att[ch][:, OUT_NEW, n], start=False, stop=True)
                    pe_steps.done(last, f"{ch}_y")

            with pe.Fori(0, NT // 2) as i:
                for u in range(2):
                    tile_of(2 * i + u, u, i)

        @block.scalar
        def _(act):
            act_steps.open(act)

            def copy(name, out, src):
                act_steps.done(nc.scalar.copy(out, src), name)

            def part_heads(u, loads):
                act.wait_ge(loaded[u], 16 * loads)
                for ch in "AB":
                    first = rwkv(ch, 0, R_KK)
                    of_pairs = tile[:, u, first * P:(first + 2 * R_SLOTS) * P].rearrange("p (a s t) -> p a s t", a=2, t=P)[:, :, 0:2]
                    for e in range(2):
                        rows = slice(64 * e, 64 * e + 64)
                        nc.scalar.copy(headed[ch][rows, e], of_pairs[rows]).then_inc(heads_apart, 1)

            def tile_of(c, u, i, last):
                def tokens(ch):
                    pe_steps.wait(act, f"{ch}_tokens", c)
                    copy(f"{ch}_tokens", tok[ch][:, 0:4], banks(token_bank[ch]))
                    copy(f"{ch}_tokens2", tok[ch][:, 4:6], banks(token_bank[ch] + 1)[:, 0:2])

                for b in LEVELS:
                    for ch in CH:
                        if b == LEVELS[0] and ch != "G":
                            tokens(ch)
                        pe_steps.wait(act, f"{ch}_x{b}", c)
                        copy(f"{ch}_xc{b}", X[ch][:], banks(bank[ch]))
                for ch in "AB":
                    pe_steps.wait(act, f"{ch}_x", c)
                    copy(f"{ch}_x", X[ch][:], banks(bank[ch]))
                pe_steps.wait(act, "G_v", c)
                copy("G_v", new["G"][:], banks(bank["G"] + 1))
                if not last:
                    part_heads(1 - u, i + 1 + u)
                pe_steps.wait(act, "G_o", c)
                copy("G_o", merged[:, 0:4, bass.ds(c * P, P)], banks(bank["G"]))
                for ch in "AB":
                    pe_steps.wait(act, f"{ch}_y", c)
                    first = 4 + 2 * "AB".index(ch)
                    for e, name in enumerate((f"{ch}_y", f"{ch}_y2")):
                        rows = slice(64 * e, 64 * e + 64)
                        copy(name, merged[rows, first:first + 2, bass.ds(c * P, P)],
                             banks(bank[ch] + 1)[rows, e:e + 3:2])

            act.wait_ge(ready, 1)
            part_heads(0, 1)
            with act.Fori(0, NT // 2 - 1) as i:
                for u in range(2):
                    tile_of(2 * i + u, u, i, False)
            for u in range(2):
                tile_of(NT - 2 + u, u, NT // 2 - 1, u == 1)

        @block.gpsimd
        def _(pool):
            pool_steps.open(pool)
            pool.wait_ge(setup, 16)
            tt = nc.gpsimd.tensor_tensor

            def coupled(ch, k, c):
                if k >= 2:
                    pe_steps.wait(pool, f"{ch}_x{LEVELS[k - 2]}", c)
                pool_steps.done(tt(level[ch][:, k % 2], att[ch][:, NT_], over_heads(6 + k), ALU.mult), f"{ch}_m{LEVELS[k]}")

            def tile_of(c):
                for ch in CH:
                    dve_steps.wait(pool, f"{ch}_n", c)
                    pe_steps.wait(pool, f"{ch}_p" if ch != "G" else "G_v", c - 1)
                    pool_steps.done(tt(X[ch][:], att[ch][:, NT_], over_heads(5), ALU.mult), f"{ch}_m1")
                    pool_steps.wait(pool, f"{ch}_m1", c)
                    pool_steps.done(tt(TT[ch][:], X[ch][:], over_heads(0), ALU.add), f"{ch}_tt")
                    coupled(ch, 0, c)
                for k in range(1, len(LEVELS)):
                    for ch in CH:
                        coupled(ch, k, c)

            with pool.Fori(0, NT // 2) as i:
                for u in range(2):
                    tile_of(2 * i + u)

        @block.vector
        def _(dve):
            dve_steps.open(dve)
            for ch in CH:
                nc.vector.memset(state[ch][:], 0.0)
                nc.vector.memset(att[ch][:], 0.0)
                if ch != "G":
                    nc.vector.memset(headed[ch][:], 0.0)
            nc.vector.memset(gate[:], 0.0).then_inc(ready, 1)
            dve.wait_ge(setup, 16)
            dve.wait_ge(ready, 1)
            tt = nc.vector.tensor_tensor

            def masked(ch, c):
                pe_steps.wait(dve, f"{ch}_products", c)
                pe_steps.wait(dve, f"{ch}_y", c - 1)
                pool_steps.wait(dve, f"{ch}_m64", c - 1)
                nc.vector.tensor_copy(gate[:, 0:1], gate[:, 1:2])
                for name, j, kind, which in ((f"{ch}_n", 0, NT_, 3), (f"{ch}_att2", 1, OUT_NEW, 2),
                                             (f"{ch}_att3", 2, IN_V, 3), (f"{ch}_att", 3, OUT_V, 2)):
                    dve_steps.done(nc.vector.copy_predicated(att[ch][:, kind], chosen(which), ps[:, first_bank[ch]:first_bank[ch] + 4, j * P:(j + 1) * P]), name)

            def tile_of(c, u, i):
                both = ps[:, first_bank["G"]:first_bank["G"] + 2].rearrange("p b w -> p (b w)").rearrange("p (n k t) -> p n k t", k=2, t=P)
                dve.wait_ge(loaded[u], 16 * (i + 1))
                pe_steps.wait(dve, "G_products", c)
                pool_steps.wait(dve, "G_m64", c - 1)
                dve_steps.done(tt(att["G"][:, NT_], both[:, :, 1], slots(u, S_STRICT, 4), ALU.mult), "G_n")
                dve_steps.done(tt(att["G"][:, OUT_NEW], both[:, :, 0], slots(u, S_INCL, 4), ALU.mult), "G_att")
                pe_steps.wait(dve, "G_tokens", c)
                dve_steps.done(tt(tok["G"][:, 0:4], banks(bank["G"]), columns(u, 2), ALU.mult), "G_kd")
                dve_steps.done(tt(tok["G"][:, 4:8], banks(bank["G"] + 1), columns(u, 0), ALU.mult), "G_vb")

                def transposed(ch, name):
                    dve_steps.done(nc.vector.transpose(T[ch].rearrange("p n t -> p (n t)"), TT[ch].rearrange("p n t -> p (n t)")), name)

                for ch in CH:
                    if ch != "G":
                        masked(ch, c)
                    pool_steps.wait(dve, f"{ch}_tt", c)
                    transposed(ch, f"{ch}_t1")
                for b in LEVELS:
                    for ch in CH:
                        pe_steps.wait(dve, f"{ch}_xt{b}", c)
                        dve_steps.done(tt(TT[ch][:], TT[ch][:], banks(bank[ch] + 1), ALU.add), f"{ch}_tt{b}")
                        if b < 32:
                            dve_steps.wait(dve, f"{ch}_tt{b}", c)
                            transposed(ch, f"{ch}_t{b}")
                        elif b == 32:
                            dve_steps.done(tt(T[ch][:], T[ch][:], banks(bank[ch]), ALU.add), f"{ch}_t{b}")
                pe_steps.wait(dve, "G_ks", c)
                dve_steps.done(tt(delta["G"][:], banks(bank["G"]), columns(u, 1), ALU.mult), "G_xb")
                dve_steps.wait(dve, "G_xb", c)
                dve_steps.done(tt(X["G"][:], delta["G"][:], tok["G"][:, 4:8], ALU.add), "G_x")
                for ch in "AB":
                    pe_steps.wait(dve, f"{ch}_p", c)
                    for e, name in enumerate((f"{ch}_p1", f"{ch}_p")):
                        half = slice(64 * e, 64 * e + 64)
                        dve_steps.done(nc.vector.tensor_copy(new[ch][:, :, half], banks(bank[ch] + 1)[:, e:e + 3:2, half]), name)
                pe_steps.wait(dve, "G_s", c)
                dve_steps.done(tt(delta["G"][:], state["G"][:], columns(u, 3), ALU.mult), "G_sg")
                for ch in "AB":
                    pe_steps.wait(dve, f"{ch}_d", c)
                    dve_steps.done(tt(delta[ch][:], banks(bank[ch])[:, 0:2], mask[:, 4:5].broadcast_to([P, 2, P]), ALU.mult), f"{ch}_d")
                dve_steps.wait(dve, "G_sg", c)
                pe_steps.wait(dve, "G_o", c)
                dve_steps.done(tt(state["G"][:], delta["G"][:], banks(bank["G"] + 1), ALU.add), "G_s")
                for ch in "AB":
                    dve_steps.wait(dve, f"{ch}_d", c)
                    pe_steps.wait(dve, f"{ch}_y", c)
                    dve_steps.done(tt(delta[ch][:], delta[ch][:], state[ch][:], ALU.add), f"{ch}_m")
                    dve_steps.wait(dve, f"{ch}_m", c)
                    for pair, name in enumerate((f"{ch}_s0", f"{ch}_s")):
                        n = 2 * "AB".index(ch) + pair
                        dve_steps.done(nc.vector.tensor_scalar(state[ch][:, pair], delta[ch][:, pair],
                                                               carry[:, bass.ds(c, 1), n], None, ALU.mult), name)

            with dve.Fori(0, NT // 2) as i:
                for u in range(2):
                    tile_of(2 * i + u, u, i)


GN_EPS = 64e-5
HEAD_N = 64


def mixer_output(nc, merged, z_gate, rwkv_gate, rwkv_bonus, norm_w, gn_w, gn_b, masks, w_out):
    with Stage(nc, "mo") as st:
        w_raw = st.sbuf("w_raw", [P, 2, D])
        w_hi = st.sbuf("w_hi", [P, 8, D], F32R)
        w_lo = st.sbuf("w_lo", [P, 8, D], F32R)
        out = merged
        m_hi = st.sbuf("m_hi", [P, 8, SEQ], F32R)
        m_lo = st.sbuf("m_lo", [P, 8, SEQ], F32R)
        z, gate, bonus = st.sbuf("z", [P, SEQ]), st.sbuf("gate", [P, SEQ]), st.sbuf("bonus", [P, SEQ])
        g_root, r_root = st.sbuf("g_root", [P, SEQ]), st.sbuf("r_root", [P, SEQ])
        g_value, r_value = st.sbuf("g_value", [P, SEQ]), st.sbuf("r_value", [P, SEQ])
        mask = st.sbuf("mask", [P, 2, P])
        cols = st.sbuf("cols", [P, 12])
        eps = st.sbuf("eps", [P, 2])
        pass_gate = st.sbuf("pass_gate", [P, 2])
        ps = st.psum("ps", [P, 8, HALF])
        setup, ready = st.sem("setup"), st.sem("ready")
        w_loaded = [st.sem(f"w_loaded{u}") for u in range(2)]
        w_rounded, w_split = st.sem("w_rounded"), st.sem("w_split")
        z_loaded, gates_loaded = st.sem("z_loaded"), st.sem("gates_loaded")
        summed, copied_act, copied_dve = st.sem("summed"), st.sem("copied_act"), st.sem("copied_dve")
        pe_steps = Steps(st.sem("pe_steps"), "R_mean G_sum R_sum")
        act_steps = Steps(st.sem("act_steps"), "R_sq G_sq G_ln G_root R_ln R_root")
        dve_steps = Steps(st.sem("dve_steps"), "R_centred G_scaled G_value G_hi R_scaled R_offset R_value R_hi")
        pool_steps = Steps(st.sem("pool_steps"), "G_lo R_lo")
        block = st.stack.enter_context(nc.Block())
        BLOCKS = 4
        MEAN, G_SUM, R_SUM = 0, 2, 4

        def bank(n):
            return ps[:, n:n + 2].rearrange("p n t -> p (n t)")

        def at(x, n):
            return x[:, bass.ds(n, 1)].rearrange("p a t -> p (a t)")

        @block.sync
        def _(sp):
            sp.dma_start(mask[:, 0], masks[:, 1]).then_inc(setup, 16)
            sp.dma_start(mask[:, 1], masks[:, 4]).then_inc(setup, 16)
            for j, v in enumerate((norm_w, gn_w, gn_b)):
                sp.dma_start(cols[:, 4 * j:4 * j + 4], v).then_inc(setup, 16)
            with sp.Fori(0, BLOCKS) as n:
                dve_steps.wait(sp, "G_value", n - 1)
                sp.dma_start(z[:], z_gate[bass.ds(n, 1)].rearrange("a p t -> p (a t)")).then_inc(z_loaded, 16)
                dve_steps.wait(sp, "R_value", n - 1)
                sp.dma_start(bonus[:], rwkv_bonus[bass.ds(n, 1)].rearrange("a p t -> p (a t)")).then_inc(gates_loaded, 16)
                sp.dma_start(gate[:], rwkv_gate[bass.ds(n, 1)].rearrange("a p t -> p (a t)")).then_inc(gates_loaded, 16)

        @block.gpsimd
        def _(pool):
            pool_steps.open(pool)
            nc.gpsimd.memset(pass_gate[:], 0.0).then_inc(w_rounded, 1)
            pool.wait_ge(w_rounded, 1)
            for u in range(2):
                pool.dma_start(w_raw[:, u], w_out[u * P:(u + 1) * P, :]).then_inc(w_loaded[u], 16)

            def split(k, u, i):
                pool.wait_ge(w_loaded[u], 16 * (i + 1))
                nc.gpsimd.tensor_tensor(pass_gate[:, 0:1], pass_gate[:, 1:2], pass_gate[:, 1:2], ALU.add)
                nc.gpsimd.tensor_copy(at(w_hi, k), w_raw[:, u]).then_inc(w_rounded, 1)
                pool.wait_ge(w_rounded, k + 2)
                nc.gpsimd.tensor_tensor(at(w_lo, k), w_raw[:, u], at(w_hi, k).bitcast(F32), ALU.subtract).then_inc(w_split, 1)

            def lower(n, i):
                dve_steps.wait(pool, "G_hi", n)
                pool_steps.done(nc.gpsimd.tensor_tensor(at(m_lo, n), g_value[:], at(m_hi, n).bitcast(F32), ALU.subtract), "G_lo")
                dve_steps.wait(pool, "R_hi", n)
                pool_steps.done(nc.gpsimd.tensor_tensor(at(m_lo, n + 4), r_value[:], at(m_hi, n + 4).bitcast(F32), ALU.subtract), "R_lo")

            with pool.Fori(0, BLOCKS - 1) as i:
                for u in range(2):
                    split(2 * i + u, u, i)
                for u in range(2):
                    pool.wait_ge(w_split, 2 * i + u + 1)
                    pool.dma_start(w_raw[:, u], w_out[bass.ds((2 * i + u + 2) * P, P), :]).then_inc(w_loaded[u], 16)
                lower(i, i)
            for u in range(2):
                split(NT - 2 + u, u, BLOCKS - 1)
            lower(BLOCKS - 1, BLOCKS - 1)

        @block.scalar
        def _(act):
            act_steps.open(act)
            act.wait_ge(ready, 1)

            def inverse_root(out, n_bank, n_eps, scale, ln, root, n):
                act_steps.done(nc.scalar.activation(out, bank(n_bank), ACT.Ln, bias=eps[:, n_eps:n_eps + 1], scale=scale), ln)
                act_steps.wait(act, ln, n)
                act_steps.done(nc.scalar.activation(out, out, ACT.Exp, scale=-0.5), root)

            with act.Fori(0, BLOCKS) as n:
                dve_steps.wait(act, "R_centred", n)
                act_steps.done(nc.scalar.activation(r_root[:], r_value[:], ACT.Square), "R_sq")
                act_steps.done(nc.scalar.activation(g_root[:], at(merged, n), ACT.Square), "G_sq")
                pe_steps.wait(act, "G_sum", n)
                inverse_root(g_root[:], G_SUM, 0, 1.0 / P, "G_ln", "G_root", n)
                pe_steps.wait(act, "R_sum", n)
                inverse_root(r_root[:], R_SUM, 1, 1.0 / HEAD_N, "R_ln", "R_root", n)
            for t in range(NT):
                act.wait_ge(summed, 2 * t + 1)
                nc.scalar.copy(out[:, t, 0:HALF], ps[:, 2 * t % 8]).then_inc(copied_act, 1)

        @block.vector
        def _(dve):
            dve_steps.open(dve)
            nc.vector.memset(eps[:, 0:1], NORM_EPS)
            nc.vector.memset(eps[:, 1:2], GN_EPS).then_inc(ready, 1)
            dve.wait_ge(setup, 16 * 5)
            stt = nc.vector.scalar_tensor_tensor

            with dve.Fori(0, BLOCKS) as n:
                pe_steps.wait(dve, "R_mean", n)
                pool_steps.wait(dve, "R_lo", n - 1)
                dve_steps.done(stt(r_value[:], bank(MEAN), -1.0 / HEAD_N, at(merged, n + 4), ALU.mult, ALU.add), "R_centred")
                act_steps.wait(dve, "G_root", n)
                pool_steps.wait(dve, "G_lo", n - 1)
                dve_steps.done(stt(g_value[:], at(merged, n), cols[:, bass.ds(n, 1)], g_root[:], ALU.mult, ALU.mult), "G_scaled")
                dve_steps.wait(dve, "G_scaled", n)
                dve.wait_ge(z_loaded, 16 * (n + 1))
                dve_steps.done(nc.vector.tensor_tensor(g_value[:], g_value[:], z[:], ALU.mult), "G_value")
                dve_steps.wait(dve, "G_value", n)
                dve_steps.done(nc.vector.tensor_scalar(at(m_hi, n), g_value[:], 1.0, None, ALU.mult), "G_hi")
                act_steps.wait(dve, "R_root", n)
                dve_steps.done(stt(r_value[:], r_value[:], cols[:, bass.ds(n + 4, 1)], r_root[:], ALU.mult, ALU.mult), "R_scaled")
                dve_steps.wait(dve, "R_scaled", n)
                dve.wait_ge(gates_loaded, 32 * (n + 1))
                dve_steps.done(stt(r_value[:], r_value[:], cols[:, bass.ds(n + 8, 1)], bonus[:], ALU.add, ALU.add), "R_offset")
                dve_steps.wait(dve, "R_offset", n)
                dve_steps.done(nc.vector.tensor_tensor(r_value[:], r_value[:], gate[:], ALU.mult), "R_value")
                dve_steps.wait(dve, "R_value", n)
                dve_steps.done(nc.vector.tensor_scalar(at(m_hi, n + 4), r_value[:], 1.0, None, ALU.mult), "R_hi")
            for t in range(NT):
                dve.wait_ge(summed, 2 * t + 2)
                nc.vector.tensor_copy(out[:, t, HALF:D], ps[:, (2 * t + 1) % 8]).then_inc(copied_dve, 1)

        @block.tensor
        def _(pe):
            pe_steps.open(pe)
            pe.wait_ge(setup, 16 * 5)

            def over_channels(which, first_bank, src, name):
                for t in range(NH):
                    last = nc.tensor.matmul(ps[:, first_bank + t], mask[:, which], src[:, t * HALF:(t + 1) * HALF], start=True, stop=True)
                pe_steps.done(last, name)

            with pe.Fori(0, BLOCKS) as n:
                dve_steps.wait(pe, "R_centred", n - 1)
                over_channels(1, MEAN, at(merged, n + 4), "R_mean")
                act_steps.wait(pe, "G_sq", n)
                over_channels(0, G_SUM, g_root, "G_sum")
                over_channels(1, R_SUM, r_root, "R_sum")
            pool_steps.wait(pe, "R_lo", BLOCKS - 1)
            pe.wait_ge(w_split, 8)
            for t in range(NT):
                tok = slice(t * P, (t + 1) * P)
                for half in range(2):
                    if t >= 4:
                        pe.wait_ge(copied_act if half == 0 else copied_dve, t - 3)
                    cols_ = slice(half * HALF, (half + 1) * HALF)
                    for c in range(8):
                        last = split_matmul(nc, ps[:, (2 * t + half) % 8], (m_hi[:, c, tok], m_lo[:, c, tok]),
                                            (w_hi[:, c, cols_], w_lo[:, c, cols_]), c == 0, c == 7)
                    last.then_inc(summed, 1)


def layer_embedding(nc, h, p, w_gate, w_proj, masks, out):
    with Stage(nc, "le") as st:
        NE = D_PLE // P
        ROWS = NE + ND
        w_raw = st.sbuf("w_raw", [P, 2, D])
        w_hi = st.sbuf("w_hi", [P, ROWS, D], F32R)
        w_lo = st.sbuf("w_lo", [P, ROWS, D], F32R)
        p_raw = st.sbuf("p_raw", [P, 2, D_PLE])
        p_hi = st.sbuf("p_hi", [P, NE, SEQ], F32R)
        p_lo = st.sbuf("p_lo", [P, NE, SEQ], F32R)
        identity = st.sbuf("identity", [P, P])
        ps = st.psum("ps", [P, 8, HALF])
        setup = st.sem("setup")
        w_loaded = [st.sem(f"w_loaded{u}") for u in range(2)]
        p_loaded = [st.sem(f"p_loaded{u}") for u in range(2)]
        w_rounded, w_split = st.sem("w_rounded"), st.sem("w_split")
        p_turned, p_rounded, p_split = st.sem("p_turned"), st.sem("p_rounded"), st.sem("p_split")
        gate_summed, proj_summed, sigmoid_done, multiplied = st.sem("gate_summed"), st.sem("proj_summed"), st.sem("sigmoid_done"), st.sem("multiplied")
        block = st.stack.enter_context(nc.Block())

        @block.sync
        def _(sp):
            sp.dma_start(identity[:], masks[:, 0]).then_inc(setup, 16)
            for t in range(NT):
                if t >= 2:
                    sp.wait_ge(p_turned, t - 1)
                sp.dma_start(p_raw[:, t % 2], p[t * P:(t + 1) * P, :]).then_inc(p_loaded[t % 2], 16)

        @block.gpsimd
        def _(pool):
            for k in range(ROWS):
                if k >= 2:
                    pool.wait_ge(w_split, k - 1)
                src = w_proj[k * P:(k + 1) * P, :] if k < NE else w_gate[(k - NE) * P:(k - NE + 1) * P, :]
                pool.dma_start(w_raw[:, k % 2], src).then_inc(w_loaded[k % 2], 16)

        @block.scalar
        def _(act):
            for k in range(ROWS):
                act.wait_ge(w_loaded[k % 2], 16 * (k // 2 + 1))
                nc.scalar.copy(w_hi[:, k], w_raw[:, k % 2]).then_inc(w_rounded, 1)
                if k < NT:
                    act.wait_ge(p_turned, k + 1)
                    nc.scalar.copy(p_hi[:, :, k * P:(k + 1) * P], ps[:, k % 2, 0:D_PLE].rearrange("p (e t) -> p e t", t=P)).then_inc(p_rounded, 1)
            for t in range(NT):
                for half in range(2):
                    n = 2 * t + half
                    act.wait_ge(gate_summed, n + 1)
                    nc.scalar.activation(out[:, t, half * HALF:(half + 1) * HALF], ps[:, n % 4], ACT.Sigmoid).then_inc(sigmoid_done, 1)

        @block.vector
        def _(dve):
            for k in range(ROWS):
                dve.wait_ge(w_rounded, k + 1)
                nc.vector.tensor_tensor(w_lo[:, k], w_raw[:, k % 2], w_hi[:, k].bitcast(F32), ALU.subtract).then_inc(w_split, 1)
                if k < NT:
                    dve.wait_ge(p_rounded, k + 1)
                    part = (slice(None), slice(None), slice(k * P, (k + 1) * P))
                    nc.vector.tensor_tensor(p_lo[part], ps[:, k % 2, 0:D_PLE].rearrange("p (e t) -> p e t", t=P),
                                            p_hi[part].bitcast(F32), ALU.subtract).then_inc(p_split, 1)
            for t in range(NT):
                for half in range(2):
                    n = 2 * t + half
                    to = out[:, t, half * HALF:(half + 1) * HALF]
                    dve.wait_ge(sigmoid_done, n + 1)
                    dve.wait_ge(proj_summed, n + 1)
                    nc.vector.tensor_tensor(to, to, ps[:, 4 + n % 4], ALU.mult).then_inc(multiplied, 1)

        @block.tensor
        def _(pe):
            pe.wait_ge(setup, 16)
            for t in range(NT):
                pe.wait_ge(p_loaded[t % 2], 16 * (t // 2 + 1))
                if t >= 2:
                    pe.wait_ge(p_split, t - 1)
                for e in range(NE):
                    last = nc.tensor.transpose(ps[:, t % 2, e * P:(e + 1) * P], p_raw[:, t % 2, e * P:(e + 1) * P], identity[:])
                last.then_inc(p_turned, 1)
            pe.wait_ge(p_split, NT)
            pe.wait_ge(w_split, NE)
            for t in range(NT):
                tok = slice(t * P, (t + 1) * P)
                for half in range(2):
                    n = 2 * t + half
                    cols = slice(half * HALF, (half + 1) * HALF)
                    if n >= 4:
                        pe.wait_ge(multiplied, n - 3)
                    for e in range(NE):
                        last = split_matmul(nc, ps[:, 4 + n % 4], (p_hi[:, e, tok], p_lo[:, e, tok]),
                                            (w_hi[:, e, cols], w_lo[:, e, cols]), e == 0, e == NE - 1)
                    last.then_inc(proj_summed, 1)
                    for d in range(ND):
                        if n == 0:
                            pe.wait_ge(w_split, NE + d + 1)
                        last = split_matmul(nc, ps[:, n % 4], (h[0][:, d, tok], h[1][:, d, tok]),
                                            (w_hi[:, NE + d, cols], w_lo[:, NE + d, cols]), d == 0, d == ND - 1)
                    last.then_inc(gate_summed, 1)


def layer(nc, x, p, ffn1_norm_pre, ffn1_w_gate, ffn1_w_up, ffn1_w_down, ffn1_norm_post, mix_norm_pre, w_in, conv_w,
          a_log, dt_bias, norm_w, rwkv_params, w2, a2, g2, w_out, mix_norm_post, ffn2_norm_pre,
          ffn2_w_gate, ffn2_w_up, ffn2_w_down, ffn2_norm_post, ple_norm_pre, ple_w_gate, ple_w_proj, ple_norm_post,
          masks, out):
    def internal(name, shape):
        return nc.dram_tensor(name, shape, F32, kind="Internal").ap()

    x1, x2, x3 = (internal(f"x{n}", [SEQ, D]) for n in (1, 2, 3))
    scratch = internal("tiles", [NT, P, TILE_W])
    z_gate, rwkv_gate, rwkv_bonus = (internal(name, [4, P, SEQ]) for name in ("z_gate", "rwkv_gate", "rwkv_bonus"))

    def h_parts(st):
        return st.sbuf("h_hi", [P, ND, SEQ], F32R), st.sbuf("h_lo", [P, ND, SEQ], F32R)

    with Stage(nc, "layer") as whole:
        identity = whole.sbuf("identity", [P, P])
        carry = whole.sbuf("carry", [P, NT, 4])
        loaded = whole.sem("loaded")
        with nc.Block() as block:
            @block.sync
            def _(sp):
                sp.dma_start(identity[:], masks[:, 0]).then_inc(loaded, 16)
                sp.wait_ge(loaded, 16)

        with Stage(nc, "first") as st:
            h = h_parts(st)
            with Stage(nc, "first_branch") as inner:
                branch = inner.sbuf("branch", [P, NT, D])
                residual_norm(nc, "n1", x, None, None, None, None, ffn1_norm_pre, h, identity[:])
                swiglu(nc, "f1", h, ffn1_w_gate, ffn1_w_up, ffn1_w_down, branch)
                residual_norm(nc, "n2", x, x1, branch, ffn1_norm_post, 0.5, mix_norm_pre, h, identity[:])
            gdn_projection(nc, h, w_in, conv_w, a_log, dt_bias, masks, scratch, z_gate)
            rwkv_projection(nc, h, w_in, w2, a2, g2, rwkv_params, masks, scratch, rwkv_gate, rwkv_bonus, carry)

        with Stage(nc, "second") as st:
            branch = st.sbuf("branch", [P, NT, D])
            recurrences(nc, masks, scratch, carry, branch)
            mixer_output(nc, branch, z_gate, rwkv_gate, rwkv_bonus, norm_w, rwkv_params[:, M_GNW:M_GNW + 4],
                         rwkv_params[:, M_GNB:M_GNB + 4], masks, w_out)
            h = h_parts(st)
            residual_norm(nc, "n3", x1, x2, branch, mix_norm_post, 1.0, ffn2_norm_pre, h, identity[:])
            swiglu(nc, "f2", h, ffn2_w_gate, ffn2_w_up, ffn2_w_down, branch)
            residual_norm(nc, "n4", x2, x3, branch, ffn2_norm_post, 0.5, ple_norm_pre, h, identity[:])
            layer_embedding(nc, h, p, ple_w_gate, ple_w_proj, masks, branch)
            residual_norm(nc, "n5", x3, out, branch, ple_norm_post, 1.0, None, None, identity[:])


def kernel(**inputs):
    import numpy as np
    import concourse.bacc as bacc
    from concourse.bass_utils import run_bass_kernel_spmd

    def rows(*names):
        return np.concatenate([np.asarray(inputs[name]).reshape(-1, P) for name in names]).T

    given = {name: np.asarray(a)[0] for name, a in inputs.items()}
    given["p"] = given["p"][0]
    position = np.arange(P)
    j, i = position[:, None], position[None, :]
    masks = np.zeros((P, MASKS, P), np.float32)
    for n, mask in enumerate([j == i, j >= 0, j <= i, j < i, j // HEAD_N == i // HEAD_N]):
        masks[:, n] = mask
    for level in range(7):
        size = 2 ** level
        masks[:, 5 + level] = (j // (2 * size) == i // (2 * size)) & (j // size < i // size)
    arrays = dict(
        x=given["x"], p=given["p"], ffn1_norm_pre=given["ffn1_norm_pre"], ffn1_w_gate=given["ffn1_w_gate"],
        ffn1_w_up=given["ffn1_w_up"], ffn1_w_down=given["ffn1_w_down"], ffn1_norm_post=given["ffn1_norm_post"],
        mix_norm_pre=given["mix_norm_pre"], w_in=given["w_in"],
        conv_w=given["gdn_conv_w"].reshape(CONV, 12, P).transpose(2, 0, 1),
        a_log=given["gdn_a_log"], dt_bias=given["gdn_dt_bias"],
        norm_w=np.repeat(given["gdn_norm_w"][:, None], 4, axis=1),
        rwkv_params=rows("rwkv_mu", "rwkv_w0", "rwkv_a0", "rwkv_k_k", "rwkv_k_a", "rwkv_r_k", "rwkv_gn_w", "rwkv_gn_b"),
        w2=given["rwkv_w2"], a2=given["rwkv_a2"], g2=given["rwkv_g2"], w_out=given["w_out"],
        mix_norm_post=given["mix_norm_post"], ffn2_norm_pre=given["ffn2_norm_pre"],
        ffn2_w_gate=given["ffn2_w_gate"], ffn2_w_up=given["ffn2_w_up"], ffn2_w_down=given["ffn2_w_down"],
        ffn2_norm_post=given["ffn2_norm_post"], ple_norm_pre=given["ple_norm_pre"], ple_w_gate=given["ple_w_gate"],
        ple_w_proj=given["ple_w_proj"], ple_norm_post=given["ple_norm_post"], masks=masks)
    nc = bacc.Bacc("TRN2", target_bir_lowering=False, num_devices=1)
    launched, args = {}, {}
    for name, a in arrays.items():
        launched[f"in_{name}"] = np.ascontiguousarray(a)
        args[name] = nc.dram_tensor(f"in_{name}", a.shape, mybir.dt.from_np(a.dtype), kind="ExternalInput").ap()
    args["out"] = nc.dram_tensor("out_x", (SEQ, D), F32, kind="ExternalOutput").ap()
    layer(nc, **args)
    result = run_bass_kernel_spmd(nc, [launched], core_ids=[0])
    return result.results[0]["out_x"].reshape(1, SEQ, D)
```

```python
from contextlib import ExitStack

import concourse.bass as bass
from concourse import mybir

F32 = mybir.dt.float32
F32R = mybir.dt.float32r
U32 = mybir.dt.uint32
ALU = mybir.AluOpType
ACT = mybir.ActivationFunctionType

P = 128
SEQ = 1024
D = 1024
D_FF = 2816
D_PLE = 256
NT = SEQ // P
ND = D // P
HALF = 512
NH = SEQ // HALF
NORM_EPS = 1e-6


class Stage:

    def __init__(self, nc, tag):
        self.nc, self.tag, self.stack, self.sems = nc, tag, ExitStack(), []

    def __enter__(self):
        self.stack.__enter__()
        return self

    def __exit__(self, *what):
        self.stack.__exit__(*what)
        if self.sems:
            self.nc.clear_and_free_semaphores(self.sems)
            self.nc.all_engine_barrier()

    def sbuf(self, name, shape, dtype=F32):
        return self.stack.enter_context(self.nc.sbuf_tensor(f"{self.tag}_{name}", shape, dtype))

    def psum(self, name, shape, dtype=F32):
        return self.stack.enter_context(self.nc.psum_tensor(f"{self.tag}_{name}", shape, dtype))

    def sem(self, name):
        self.sems.append(self.nc.alloc_semaphore(f"{self.tag}_{name}"))
        return self.sems[-1]


def split_matmul(nc, out, weights, moving, first, last):
    (w_hi, w_lo), (m_hi, m_lo) = weights, moving
    nc.tensor.matmul(out, w_hi, m_hi, start=first, stop=False)
    nc.tensor.matmul(out, w_hi, m_lo, start=False, stop=False)
    return nc.tensor.matmul(out, w_lo, m_hi, start=False, stop=last)


def row_of(vector):
    return bass.AP(tensor=vector.tensor, offset=vector.offset, ap=[[0, P], [1, vector.shape[-1]]])


class Ahead:

    def __init__(self, pieces):
        self.pieces = pieces

    def load(self, engine, piece, loaded):
        loads = self.pieces[piece][0]
        for place, source in loads:
            engine.dma_start(place, source).then_inc(loaded, 16)
        return 16 * len(loads)

    def upper(self, copy, piece):
        _, raw, hi, _ = self.pieces[piece]
        return copy(hi, raw)

    def lower(self, nc, piece):
        _, raw, hi, lo = self.pieces[piece]
        return nc.gpsimd.tensor_tensor(lo, raw, hi.bitcast(F32), ALU.subtract)


def residual_norm(nc, tag, x_in, x_out, branch, post_gain, share, pre_gain, h, identity, ahead=None,
                  maker=None, loaded=None):
    QUARTER = 0.25
    has_branch, has_h = branch is not None, pre_gain is not None
    with Stage(nc, tag) as st:
        if maker:
            x, added, squares = (branch[:, n:n + 2] for n in (2, 4, 6))
        else:
            added, squares = (st.sbuf(name, [P, 2, D]) for name in ("added", "squares"))
            x = loaded[0] if loaded else st.sbuf("x", [P, 2, D])
        normed = st.sbuf("normed", [P, 2, D]) if has_h else None
        stats = st.sbuf("stats", [P, 2, 8])
        post_row = loaded[1] if loaded else st.sbuf("post_row", [P, D])
        pre_row = loaded[2] if loaded else st.sbuf("pre_row", [P, D]) if has_h else None
        turned = st.psum("turned", [P, 4, HALF]) if has_h else None
        ahead_loaded = [st.sem(f"ahead_loaded{u}") for u in range(2)]
        ahead_rounded, ahead_split = st.sem("ahead_rounded"), st.sem("ahead_split")
        rows_in, row_shared = st.sem("rows_in"), st.sem("row_shared")
        x_loaded = [st.sem(f"x_loaded{u}") for u in range(2)]
        x_stored = [st.sem(f"x_stored{u}") for u in range(2)]
        branch_squared, branch_mean, branch_root = st.sem("branch_squared"), st.sem("branch_mean"), st.sem("branch_root")
        branch_inverse, branch_scaled, x_ready = st.sem("branch_inverse"), st.sem("branch_scaled"), st.sem("x_ready")
        x_squared, x_mean, x_root = st.sem("x_squared"), st.sem("x_mean"), st.sem("x_root")
        x_inverse, x_normed = st.sem("x_inverse"), st.sem("x_normed")
        transposed, hi_done, lo_done = st.sem("transposed"), st.sem("hi_done"), st.sem("lo_done")
        made_act, made_dve = st.sem("made_act"), st.sem("made_dve")
        source = maker(st, made_act, made_dve) if maker else None
        block = st.stack.enter_context(nc.Block())

        def at(u):
            return added[:, u] if has_branch else x[:, u]

        def branch_tile(n, u):
            return branch[:, u] if source else branch[:, bass.ds(n, 1), :].rearrange("p a d -> p (a d)")

        def h_part(part, n, b):
            return h[part][:, 4 * b:4 * b + 4, bass.ds(n * P, P)]

        def staggered(engine, step, aside=lambda piece: None):
            step(-1, 1, 1, has_branch, False, False)
            step(0, 0, 1, has_branch, has_h, False)
            if ahead:
                aside(0)
            with engine.Fori(0, NT // 2 - 1) as i:
                step(2 * i + 1, 1, i + 2, has_branch, has_h, has_h)
                step(2 * i + 2, 0, i + 2, has_branch, has_h, has_h)
            if ahead:
                aside(1)
            step(NT - 1, 1, NT // 2 + 1, False, has_h, has_h)
            step(NT, 0, NT // 2 + 1, False, False, has_h)

        def early(n, count):
            return isinstance(n, int) and n < count

        @block.sync
        def _(sp):
            if loaded:
                sp.nop().then_inc(rows_in, 32)
                for u in range(2):
                    sp.nop().then_inc(x_loaded[u], 16)
            else:
                for u in range(2):
                    sp.dma_start(x[:, u], x_in[u * P:(u + 1) * P, :]).then_inc(x_loaded[u], 16)
                if has_branch:
                    sp.dma_start(post_row[:], row_of(post_gain)).then_inc(rows_in, 16)
                if has_h:
                    sp.dma_start(pre_row[:], row_of(pre_gain)).then_inc(rows_in, 16)

            if ahead:
                for piece in range(2):
                    ahead.load(sp, piece, ahead_loaded[piece])

            def store(n, u):
                sp.wait_ge(x_ready, n + 1)
                sp.dma_start(x_out[bass.ds(n * P, P), :], added[:, u]).then_inc(x_stored[u], 16)

            with sp.Fori(0, NT // 2 - 1) as i:
                for u in range(2):
                    n = 2 * i + u
                    if has_branch:
                        store(n, u)
                    else:
                        sp.wait_ge(x_normed, n + 1)
                    sp.dma_start(x[:, u], x_in[bass.ds((n + 2) * P, P), :]).then_inc(x_loaded[u], 16)
            if has_branch:
                for u in range(2):
                    store(NT - 2 + u, u)
                for u in range(2):
                    sp.wait_ge(x_stored[u], 16 * (NT // 2))

        @block.scalar
        def _(act):
            def step(k, v, pair, adds, norms, turns):
                if adds:
                    if not early(k + 1, 1):
                        act.wait_ge(branch_mean, k + 1)
                    if source:
                        if not early(k + 1, 2):
                            act.wait_ge(branch_scaled, k)
                        source.act(act, k + 1, branch[:, 1 - v], 1 - v)
                        act.wait_ge(made_act, k + 2)
                        act.wait_ge(made_dve, k + 2)
                    nc.scalar.activation(squares[:, 0], branch_tile(k + 1, 1 - v), ACT.Square,
                                         accum_out=stats[:, 1 - v, 0:1]).then_inc(branch_squared, 1)
                if adds:
                    act.wait_ge(branch_mean, k + 2)
                    nc.scalar.activation(stats[:, 1 - v, 2:3], stats[:, 1 - v, 1:2], ACT.Sqrt).then_inc(branch_root, 1)
                if norms:
                    if has_branch:
                        act.wait_ge(x_ready, k + 1)
                    else:
                        act.wait_ge(x_loaded[v], 16 * (pair - v))
                    if not early(k, 1):
                        act.wait_ge(x_mean, k)
                    nc.scalar.activation(squares[:, 1], at(v), ACT.Square, accum_out=stats[:, v, 4:5]).then_inc(x_squared, 1)
                if norms:
                    act.wait_ge(x_mean, k + 1)
                    nc.scalar.activation(stats[:, v, 6:7], stats[:, v, 5:6], ACT.Sqrt).then_inc(x_root, 1)
                if turns:
                    for b in range(2):
                        act.wait_ge(transposed, 2 * k + b - 1)
                        nc.scalar.copy(h_part(0, k - 1, b), turned[:, 2 * (1 - v) + b].rearrange("p (c t) -> p c t", t=P)).then_inc(hi_done, 1)

            def aside(piece):
                act.wait_ge(ahead_loaded[piece], 16 * len(ahead.pieces[piece][0]))
                ahead.upper(nc.scalar.copy, piece).then_inc(ahead_rounded, 1)

            staggered(act, step, aside)

        if has_branch or ahead:
            @block.gpsimd
            def _(pool):
                def step(k, v, pair, adds, norms, turns):
                    if adds:
                        pool.wait_ge(branch_scaled, k + 2)
                        pool.wait_ge(x_loaded[1 - v], 16 * pair)
                        nc.gpsimd.tensor_tensor(added[:, 1 - v], added[:, 1 - v], x[:, 1 - v], ALU.add).then_inc(x_ready, 1)

                staggered(pool, step)
                if ahead:
                    for piece in range(2):
                        pool.wait_ge(ahead_rounded, piece + 1)
                        ahead.lower(nc, piece).then_inc(ahead_split, 1)

        @block.vector
        def _(dve):
            dve.wait_ge(rows_in, 16 * (has_branch + has_h))
            if has_branch:
                nc.vector.tensor_scalar(post_row[:], post_row[:], share, None, ALU.mult).then_inc(row_shared, 1)
                dve.wait_ge(row_shared, 1)

            def inverse_root(s, done, n):
                nc.vector.reciprocal(s[:, 3:4], s[:, 2:3]).then_inc(done, 1)
                dve.wait_ge(done, 3 * n + 1)
                nc.vector.scalar_tensor_tensor(s[:, 0:1], s[:, 1:2], s[:, 3:4], s[:, 2:3], ALU.mult, ALU.add).then_inc(done, 1)
                dve.wait_ge(done, 3 * n + 2)
                nc.vector.reciprocal(s[:, 3:4], s[:, 0:1]).then_inc(done, 1)
                dve.wait_ge(done, 3 * n + 3)

            def step(k, v, pair, adds, norms, turns):
                n, u = k + 1, 1 - v
                if adds and source:
                    if not early(n, 2):
                        dve.wait_ge(branch_scaled, n - 1)
                    source.dve(dve, n, branch[:, u], u)
                if adds:
                    dve.wait_ge(branch_squared, n + 1)
                    nc.vector.tensor_scalar(stats[:, u, 1:2], stats[:, u, 0:1], QUARTER / D, QUARTER * NORM_EPS, ALU.mult, ALU.add).then_inc(branch_mean, 1)
                if adds:
                    dve.wait_ge(branch_root, n + 1)
                    inverse_root(stats[:, u, 0:4], branch_inverse, n)
                    if not early(n, 2):
                        dve.wait_ge(x_stored[u], 16 * (pair - 1))
                        if has_h:
                            dve.wait_ge(x_normed, n - 1)
                    nc.vector.scalar_tensor_tensor(added[:, u], branch_tile(n, u), stats[:, u, 3:4], post_row[:],
                                                   ALU.mult, ALU.mult).then_inc(branch_scaled, 1)
                if norms:
                    dve.wait_ge(x_squared, k + 1)
                    nc.vector.tensor_scalar(stats[:, v, 5:6], stats[:, v, 4:5], QUARTER / D, QUARTER * NORM_EPS, ALU.mult, ALU.add).then_inc(x_mean, 1)
                if norms:
                    dve.wait_ge(x_root, k + 1)
                    inverse_root(stats[:, v, 4:8], x_inverse, k)
                    nc.vector.scalar_tensor_tensor(normed[:, v], at(v), stats[:, v, 7:8], pre_row[:],
                                                   ALU.mult, ALU.mult).then_inc(x_normed, 1)
                if turns:
                    for b in range(2):
                        dve.wait_ge(hi_done, 2 * k + b - 1)
                        nc.vector.tensor_tensor(h_part(1, k - 1, b), turned[:, 2 * u + b].rearrange("p (c t) -> p c t", t=P),
                                                h_part(0, k - 1, b).bitcast(F32), ALU.subtract).then_inc(lo_done, 1)

            staggered(dve, step)

        if has_h or source:
            @block.tensor
            def _(pe):
                def turn(n, u):
                    pe.wait_ge(x_normed, n + 1)
                    for b in range(2):
                        if not early(n, 2):
                            pe.wait_ge(lo_done, 2 * n + b - 3)
                        for c in range(4):
                            d = 4 * b + c
                            last = nc.tensor.transpose(turned[:, 2 * u + b, c * P:(c + 1) * P],
                                                       normed[:, u, d * P:(d + 1) * P], identity)
                        last.then_inc(transposed, 1)

                if not source:
                    for u in range(2):
                        turn(u, u)
                    with pe.Fori(1, NT // 2) as i:
                        for u in range(2):
                            turn(2 * i + u, u)
                else:
                    for n in range(NT + 2):
                        if n < NT:
                            source.products(pe, n)
                        if has_h and n >= 2:
                            turn(n - 2, n % 2)


def first_chunks(up, w_gate, w_up):
    raw, hi, lo = up
    cols = [w.rearrange("(d p) f -> p d f", p=P) for w in (w_gate, w_up)]
    return Ahead([([(raw[:, u, k], cols[k][:, :, u * P:(u + 1) * P]) for k in range(2)], raw[:, u], hi[:, u], lo[:, u]) for u in range(2)])


def swiglu(nc, tag, h, w_gate, w_up, w_down, out, up, ahead=True, after=()):
    CH = D_FF // P
    GROUPS = CH // 2
    LOOPS = (GROUPS - 1) // 2
    START = 2 * NT + 1
    with Stage(nc, tag) as st:
        up_raw, up_hi, up_lo = up
        down_raw = st.sbuf("down_raw", [P, 2, 2, HALF])
        down_hi = st.sbuf("down_hi", [P, 2, 2, HALF], F32R)
        down_lo = st.sbuf("down_lo", [P, 2, 2, HALF], F32R)
        a_hi = st.sbuf("a_hi", [P, 4, SEQ], F32R)
        a_lo = st.sbuf("a_lo", [P, 4, SEQ], F32R)
        product = st.sbuf("product", [P, 2, HALF])
        up_ps = st.psum("up_ps", [P, 2, 2, HALF])
        down_ps = st.psum("down_ps", [P, 4, HALF])
        up_loaded = [st.sem(f"up_loaded{u}") for u in range(2)]
        down_loaded = [st.sem(f"down_loaded{u}") for u in range(2)]
        up_rounded, up_split = st.sem("up_rounded"), st.sem("up_split")
        down_rounded, down_split = st.sem("down_rounded"), st.sem("down_split")
        up_summed, silu_done, multiplied = st.sem("up_summed"), st.sem("silu_done"), st.sem("multiplied")
        a_rounded, a_split = st.sem("a_rounded"), st.sem("a_split")
        down_summed, down_added = st.sem("down_summed"), st.sem("down_added")
        after_loaded = st.sem("after_loaded")
        block = st.stack.enter_context(nc.Block())

        gate_cols = w_gate.rearrange("(d p) f -> p d f", p=P)
        up_cols = w_up.rearrange("(d p) f -> p d f", p=P)
        down_rows = w_down.rearrange("(c p) n -> p c n", p=P)

        def steps(engine, up, down):
            up(0, 0, 0)
            up(1, 1, 0)
            with engine.Fori(0, LOOPS) as i:
                for g in range(2):
                    up(4 * i + 2 * g + 2, (2 * g + 2) % 4, 2 * i + g + 1)
                    up(4 * i + 2 * g + 3, (2 * g + 3) % 4, 2 * i + g + 1)
                    down(2 * i + g, g)


        def is_first(c, n=1):
            return isinstance(c, int) and c < n

        @block.sync
        def _(sp):
            def load_up(c, u, free):
                if free is not None:
                    sp.wait_ge(up_split, free)
                for k, cols in enumerate((gate_cols, up_cols)):
                    sp.dma_start(up_raw[:, u, k], cols[:, :, bass.ds(c * P, P)]).then_inc(up_loaded[u], 16)

            def load_down(g, half, free):
                if free is not None:
                    sp.wait_ge(down_split, free)
                sp.dma_start(down_raw[:, half], down_rows[:, bass.ds(2 * g, 2), half * HALF:(half + 1) * HALF]).then_inc(down_loaded[half], 16)

            for u in range(2):
                if ahead:
                    sp.nop().then_inc(up_loaded[u], 32)
                else:
                    load_up(u, u, None)
            load_down(0, 0, None)
            load_down(0, 1, None)
            with sp.Fori(1, GROUPS) as g:
                load_up(2 * g, 0, 2 * g - 1)
                load_up(2 * g + 1, 1, 2 * g)
                load_down(g, 0, 2 * g - 1)
                load_down(g, 1, 2 * g)
            sp.wait_ge(up_split, CH)
            for place, source in after:
                sp.dma_start(place, source).then_inc(after_loaded, 16)
            if after:
                sp.wait_ge(after_loaded, 16 * len(after))

        @block.scalar
        def _(act):
            def finish(c, q, g):
                for t in range(NH):
                    n = 2 * c + t
                    act.wait_ge(up_summed, n + 1)
                    if not is_first(c):
                        act.wait_ge(a_split, n - 1)
                    nc.scalar.activation(product[:, t], up_ps[:, t, 0], ACT.Silu).then_inc(silu_done, 1)
                    act.wait_ge(multiplied, n + 1)
                    act.wait_ge(down_added, START + 2 * NT * (g - 1))
                    nc.scalar.copy(a_hi[:, q, t * HALF:(t + 1) * HALF], product[:, t]).then_inc(a_rounded, 1)

            def round_down(g):
                for half in range(2):
                    act.wait_ge(down_loaded[half], 16 * (g + 1))
                    act.wait_ge(down_added, START + NT * (2 * g + half - 1))
                    nc.scalar.copy(down_hi[:, half], down_raw[:, half]).then_inc(down_rounded, 1)

            def up(c, q, g):
                u = q % 2
                act.wait_ge(up_loaded[u], 32 * (g + 1))
                if not is_first(c, 2):
                    act.wait_ge(up_summed, 2 * c - 2)
                if ahead and is_first(c, 2):
                    nc.scalar.nop().then_inc(up_rounded, 1)
                else:
                    nc.scalar.copy(up_hi[:, u], up_raw[:, u]).then_inc(up_rounded, 1)
                if not is_first(c):
                    finish(c - 1, (q - 1) % 4, g - (1 - u))
                if not is_first(c, 2) and u == 0:
                    round_down(g - 1)

            steps(act, up, lambda g, odd: None)
            finish(CH - 1, (CH - 1) % 4, GROUPS - 1)
            round_down(GROUPS - 1)

        @block.gpsimd
        def _(pool):
            def finish(c, q, g):
                for t in range(NH):
                    part = (slice(None), q, slice(t * HALF, (t + 1) * HALF))
                    pool.wait_ge(a_rounded, 2 * c + t + 1)
                    nc.gpsimd.tensor_tensor(a_lo[part], product[:, t], a_hi[part].bitcast(F32), ALU.subtract).then_inc(a_split, 1)

            def split_down(g):
                for half in range(2):
                    pool.wait_ge(down_rounded, 2 * g + half + 1)
                    nc.gpsimd.tensor_tensor(down_lo[:, half], down_raw[:, half], down_hi[:, half].bitcast(F32), ALU.subtract).then_inc(down_split, 1)

            def up(c, q, g):
                u = q % 2
                pool.wait_ge(up_rounded, c + 1)
                if ahead and is_first(c, 2):
                    nc.gpsimd.nop().then_inc(up_split, 1)
                else:
                    nc.gpsimd.tensor_tensor(up_lo[:, u], up_raw[:, u], up_hi[:, u].bitcast(F32), ALU.subtract).then_inc(up_split, 1)
                if not is_first(c):
                    finish(c - 1, (q - 1) % 4, g - (1 - u))
                if not is_first(c, 2) and u == 0:
                    split_down(g - 1)

            steps(pool, up, lambda g, odd: None)
            finish(CH - 1, (CH - 1) % 4, GROUPS - 1)
            split_down(GROUPS - 1)

        @block.vector
        def _(dve):
            nc.vector.nop().then_inc(down_added, 1)
            for t in range(NT):
                for half in range(2):
                    nc.vector.memset(out[:, t, half * HALF:(half + 1) * HALF], 0.0).then_inc(down_added, 1)

            def up(c, q, g):
                for t in range(NH):
                    n = 2 * c + t
                    dve.wait_ge(silu_done, n + 1)
                    nc.vector.tensor_tensor(product[:, t], product[:, t], up_ps[:, t, 1], ALU.mult).then_inc(multiplied, 1)

            def down(g, odd):
                for half in range(2):
                    for t in range(NT):
                        k = half * NT + t
                        dve.wait_ge(down_summed, 2 * NT * g + k + 1)
                        dve.wait_ge(down_added, START + 2 * NT * g + k)
                        to = out[:, t, half * HALF:(half + 1) * HALF]
                        nc.vector.tensor_tensor(to, to, down_ps[:, k % 4], ALU.add).then_inc(down_added, 1)

            steps(dve, up, down)
            down(GROUPS - 1, (GROUPS - 1) % 2)

        @block.tensor
        def _(pe):
            def up(c, q, g):
                u = q % 2
                pe.wait_ge(up_split, c + 1)
                for t in range(NH):
                    if not is_first(c):
                        pe.wait_ge(multiplied, 2 * c + t - 1)
                    for k in range(2):
                        for d in range(ND):
                            last = split_matmul(nc, up_ps[:, t, k], (up_hi[:, u, k, d], up_lo[:, u, k, d]),
                                                tuple(part[:, d, t * HALF:(t + 1) * HALF] for part in h), d == 0, d == ND - 1)
                    last.then_inc(up_summed, 1)

            def down(g, odd):
                pe.wait_ge(a_split, 4 * g + 4)
                for half in range(2):
                    pe.wait_ge(down_split, 2 * g + half + 1)
                    for t in range(NT):
                        k = half * NT + t
                        pe.wait_ge(down_added, START + 2 * NT * g + k - 3)
                        for j in range(2):
                            slot = 2 * odd + j
                            last = split_matmul(nc, down_ps[:, k % 4], (a_hi[:, slot, t * P:(t + 1) * P], a_lo[:, slot, t * P:(t + 1) * P]),
                                                (down_hi[:, half, j], down_lo[:, half, j]), j == 0, j == 1)
                        last.then_inc(down_summed, 1)

            steps(pe, up, down)
            down(GROUPS - 1, (GROUPS - 1) % 2)


GDN_HEADS, GDN_DK = 4, 128
CONV = 4
RWKV_BLOCKS = 4
GDN_QK, GDN_V, GDN_Z = 0, 1024, 1536
GDN_SMALL = 2048
RWKV_COLS = 2056
RWKV_W = 512
L2_EPS = 1e-6

S_Q, S_K, S_V, S_INCL, S_STRICT, S_RWKV = 0, 8, 16, 20, 24, 28
R_KK, R_R, R_K, R_B, R_V, R_SLOTS = 0, 1, 2, 3, 4, 5
SLOTS = S_RWKV + R_SLOTS * RWKV_BLOCKS
COLS = 16
C_GDN = SLOTS * P
TILE_W = SLOTS * P + COLS


class Steps:

    def __init__(self, sem, names):
        self.sem, self.names, self.next = sem, names.split(), 0

    def open(self, engine):
        engine.nop().then_inc(self.sem, len(self.names))

    def done(self, instruction, name):
        assert name == self.names[self.next], (name, self.names[self.next])
        self.next = (self.next + 1) % len(self.names)
        instruction.then_inc(self.sem, 1)

    def wait(self, engine, name, turn):
        engine.wait_ge(self.sem, len(self.names) * (turn + 1) + self.names.index(name) + 1)


def stream_weights(nc, pool, gate, w_raw, w_hi, w_lo, w_loaded, w_rounded, w_split, projected, blocks, ahead):
    def split(k, s, first):
        pool.wait_ge(w_loaded[s], 16 * (k // 2 + 1) if isinstance(k, int) else 16 * first)
        if not (isinstance(k, int) and k < 2):
            pool.wait_ge(projected, k - 1)
        nc.gpsimd.tensor_tensor(gate[:, 0:1], gate[:, 1:2], gate[:, 1:2], ALU.add)
        nc.gpsimd.tensor_copy(w_hi[:, s], w_raw[:, s]).then_inc(w_rounded, 1)
        pool.wait_ge(w_rounded, k + 2)
        nc.gpsimd.tensor_tensor(w_lo[:, s], w_raw[:, s], w_hi[:, s].bitcast(F32), ALU.subtract).then_inc(w_split, 1)

    nc.gpsimd.memset(gate, 0.0).then_inc(w_rounded, 1)
    pool.wait_ge(w_rounded, 1)
    if ahead:
        for _ in range(2):
            nc.gpsimd.nop().then_inc(w_rounded, 1)
            nc.gpsimd.nop().then_inc(w_split, 1)
    else:
        split(0, 0, 1)
        split(1, 1, 1)
    with pool.Fori(1, blocks // 2) as i:
        split(2 * i, 0, i + 1)
        split(2 * i + 1, 1, i + 1)
    if blocks % 2:
        split(blocks - 1, 0, None)


def first_blocks(places, w_in, starts):
    raw, hi, lo = places
    cols = w_in.rearrange("(d p) f -> p d f", p=P)
    return Ahead([([(raw[:, u], cols[:, :, start:start + P])], raw[:, u], hi[:, u], lo[:, u]) for u, start in enumerate(starts)])


def gdn_projection(nc, h, w_in, conv_w, a_log, dt_bias, masks, scratch, z_gate, places):
    with Stage(nc, "gp") as st:
        w_raw, w_hi, w_lo = places
        x_ext = st.sbuf("x_ext", [P, 2, 4 + SEQ])
        conv = st.sbuf("conv", [P, SEQ])
        act_out = st.sbuf("act_out", [P, 2, SEQ])
        square = st.sbuf("square", [P, SEQ])
        root = st.sbuf("root", [P, SEQ])
        unit = st.sbuf("unit", [P, 2, SEQ])
        scaled = st.sbuf("scaled", [P, 2, SEQ])
        rows = st.sbuf("rows", [P, 8, SEQ])
        taps = st.sbuf("taps", [P, CONV, 12])
        scale_col = st.sbuf("scale_col", [P, 8])
        eps = st.sbuf("eps", [P, 1])
        gate = st.sbuf("gate", [P, 2])
        mask = st.sbuf("mask", [P, 4, P])
        a_row = st.sbuf("a_row", [P, GDN_HEADS])
        dt_row = st.sbuf("dt_row", [P, GDN_HEADS])
        s = st.sbuf("small", [P, 12, NT, GDN_HEADS])
        gb = st.sbuf("gb", [P, NT, 8])
        gc_rows = st.sbuf("gc_rows", [P, 4, P])
        spread = st.sbuf("spread", [P, 2, 4, P])
        gaps = st.sbuf("gaps", [P, 4, P])
        decay = st.sbuf("decay", [P, 4, P])
        diag = decay
        decays = st.sbuf("decays", [P, 8, P])
        exps = st.sbuf("exps", [P, 16])
        cols = st.sbuf("cols", [P, 16])
        proj = st.psum("proj", [P, 2, 2, HALF])
        sums = st.psum("sums", [P, 2, HALF])
        row_ps = st.psum("row_ps", [P, 2, HALF])

        setup, ready = st.sem("setup"), st.sem("ready")
        w_loaded = [st.sem(f"w_loaded{u}") for u in range(2)]
        w_rounded, w_split, projected = st.sem("w_rounded"), st.sem("w_split"), st.sem("projected")
        copied, tapped, convolved, silu_done = st.sem("copied"), st.sem("tapped"), st.sem("convolved"), st.sem("silu_done")
        squared, summed, rooted = st.sem("squared"), st.sem("summed"), st.sem("rooted")
        unit_ready, scaled_ready = st.sem("unit_ready"), st.sem("scaled_ready")
        turned, small_dve, small_act = st.sem("turned"), st.sem("small_dve"), st.sem("small_act")
        spread_ready, rows_summed, rows_copied = st.sem("spread_ready"), st.sem("rows_summed"), st.sem("rows_copied")
        col_step, gaps_ready, decayed, decays_ready = st.sem("col_step"), st.sem("gaps_ready"), st.sem("decayed"), st.sem("decays_ready")
        exps_done = st.sem("exps_done")
        act_stored, decay_stored = [st.sem(f"act_stored{u}") for u in range(2)], st.sem("decay_stored")
        unit_stored, scaled_stored = [st.sem(f"unit_stored{u}") for u in range(2)], [st.sem(f"scaled_stored{u}") for u in range(2)]
        block = st.stack.enter_context(nc.Block())

        w_cols = w_in.rearrange("(d p) f -> p d f", p=P)
        tiles = scratch.rearrange("c p w -> p c w")
        K_V, K_Z, K_QK, BLOCKS = 1, 5, 9, 17
        SETUP = 16 * 4

        def in_pairs(engine, body, n):
            with engine.Fori(0, n // 2) as i:
                for u in range(2):
                    body(2 * i + u, u, i)

        def lagged(engine, first, second):
            first(0, 0, 0)
            with engine.Fori(0, 3) as i:
                for u in range(2):
                    first(2 * i + u + 1, (u + 1) % 2, i + u)
                    second(2 * i + u, u, i)
            first(7, 1, 3)
            second(6, 0, 3)
            second(7, 1, 3)

        @block.sync
        def _(sp):
            for stored in act_stored + unit_stored + scaled_stored:
                sp.nop().then_inc(stored, 16)
            sp.nop().then_inc(decay_stored, 32)
            sp.dma_start(taps[:], conv_w).then_inc(setup, 16)
            sp.dma_start(mask[:], masks[:, 0:4]).then_inc(setup, 16)
            sp.dma_start(a_row[:], row_of(a_log)).then_inc(setup, 16)
            sp.dma_start(dt_row[:], row_of(dt_bias)).then_inc(setup, 16)

            def load(col, s_, split):
                if split is not None:
                    sp.wait_ge(w_split, split)
                sp.dma_start(w_raw[:, s_], w_cols[:, :, bass.ds(col, P)]).then_inc(w_loaded[s_], 16)

            for u in range(2):
                sp.nop().then_inc(w_loaded[u], 16)
            load(GDN_V + P, 0, 1)

            def decays_out(c):
                sp.wait_ge(decays_ready, c + 1)
                sp.dma_start(scratch[bass.ds(c, 1), :, S_INCL * P:S_RWKV * P].rearrange("a p w -> p (a w)"),
                             decays[:].rearrange("p s t -> p (s t)")).then_inc(decay_stored, 16)
                sp.dma_start(scratch[bass.ds(c, 1), :, C_GDN:C_GDN + 16].rearrange("a p w -> p (a w)"), cols[:]).then_inc(decay_stored, 16)

            def v_step(j, u, i):
                load(GDN_V + (j + 2) * P, 1 - u, j + 2)
                decays_out(j)
                sp.wait_ge(silu_done, j + 1)
                sp.dma_start(tiles[:, :, bass.ds((S_V + j) * P, P)], act_out[:, u].rearrange("p (c t) -> p c t", t=P)).then_inc(act_stored[u], 16)

            def z_step(j, u, i):
                load((GDN_Z + (j + 2) * P) % GDN_SMALL, 1 - u, j + 6)
                decays_out(j + 4)
                sp.wait_ge(silu_done, j + 5)
                sp.dma_start(z_gate[bass.ds(j, 1)].rearrange("a p t -> p (a t)"), act_out[:, u]).then_inc(act_stored[u], 16)

            in_pairs(sp, v_step, 4)
            for j in range(4):
                z_step(j, j % 2, j // 2)

            def qk_store(b, u, i):
                sp.wait_ge(unit_ready, b + 2)
                sp.dma_start(tiles[:, :, bass.ds(2 * b * P, P)], unit[:, u].rearrange("p (c t) -> p c t", t=P)).then_inc(unit_stored[u], 16)
                sp.wait_ge(scaled_ready, b + 1)
                sp.dma_start(tiles[:, :, bass.ds((2 * b + 1) * P, P)], scaled[:, u].rearrange("p (c t) -> p c t", t=P)).then_inc(scaled_stored[u], 16)

            load(2 * P, 1, K_QK + 1)
            with sp.Fori(0, 2) as i:
                for u in range(2):
                    load((2 * i + u + 3) * P, u, 2 * i + u + K_QK + 2)
                    qk_store(2 * i + u, u, i)
            load(7 * P, 0, 5 + K_QK + 1)
            for b in range(4, 8):
                qk_store(b, b % 2, b // 2)
            for u in range(2):
                sp.wait_ge(act_stored[u], 16 * 5)
                sp.wait_ge(unit_stored[u], 16 * 5)
                sp.wait_ge(scaled_stored[u], 16 * 5)
            sp.wait_ge(decay_stored, 32 * (NT + 1))

        @block.gpsimd
        def _(pool):
            stream_weights(nc, pool, gate[:], w_raw, w_hi, w_lo, w_loaded, w_rounded, w_split, projected, BLOCKS, True)

        @block.tensor
        def _(pe):
            def project(k, s_):
                pe.wait_ge(w_split, k + 1)
                if not (isinstance(k, int) and k < 2):
                    pe.wait_ge(copied, k)
                for t in range(NH):
                    for d in range(ND):
                        last = split_matmul(nc, proj[:, s_, t], (w_hi[:, s_, d], w_lo[:, s_, d]),
                                            tuple(part[:, d, t * HALF:(t + 1) * HALF] for part in h), d == 0, d == ND - 1)
                last.then_inc(projected, 1)

            def sum_rows(c):
                pe.wait_ge(spread_ready, 2 * c + 2)
                pe.wait_ge(rows_copied, 2 * c + 1)
                for n in range(2):
                    last = nc.tensor.matmul(row_ps[:, n], mask[:, 1], spread[:, n].rearrange("p n t -> p (n t)"), start=True, stop=True)
                last.then_inc(rows_summed, 1)

            project(0, 0)
            pe.wait_ge(setup, SETUP)
            pe.wait_ge(copied, 2)
            for c in range(NT):
                last = nc.tensor.transpose(sums[:, c // 4, (c % 4) * P:(c % 4 + 1) * P], x_ext[:, 0, 4 + c * P:4 + (c + 1) * P], mask[:, 0])
            last.then_inc(turned, 1)

            def vz_step(j, u, i):
                project(j + 1, (u + 1) % 2)
                sum_rows(j)

            in_pairs(pe, vz_step, 8)

            def sum_squares(b, u, i):
                pe.wait_ge(squared, b + 1)
                for t in range(NH):
                    pe.wait_ge(rooted, 2 * b + 1)
                    last = nc.tensor.matmul(sums[:, t], mask[:, 1], square[:, t * HALF:(t + 1) * HALF], start=True, stop=True)
                last.then_inc(summed, 1)

            lagged(pe, lambda b, u, i: project(b + K_QK, (u + 1) % 2), sum_squares)

        @block.scalar
        def _(act):
            act.wait_ge(setup, SETUP)
            act.wait_ge(ready, 1)

            def copy_block(k, s_):
                act.wait_ge(projected, k + 1)
                nc.scalar.copy(x_ext[:, s_, 4:], proj[:, s_].rearrange("p n t -> p (n t)")).then_inc(copied, 1)

            copy_block(0, 0)
            act.wait_ge(small_dve, 1)
            nc.scalar.activation(s[:, 0], gb[:, :, 0:4], ACT.Sigmoid).then_inc(small_act, 1)
            nc.scalar.activation(a_row[:], a_row[:], ACT.Exp).then_inc(small_act, 1)
            act.wait_ge(small_dve, 4)
            nc.scalar.activation(s[:, 4], s[:, 3], ACT.Exp, scale=-1.0).then_inc(small_act, 1)
            act.wait_ge(small_dve, 5)
            nc.scalar.activation(s[:, 6], s[:, 5], ACT.Ln).then_inc(small_act, 1)

            def rows_of(c):
                act.wait_ge(rows_summed, c + 1)
                nc.scalar.copy(gc_rows[:], row_ps[:, 0].rearrange("p (n t) -> p n t", t=P)).then_inc(rows_copied, 1)
                nc.scalar.copy(rows[:, 4:8, bass.ds(c * P, P)], row_ps[:, 1].rearrange("p (n t) -> p n t", t=P)).then_inc(rows_copied, 1)
                act.wait_ge(rows_copied, 2 * c + 3)
                nc.scalar.activation(rows[:, 0:4, bass.ds(c * P, P)], gc_rows[:], ACT.Exp)
                act.wait_ge(gaps_ready, c + 1)
                nc.scalar.activation(decay[:], gaps[:], ACT.Exp).then_inc(decayed, 1)
                nc.scalar.activation(exps[:, 0:12], exps[:, 0:12], ACT.Exp).then_inc(exps_done, 1)

            def tap_last(s_, blk):
                nc.scalar.activation(conv[:], x_ext[:, s_, 4:], ACT.Copy, scale=taps[:, CONV - 1, bass.ds(blk, 1)]).then_inc(tapped, 1)

            def v_step(j, u, i):
                s_ = (u + 1) % 2
                copy_block(j + K_V, s_)
                act.wait_ge(copied, j + K_V + 2)
                tap_last(s_, j + 8)
                rows_of(j)
                act.wait_ge(convolved, 3 * j + 3)
                act.wait_ge(act_stored[u], 16 * (i + 1))
                nc.scalar.activation(act_out[:, u], conv[:], ACT.Silu).then_inc(silu_done, 1)

            def z_step(j, u, i):
                s_ = (u + 1) % 2
                copy_block(j + K_Z, s_)
                rows_of(j + 4)
                act.wait_ge(copied, j + K_Z + 2)
                act.wait_ge(act_stored[u], 16 * (i + 3))
                nc.scalar.activation(act_out[:, u], x_ext[:, s_, 4:], ACT.Silu).then_inc(silu_done, 1)

            in_pairs(act, v_step, 4)
            in_pairs(act, z_step, 4)

            def qk_first(b, u, i):
                s_ = (u + 1) % 2
                copy_block(b + K_QK, s_)
                act.wait_ge(copied, b + K_QK + 2)
                tap_last(s_, b)
                act.wait_ge(convolved, 3 * (b + 4) + 3)
                act.wait_ge(act_stored[u], 16 * 5)
                if not (isinstance(b, int) and b < 1):
                    act.wait_ge(unit_ready, b)
                nc.scalar.activation(act_out[:, u], conv[:], ACT.Silu).then_inc(silu_done, 1)
                act.wait_ge(silu_done, b + 9)
                if not (isinstance(b, int) and b < 1):
                    act.wait_ge(summed, b)
                nc.scalar.activation(square[:], act_out[:, u], ACT.Square).then_inc(squared, 1)

            def qk_second(b, u, i):
                act.wait_ge(summed, b + 1)
                act.wait_ge(unit_ready, b + 1)
                nc.scalar.activation(root[:], sums[:].rearrange("p n t -> p (n t)"), ACT.Ln, bias=eps[:]).then_inc(rooted, 1)
                act.wait_ge(rooted, 2 * b + 2)
                nc.scalar.activation(root[:], root[:], ACT.Exp, scale=-0.5).then_inc(rooted, 1)

            lagged(act, qk_first, qk_second)

        @block.vector
        def _(dve):
            nc.vector.memset(eps[:], L2_EPS)
            nc.vector.memset(scale_col[:, 0:4], GDN_DK ** -0.5)
            nc.vector.memset(scale_col[:, 4:8], 1.0)
            nc.vector.memset(x_ext[:, :, 0:4], 0.0).then_inc(ready, 1)
            for free in (rows_copied, copied, rooted, unit_ready):
                nc.vector.nop().then_inc(free, 1)
            dve.wait_ge(setup, SETUP)
            dve.wait_ge(ready, 1)
            step = [0]

            def small(ins):
                ins.then_inc(small_dve, 1)
                step[0] += 1
                dve.wait_ge(small_dve, step[0])

            dt = dt_row[:].rearrange("p (a n) -> p a n", a=1).broadcast_to([P, NT, GDN_HEADS])
            ea = a_row[:].rearrange("p (a n) -> p a n", a=1).broadcast_to([P, NT, GDN_HEADS])
            dve.wait_ge(turned, 1)
            small(nc.vector.tensor_copy(gb[:], sums[:].rearrange("p n (c t) -> p (n c) t", t=P)[:, :, 0:8]))
            small(nc.vector.tensor_tensor(s[:, 1], gb[:, :, 4:8], dt, ALU.add))
            small(nc.vector.tensor_scalar(s[:, 2], s[:, 1], -1.0, None, ALU.mult))
            small(nc.vector.tensor_tensor(s[:, 3], s[:, 1], s[:, 2], ALU.max))
            dve.wait_ge(small_act, 3)
            small(nc.vector.tensor_scalar(s[:, 5], s[:, 4], 1.0, None, ALU.add))
            small(nc.vector.tensor_scalar(s[:, 7], s[:, 5], 1.0, None, ALU.is_equal))
            small(nc.vector.scalar_tensor_tensor(s[:, 8], s[:, 5], -1.0, s[:, 7], ALU.add, ALU.add))
            small(nc.vector.reciprocal(s[:, 9], s[:, 8]))
            dve.wait_ge(small_act, 4)
            small(nc.vector.tensor_tensor(s[:, 8], s[:, 6], s[:, 7], ALU.add))
            small(nc.vector.tensor_tensor(s[:, 8], s[:, 8], s[:, 9], ALU.mult))
            small(nc.vector.tensor_tensor(s[:, 8], s[:, 8], s[:, 4], ALU.mult))
            small(nc.vector.scalar_tensor_tensor(s[:, 10], s[:, 1], 0.0, s[:, 8], ALU.max, ALU.add))
            small(nc.vector.scalar_tensor_tensor(s[:, 10], s[:, 10], -1.0, ea, ALU.mult, ALU.mult))
            small(nc.vector.tensor_scalar(s[:, 11], s[:, 0], -1.0, None, ALU.mult))

            def over_heads(n):
                return mask[:, n:n + 1].broadcast_to([P, GDN_HEADS, P])

            def spread_rows(c):
                for n, (m, of) in enumerate(((2, 10), (0, 11))):
                    nc.vector.tensor_tensor(spread[:, n], over_heads(m), per_head(s[:, of, bass.ds(c, 1), :]), ALU.mult).then_inc(spread_ready, 1)

            def per_head(ap):
                return ap.rearrange("p a n -> p n a").broadcast_to([P, GDN_HEADS, P])

            def decays_of(c):
                g_rows = gc_rows[:]
                dve.wait_ge(rows_copied, 2 * c + 2)
                nc.vector.tensor_tensor(diag[:], g_rows, over_heads(0), ALU.mult).then_inc(col_step, 1)
                dve.wait_ge(col_step, 6 * c + 1)
                nc.vector.tensor_reduce(exps[:, 0:4], diag[:], mybir.AxisListType.X, ALU.add).then_inc(col_step, 1)
                nc.vector.tensor_copy(exps[:, 8:12], g_rows[:, :, P - 1]).then_inc(col_step, 1)
                dve.wait_ge(col_step, 6 * c + 3)
                nc.vector.tensor_tensor(gaps[:], g_rows, exps[:, 0:4].rearrange("p (n a) -> p n a", a=1).broadcast_to([P, GDN_HEADS, P]), ALU.subtract).then_inc(col_step, 1)
                nc.vector.tensor_tensor(exps[:, 4:8], exps[:, 8:12], exps[:, 0:4], ALU.subtract).then_inc(col_step, 1)
                dve.wait_ge(col_step, 6 * c + 5)
                nc.vector.tensor_scalar(exps[:, 4:8], exps[:, 4:8], 0.0, None, ALU.min).then_inc(col_step, 1)
                nc.vector.tensor_scalar(gaps[:], gaps[:], 0.0, None, ALU.min).then_inc(gaps_ready, 1)
                dve.wait_ge(exps_done, c + 1)
                dve.wait_ge(decay_stored, 32 * (c + 1))
                beta = s[:, 0, bass.ds(c, 1), :].rearrange("p a n -> p (a n)")
                minus_beta = s[:, 11, bass.ds(c, 1), :].rearrange("p a n -> p (a n)")
                nc.vector.tensor_copy(cols[:, 0:4], beta)
                nc.vector.tensor_tensor(cols[:, 4:8], exps[:, 0:4], minus_beta, ALU.mult)
                nc.vector.tensor_copy(cols[:, 8:16], exps[:, 4:12])
                nc.vector.tensor_tensor(decays[:, 0:4], decay[:], over_heads(2), ALU.mult)
                nc.vector.tensor_tensor(decays[:, 4:8], decay[:], over_heads(3), ALU.mult).then_inc(decays_ready, 1)

            def convolve(n, s_, blk):
                dve.wait_ge(tapped, n + 1)
                for j in range(CONV - 1):
                    if j:
                        dve.wait_ge(convolved, 3 * n + j)
                    nc.vector.scalar_tensor_tensor(conv[:], x_ext[:, s_, j + 1:j + 1 + SEQ], taps[:, j, bass.ds(blk, 1)], conv[:],
                                                   ALU.mult, ALU.add).then_inc(convolved, 1)

            def v_step(j, u, i):
                spread_rows(j)
                convolve(j, (u + 1) % 2, j + 8)
                decays_of(j)

            def z_step(j, u, i):
                spread_rows(j + 4)
                decays_of(j + 4)

            in_pairs(dve, v_step, 4)
            in_pairs(dve, z_step, 4)

            def qk_first(b, u, i):
                convolve(b + 4, (u + 1) % 2, b)

            def qk_second(b, u, i):
                dve.wait_ge(rooted, 2 * b + 3)
                dve.wait_ge(unit_stored[u], 16 * (i + 1))
                dve.wait_ge(scaled_stored[u], 16 * (i + 1))
                nc.vector.scalar_tensor_tensor(unit[:, u], act_out[:, u], scale_col[:, bass.ds(b, 1)], root[:], ALU.mult, ALU.mult).then_inc(unit_ready, 1)
                dve.wait_ge(unit_ready, b + 2)
                nc.vector.tensor_tensor(scaled[:, u], unit[:, u], rows[:, bass.ds(b, 1), :].rearrange("p a t -> p (a t)"), ALU.mult).then_inc(scaled_ready, 1)

            lagged(dve, qk_first, qk_second)


EXP_HALF = 0.6065306597126334
M_MU, M_W0, M_A0, M_KK, M_KA, M_RK, M_GNW, M_GNB, M_COLS = 0, 14, 18, 22, 26, 30, 34, 38, 42
LORA_WA, LORA_G = 12, 13


def rwkv_projection(nc, h, w_in, w2, a2, g2, params, masks, scratch, gate_out, bonus_out, carry):
    with Stage(nc, "rp") as st:
        w_raw = st.sbuf("w_raw", [P, 2, ND, P])
        w_hi = st.sbuf("w_hi", [P, 2, ND, P], F32R)
        w_lo = st.sbuf("w_lo", [P, 2, ND, P], F32R)
        gate = st.sbuf("gate", [P, 2])
        wa2 = st.sbuf("wa2", [P, RWKV_W])
        g2_sb = st.sbuf("g2", [P, RWKV_W])
        col = st.sbuf("col", [P, M_COLS])
        one_less_ka = st.sbuf("one_less_ka", [P, 4])
        head_ones = st.sbuf("head_ones", [P, P])
        eps = st.sbuf("eps", [P, 1])
        reset = st.sbuf("reset", [P, NT, P])
        sig = st.sbuf("sig", [P, 4, SEQ])
        rate = st.sbuf("rate", [P, 4, SEQ])
        kr_x, r_x, v_x = (st.sbuf(n, [P, 4 + SEQ]) for n in ("kr_x", "r_x", "v_x"))
        k = st.sbuf("k", [P, SEQ])
        kk = st.sbuf("kk", [P, SEQ])
        r = st.sbuf("r", [P, SEQ])
        sq = st.sbuf("sq", [P, SEQ])
        cs = st.sbuf("cs", [P, NT, P])
        cm = st.sbuf("cm", [P, NT, P])
        before = st.sbuf("before", [P, NT, P])
        grow = st.sbuf("grow", [P, NT, P])
        shrink = st.sbuf("shrink", [P, NT, P])
        out = st.sbuf("out", [P, NT, R_SLOTS, P])
        bonus = st.sbuf("bonus", [P, SEQ])
        ends = st.sbuf("ends", [P, NT])
        proj = st.psum("proj", [P, 2, 2, HALF])
        sums = st.psum("sums", [P, 4, HALF])

        setup, ready, setup_v, lora_g = st.sem("setup"), st.sem("ready"), st.sem("setup_v"), st.sem("lora_g")
        w_loaded = [st.sem(f"w_loaded{u}") for u in range(2)]
        w_rounded, w_split, projected, copied = st.sem("w_rounded"), st.sem("w_split"), st.sem("projected"), st.sem("copied")
        lora_in, lora_summed, lora_read = st.sem("lora_in"), st.sem("lora_summed"), st.sem("lora_read")
        gate_ready, gate_stored = st.sem("gate_ready"), st.sem("gate_stored")
        out_stored, bonus_stored = st.sem("out_stored"), st.sem("bonus_stored")
        dve_steps = Steps(st.sem("dve_steps"), "kr_diff kr kk_raw cs cm before k_factor k r_diff r rk kk "
                          "kk_out r_out k_out b_pre b_out v_diff v_out bonus ends ends_next")
        act_steps = Steps(st.sem("act_steps"), "kr_copied kk_squared r_copied shrink grow before log_norm norm v_copied carry")
        pe_steps = Steps(st.sem("pe_steps"), "norm_summed bonus_summed")
        block = st.stack.enter_context(nc.Block())
        w_cols = w_in.rearrange("(d p) f -> p d f", p=P)
        tiles = scratch.rearrange("c p w -> p c w")
        BLOCKS = 14
        kr_lora, g_lora = k, kk

        @block.sync
        def _(sp):
            sp.nop().then_inc(out_stored, 16)
            sp.nop().then_inc(bonus_stored, 16)
            sp.nop().then_inc(gate_stored, 16)
            sp.dma_start(col[:], params).then_inc(setup, 16)
            sp.dma_start(wa2[0:64], w2).then_inc(setup, 16)
            sp.dma_start(wa2[64:128], a2).then_inc(setup, 16)
            sp.dma_start(g2_sb[:], g2).then_inc(setup, 16)
            sp.dma_start(head_ones[:], masks[:, 4]).then_inc(setup, 16)

            def load(kk_, s, start):
                if not (isinstance(kk_, int) and kk_ < 2):
                    sp.wait_ge(w_split, kk_ - 1)
                sp.dma_start(w_raw[:, s], w_cols[:, :, bass.ds(start, P)]).then_inc(w_loaded[s], 16)

            load(0, 0, RWKV_COLS + LORA_WA * P)
            load(1, 1, RWKV_COLS + LORA_G * P)
            load(2, 0, RWKV_COLS + RWKV_W)
            load(3, 1, RWKV_COLS)
            for b in range(4):
                sp.wait_ge(gate_ready, b + 1)
                sp.dma_start(gate_out[b], sq[:]).then_inc(gate_stored, 16)

            def store(b):
                dve_steps.wait(sp, "v_out", b)
                sp.dma_start(tiles[:, :, bass.ds((S_RWKV + R_SLOTS * b) * P, R_SLOTS * P)],
                             out[:].rearrange("p c s t -> p c (s t)")).then_inc(out_stored, 16)
                dve_steps.wait(sp, "bonus", b)
                sp.dma_start(bonus_out[bass.ds(b, 1)].rearrange("a p t -> p (a t)"), bonus[:]).then_inc(bonus_stored, 16)

            for b in range(4):
                n = 3 * b + 4
                load(n, n % 2, RWKV_COLS + 2 * RWKV_W + b * P)
                if b < 3:
                    load(n + 1, (n + 1) % 2, RWKV_COLS + RWKV_W + (b + 1) * P)
                    load(n + 2, n % 2, RWKV_COLS + (b + 1) * P)
                store(b)
            sp.wait_ge(out_stored, 16 * 5)
            sp.wait_ge(bonus_stored, 16 * 5)
            sp.wait_ge(gate_stored, 16 * 5)

        @block.gpsimd
        def _(pool):
            stream_weights(nc, pool, gate[:], w_raw, w_hi, w_lo, w_loaded, w_rounded, w_split, projected, BLOCKS, False)

        @block.tensor
        def _(pe):
            pe_steps.open(pe)

            def project(n, s):
                pe.wait_ge(w_split, n + 1)
                if not (isinstance(n, int) and n < 2):
                    pe.wait_ge(copied, n)
                for t in range(NH):
                    for d in range(ND):
                        last = split_matmul(nc, proj[:, s, t], (w_hi[:, s, d], w_lo[:, s, d]),
                                            tuple(part[:, d, t * HALF:(t + 1) * HALF] for part in h), d == 0, d == ND - 1)
                last.then_inc(projected, 1)

            project(0, 0)
            project(1, 1)
            pe.wait_ge(setup, 16 * 5)
            for b in range(4):
                cols = slice(b * P, (b + 1) * P)
                pe.wait_ge(lora_in, 2)
                if b:
                    pe.wait_ge(lora_read, 3 * b)
                for t in range(NH):
                    tok = slice(t * HALF, (t + 1) * HALF)
                    nc.tensor.matmul(sums[:, t], wa2[0:64, cols], kr_lora[0:64, tok], start=True, stop=True)
                    last = nc.tensor.matmul(sums[:, 2 + t], wa2[64:128, cols], kr_lora[64:128, tok], start=True, stop=True)
                last.then_inc(lora_summed, 1)
                pe.wait_ge(lora_in, 3)
                pe.wait_ge(lora_read, 3 * b + 1)
                for t in range(NH):
                    last = nc.tensor.matmul(sums[:, t], g2_sb[:, cols], g_lora[:, t * HALF:(t + 1) * HALF], start=True, stop=True)
                last.then_inc(lora_summed, 1)

            def over_heads(what, bank):
                for t in range(NH):
                    last = nc.tensor.matmul(sums[:, bank + t], head_ones[:], sq[:, t * HALF:(t + 1) * HALF], start=True, stop=True)
                pe_steps.done(last, what)

            def heads(b, s, n):
                project(n, s)
                project(n + 1, 1 - s)
                act_steps.wait(pe, "kk_squared", b)
                act_steps.wait(pe, "log_norm", b - 1)
                over_heads("norm_summed", 0)
                project(n + 2, s)
                dve_steps.wait(pe, "rk", b)
                dve_steps.wait(pe, "bonus", b - 1)
                over_heads("bonus_summed", 2)

            with pe.Fori(0, 2) as i:
                heads(2 * i, 0, 6 * i + 2)
                heads(2 * i + 1, 1, 6 * i + 5)

        @block.scalar
        def _(act):
            act_steps.open(act)
            act.wait_ge(setup, 16 * 5)
            act.wait_ge(ready, 1)

            def copy_block(n, to, s):
                act.wait_ge(projected, n + 1)
                return nc.scalar.copy(to[:, 4:], proj[:, s].rearrange("p n t -> p (n t)"))

            copy_block(0, kr_x, 0).then_inc(copied, 1)
            copy_block(1, r_x, 1).then_inc(copied, 1)
            act.wait_ge(lora_in, 1)
            nc.scalar.activation(kr_lora[0:64], k[0:64], ACT.Tanh).then_inc(lora_in, 1)
            act.wait_ge(lora_in, 2)
            act.wait_ge(lora_g, 1)
            nc.scalar.activation(g_lora[:], kk[:], ACT.Sigmoid).then_inc(lora_in, 1)
            for b in range(4):
                act.wait_ge(lora_summed, 2 * b + 1)
                nc.scalar.activation(sig[:, b], sums[:, 0:2].rearrange("p n t -> p (n t)"), ACT.Sigmoid, bias=col[:, M_W0 + b:M_W0 + b + 1]).then_inc(lora_read, 1)
                nc.scalar.activation(rate[:, b], sums[:, 2:4].rearrange("p n t -> p (n t)"), ACT.Sigmoid, bias=col[:, M_A0 + b:M_A0 + b + 1]).then_inc(lora_read, 1)
                act.wait_ge(lora_summed, 2 * b + 2)
                act.wait_ge(gate_stored, 16 * (b + 1))
                nc.scalar.copy(sq[:], sums[:, 0:2].rearrange("p n t -> p (n t)")).then_inc(lora_read, 1)
                act.wait_ge(lora_read, 3 * b + 3)
                nc.scalar.nop().then_inc(gate_ready, 1)
            act.wait_ge(gate_stored, 16 * 5)

            def heads(b, s, n):
                dve_steps.wait(act, "kr", b - 1)
                ins = copy_block(n, kr_x, s)
                act_steps.done(ins, "kr_copied")
                act_steps.wait(act, "kr_copied", b)
                nc.scalar.nop().then_inc(copied, 1)
                dve_steps.wait(act, "kk_raw", b)
                pe_steps.wait(act, "bonus_summed", b - 1)
                act_steps.done(nc.scalar.activation(sq[:], kk[:], ACT.Square), "kk_squared")
                dve_steps.wait(act, "r", b - 1)
                ins = copy_block(n + 1, r_x, 1 - s)
                act_steps.done(ins, "r_copied")
                act_steps.wait(act, "r_copied", b)
                nc.scalar.nop().then_inc(copied, 1)
                dve_steps.wait(act, "cm", b)
                act_steps.done(nc.scalar.activation(shrink[:], cm[:], ACT.Exp, scale=-EXP_HALF), "shrink")
                act_steps.done(nc.scalar.activation(grow[:], cm[:], ACT.Exp, scale=EXP_HALF), "grow")
                dve_steps.wait(act, "before", b)
                act_steps.done(nc.scalar.activation(before[:], before[:], ACT.Exp, scale=-EXP_HALF), "before")
                pe_steps.wait(act, "norm_summed", b)
                act.wait_ge(bonus_stored, 16 * (b + 1))
                act_steps.done(nc.scalar.activation(bonus[:], sums[:, 0:2].rearrange("p n t -> p (n t)"), ACT.Ln, bias=eps[:]), "log_norm")
                act_steps.wait(act, "log_norm", b)
                act_steps.done(nc.scalar.activation(bonus[:], bonus[:], ACT.Exp, scale=-0.5), "norm")
                dve_steps.wait(act, "v_out", b - 1)
                ins = copy_block(n + 2, v_x, s)
                act_steps.done(ins, "v_copied")
                act_steps.wait(act, "v_copied", b)
                nc.scalar.nop().then_inc(copied, 1)
                dve_steps.wait(act, "ends_next", b)
                act_steps.done(nc.scalar.activation(carry[:, :, bass.ds(b, 1)].rearrange("p c a -> p (c a)"), ends[:], ACT.Exp, scale=-EXP_HALF), "carry")

            with act.Fori(0, 2) as i:
                heads(2 * i, 0, 6 * i + 2)
                heads(2 * i + 1, 1, 6 * i + 5)

        @block.vector
        def _(dve):
            dve_steps.open(dve)
            nc.vector.nop().then_inc(copied, 1)
            nc.vector.memset(eps[:], L2_EPS)
            nc.vector.memset(reset[:], 1.0).then_inc(setup_v, 1)
            dve.wait_ge(setup_v, 1)
            nc.vector.memset(reset[:, :, 0:1], 0.0).then_inc(setup_v, 1)
            dve.wait_ge(setup, 16 * 5)
            nc.vector.tensor_scalar(one_less_ka[:], col[:, M_KA:M_KA + 4], -1.0, 1.0, ALU.mult, ALU.add).then_inc(setup_v, 1)
            for x in (r_x, v_x, kr_x):
                last = nc.vector.memset(x[:, 0:4], 0.0)
            last.then_inc(ready, 1)
            dve.wait_ge(setup_v, 3)
            dve.wait_ge(ready, 1)

            def mu(blk):
                return col[:, bass.ds(M_MU + blk, 1)]

            def shift(x, blk, diff, to, name_diff, name, b):
                ins = nc.vector.tensor_tensor(diff, x[:, 3:3 + SEQ], x[:, 4:], ALU.subtract)
                dve_steps.done(ins, name_diff)
                dve_steps.wait(dve, name_diff, b)
                dve_steps.done(nc.vector.scalar_tensor_tensor(to, diff, mu(blk), x[:, 4:], ALU.mult, ALU.add), name)

            for n, (x, to, sem) in enumerate(((kr_x, k, lora_in), (r_x, kk, lora_g))):
                dve.wait_ge(copied, n + 2)
                nc.vector.tensor_tensor(to[:], x[:, 3:3 + SEQ], x[:, 4:], ALU.subtract).then_inc(setup_v, 1)
                dve.wait_ge(setup_v, 4 + n)
                nc.vector.scalar_tensor_tensor(to[:], to[:], mu(LORA_WA + n), x[:, 4:], ALU.mult, ALU.add).then_inc(sem, 1)
            dve.wait_ge(lora_read, 12)
            dve.wait_ge(gate_stored, 16 * 5)

            def heads(b):
                one = lambda base: col[:, bass.ds(base + b, 1)]
                flat = lambda x: x[:].rearrange("p c t -> p (c t)")
                at_head = lambda x: x[:, bass.ds(b, 1)].rearrange("p a t -> p (a t)")
                slot = lambda j: out[:, :, j]
                act_steps.wait(dve, "kr_copied", b)
                shift(kr_x, b + 4, k[:], k[:], "kr_diff", "kr", b)
                dve_steps.wait(dve, "kr", b)
                dve_steps.done(nc.vector.tensor_scalar(kk[:], k[:], one(M_KK), None, ALU.mult), "kk_raw")
                dve_steps.done(nc.vector.tensor_tensor_scan(flat(cs), flat(reset), at_head(sig), 0.0, ALU.mult, ALU.add), "cs")
                dve_steps.wait(dve, "cs", b)
                dve_steps.done(nc.vector.tensor_tensor(cm[:], cs[:], cs[:, :, P // 2 - 1:P // 2].broadcast_to([P, NT, P]), ALU.subtract), "cm")
                dve_steps.wait(dve, "cm", b)
                dve_steps.done(nc.vector.tensor_tensor(flat(before), flat(cm), at_head(sig), ALU.subtract), "before")
                dve_steps.done(nc.vector.tensor_scalar(r[:], at_head(rate), one(M_KA), one_less_ka[:, bass.ds(b, 1)], ALU.mult, ALU.add), "k_factor")
                dve_steps.wait(dve, "k_factor", b)
                dve_steps.done(nc.vector.tensor_tensor(k[:], k[:], r[:], ALU.mult), "k")
                act_steps.wait(dve, "r_copied", b)
                dve_steps.wait(dve, "k", b)
                shift(r_x, b, r[:], r[:], "r_diff", "r", b)
                dve_steps.wait(dve, "r", b)
                pe_steps.wait(dve, "norm_summed", b)
                dve_steps.done(nc.vector.scalar_tensor_tensor(sq[:], r[:], one(M_RK), k[:], ALU.mult, ALU.mult), "rk")
                act_steps.wait(dve, "norm", b)
                dve_steps.done(nc.vector.tensor_tensor(kk[:], kk[:], bonus[:], ALU.mult), "kk")
                dve_steps.wait(dve, "kk", b)
                dve.wait_ge(out_stored, 16 * (b + 1))
                by_tile = lambda x: x[:].rearrange("p (c t) -> p c t", t=P)
                dve_steps.done(nc.vector.tensor_tensor(slot(R_KK), by_tile(kk), before[:], ALU.mult), "kk_out")
                dve_steps.done(nc.vector.tensor_tensor(slot(R_R), by_tile(r), shrink[:], ALU.mult), "r_out")
                dve_steps.done(nc.vector.tensor_tensor(slot(R_K), by_tile(k), grow[:], ALU.mult), "k_out")
                dve_steps.done(nc.vector.scalar_tensor_tensor(kk[:], kk[:], -1.0, at_head(rate), ALU.mult, ALU.mult), "b_pre")
                dve_steps.wait(dve, "b_pre", b)
                dve_steps.done(nc.vector.tensor_tensor(slot(R_B), by_tile(kk), grow[:], ALU.mult), "b_out")
                act_steps.wait(dve, "v_copied", b)
                dve_steps.done(nc.vector.tensor_tensor(cm[:], v_x[:, 3:3 + SEQ].rearrange("p (c t) -> p c t", t=P),
                                                       v_x[:, 4:].rearrange("p (c t) -> p c t", t=P), ALU.subtract), "v_diff")
                dve_steps.wait(dve, "v_diff", b)
                dve_steps.done(nc.vector.scalar_tensor_tensor(slot(R_V), cm[:], mu(b + 8), v_x[:, 4:].rearrange("p (c t) -> p c t", t=P),
                                                              ALU.mult, ALU.add), "v_out")
                pe_steps.wait(dve, "bonus_summed", b)
                dve_steps.wait(dve, "v_out", b)
                dve.wait_ge(bonus_stored, 16 * (b + 1))
                dve_steps.done(nc.vector.tensor_tensor(by_tile(bonus), slot(R_V), sums[:, 2:4].rearrange("p n (c t) -> p (n c) t", t=P), ALU.mult), "bonus")
                dve_steps.done(nc.vector.tensor_tensor(ends[:], cs[:, :, P - 1], cs[:, :, P // 2 - 1], ALU.subtract), "ends")
                dve_steps.wait(dve, "ends", b)
                dve_steps.done(nc.vector.tensor_tensor(ends[:, 0:NT - 1], ends[:, 0:NT - 1], cs[:, 1:NT, P // 2 - 1], ALU.add), "ends_next")

            with dve.Fori(0, 4) as b:
                heads(b)


LEVELS = (2, 4, 8, 16, 32, 64)
HEADS = 4
MASKS = 5 + 7


def recurrences(nc, masks, scratch, carry, merged):
    with Stage(nc, "rc") as st:
        CH = "GAB"
        mask = st.sbuf("mask", [P, MASKS, P])
        tile = st.sbuf("tile", [P, 2, TILE_W])
        att = {ch: st.sbuf(f"att_{ch}", [P, 2 if ch == "G" else 4, HEADS, P]) for ch in CH}
        level = {ch: st.sbuf(f"level_{ch}", [P, 2, HEADS, P]) for ch in CH}
        T = {ch: st.sbuf(f"T_{ch}", [P, HEADS, P]) for ch in CH}
        TT = {ch: st.sbuf(f"TT_{ch}", [P, HEADS, P]) for ch in CH}
        X = {ch: st.sbuf(f"X_{ch}", [P, HEADS, P]) for ch in CH}
        tok = {ch: st.sbuf(f"tok_{ch}", [P, 8 if ch == "G" else 6, P]) for ch in CH}
        new = {ch: st.sbuf(f"new_{ch}", [P, HEADS if ch == "G" else 2, P]) for ch in CH}
        delta = {ch: st.sbuf(f"delta_{ch}", [P, HEADS if ch == "G" else 2, P]) for ch in CH}
        state = {ch: st.sbuf(f"state_{ch}", [P, HEADS if ch == "G" else 2, P]) for ch in CH}
        headed = {ch: st.sbuf(f"headed_{ch}", [P, 2, 2, 2, P]) for ch in "AB"}
        gate = st.sbuf("gate", [P, 2])
        ps = st.psum("ps", [P, 8, HALF])
        bank = {"G": 6, "A": 0, "B": 2}
        first_bank = {"G": 4, "A": 0, "B": 2}
        token_bank = {"A": 0, "B": 4}
        NT_, OUT_NEW, IN_V, OUT_V = 0, 1, 2, 3

        levels = [f"{ch}_{{}}{b}" for b in LEVELS for ch in CH]
        setup, ready = st.sem("setup"), st.sem("ready")
        heads_apart = st.sem("heads_apart")
        loaded = [st.sem(f"loaded{u}") for u in range(2)]

        def level_names(kinds):
            return " ".join(f"{ch}_{k}{b}" for b in LEVELS for ch in CH for k in kinds if not (b == 64 and k == "t"))

        grown = [("products", "G", 0), ("tokens", "G", 0), ("products", "A", 0), ("early", "B", 0), ("x", "G", 2),
                 ("products", "B", 0), ("tokens", "A", 0), ("xt", "G", 2), ("x", "A", 2), ("tokens", "B", 0), ("x", "B", 2), ("xt", "A", 2)]
        for before, b in zip(LEVELS, LEVELS[1:]):
            grown += [("x", "G", b), ("xt", "B", before), ("x", "A", b), ("xt", "G", b), ("x", "B", b), ("xt", "A", b)]
        grown += [("xt", "B", LEVELS[-1])]
        pe_steps = Steps(st.sem("pe_steps"), " ".join((f"{ch}_tx{b} " if (kind, b) == ("xt", 32) else "") + f"{ch}_{kind}{b or ''}"
                                                      for kind, ch, b in grown)
                         + " G_ks A_x B_x G_v A_p B_p G_s A_d B_d G_o A_y B_y")
        act_steps = Steps(st.sem("act_steps"), level_names(("xc",)).replace("A_xc2", "A_tokens A_tokens2 A_xc2").replace("B_xc2", "B_tokens B_tokens2 B_xc2")
                          + " A_x B_x G_v G_o A_y A_y2 B_y B_y2")
        dve_steps = Steps(st.sem("dve_steps"), "G_n G_att G_kd G_vb G_t1 A_n A_att2 A_att3 A_att A_t1 B_n B_att2 B_att3 B_att B_t1 "
                          + level_names(("tt", "t"))
                          + " G_xb G_x A_p1 A_p B_p1 B_p G_sg A_d B_d G_s A_m A_s0 A_s B_m B_s0 B_s")
        pool_steps = Steps(st.sem("pool_steps"), "G_m1 G_tt G_m2 A_m1 A_tt A_m2 B_m1 B_tt B_m2 "
                           + level_names(("m",)).replace("G_m2 A_m2 B_m2 ", ""))
        block = st.stack.enter_context(nc.Block())

        def slot(u, n, count=1):
            return tile[:, u, n * P:(n + count) * P]

        def slots(u, n, count, step=1):
            v = tile[:, u, 0:SLOTS * P].rearrange("p (s t) -> p s t", t=P)
            return v[:, n:n + step * (count - 1) + 1:step]

        def rwkv(ch, pair, j):
            return S_RWKV + R_SLOTS * (2 * "AB".index(ch) + pair) + j

        def columns(u, n):
            return tile[:, u, C_GDN + 4 * n:C_GDN + 4 * n + 4].rearrange("p (n a) -> p n a", a=1).broadcast_to([P, HEADS, P])

        def over_heads(n):
            return mask[:, n:n + 1].broadcast_to([P, HEADS, P])

        def banks(n, count=1):
            return ps[:, n:n + count].rearrange("p b w -> p (b w)").rearrange("p (n t) -> p n t", t=P)

        def chosen(n):
            return mask[:, n:n + 1].bitcast(U32).broadcast_to([P, HEADS, P])

        @block.sync
        def _(sp):
            sp.dma_start(mask[:], masks).then_inc(setup, 16)
            for u in range(2):
                sp.dma_start(tile[:, u], scratch[u]).then_inc(loaded[u], 16)
            with sp.Fori(0, NT // 2 - 1) as i:
                for u in range(2):
                    pe_steps.wait(sp, "B_y", 2 * i + u)
                    dve_steps.wait(sp, "B_s", 2 * i + u)
                    sp.dma_start(tile[:, u], scratch[bass.ds(2 * i + u + 2, 1)].rearrange("a p w -> p (a w)")).then_inc(loaded[u], 16)

        @block.tensor
        def _(pe):
            pe_steps.open(pe)
            mm = nc.tensor.matmul
            pe.wait_ge(setup, 16)
            pe.wait_ge(ready, 1)

            def turn(out, sources):
                for n, src in enumerate(sources):
                    last = nc.tensor.transpose(out[:, n], src, mask[:, 0])
                return last

            def products(ch, u, name, heads):
                for n in heads:
                    if ch == "G":
                        last = mm(ps[:, first_bank[ch] + n // 2, n % 2 * 2 * P:(n % 2 + 1) * 2 * P], slot(u, S_K + 2 * n),
                                  slots(u, 2 * n, 2, S_K + 1), start=True, stop=True)
                    else:
                        for j, kind in enumerate((R_B, R_K)):
                            last = mm(ps[:, first_bank[ch] + n, 2 * j * P:2 * (j + 1) * P], slot(u, rwkv(ch, n // 2, kind)),
                                      headed[ch][:, n % 2, n // 2].rearrange("p k t -> p (k t)"), start=True, stop=True)
                pe_steps.done(last, name)

            def tile_of(c, u, i):
                pe.wait_ge(loaded[u], 16 * (i + 1))
                for kind, ch, b in grown:
                    if kind == "products" and ch == "G":
                        products("G", u, "G_products", range(HEADS))
                    elif kind == "products" and ch == "A":
                        pe.wait_ge(heads_apart, 4 * c + 2)
                        act_steps.wait(pe, "B_y2", c - 1)
                        dve_steps.wait(pe, "B_d", c - 1)
                        products("A", u, "A_products", range(HEADS))
                    elif kind == "early":
                        pe.wait_ge(heads_apart, 4 * c + 4)
                        dve_steps.wait(pe, "G_att", c)
                        products("B", u, "B_early", (2, 3))
                    elif kind == "products":
                        dve_steps.wait(pe, "A_att", c)
                        products("B", u, "B_products", (0, 1))
                    elif kind == "tokens" and ch == "G":
                        act_steps.wait(pe, "G_o", c - 1)
                        dve_steps.wait(pe, "G_s", c - 1)
                        turn(banks(bank["G"]), [slot(u, S_K + 2 * n) for n in range(HEADS)])
                        pe_steps.done(turn(banks(bank["G"] + 1), [slot(u, S_V + n) for n in range(HEADS)]), "G_tokens")
                    elif kind == "tokens":
                        dve_steps.wait(pe, f"{ch}_att", c)
                        srcs = [slot(u, rwkv(ch, pair, j)) for j in (R_V, R_K, R_B) for pair in range(2)]
                        turn(banks(token_bank[ch]), srcs[0:4])
                        pe_steps.done(turn(banks(token_bank[ch] + 1), srcs[4:6]), f"{ch}_tokens")
                    elif kind == "x":
                        pool_steps.wait(pe, f"{ch}_m{b}", c)
                        if b == LEVELS[0]:
                            if ch == "A":
                                act_steps.wait(pe, "A_tokens2", c)
                            else:
                                dve_steps.wait(pe, f"{ch}_{'vb' if ch == 'G' else 'att'}", c)
                        dve_steps.wait(pe, f"{ch}_t{b // 2}", c)
                        for n in range(HEADS):
                            last = mm(banks(bank[ch])[:, n], level[ch][:, LEVELS.index(b) % 2, n], T[ch][:, n], start=True, stop=True)
                    else:
                        act_steps.wait(pe, f"{ch}_xc{b}", c)
                        if b == 32:
                            for n in range(HEADS):
                                last = mm(banks(bank[ch])[:, n], TT[ch][:, n], X[ch][:, n], start=True, stop=True)
                            pe_steps.done(last, f"{ch}_tx{b}")
                        for n in range(HEADS):
                            last = mm(banks(bank[ch] + 1)[:, n], X[ch][:, n], TT[ch][:, n], start=True, stop=True)
                    if kind in ("x", "xt"):
                        pe_steps.done(last, f"{ch}_{kind}{b}")

                dve_steps.wait(pe, "G_s", c - 1)
                for n in range(HEADS):
                    last = mm(banks(bank["G"])[:, n], slot(u, S_K + 2 * n), state["G"][:, n], start=True, stop=True)
                pe_steps.done(last, "G_ks")
                for ch in "AB":
                    dve_steps.wait(pe, f"{ch}_s", c - 1)
                    for n in range(HEADS):
                        o = banks(bank[ch])[:, n]
                        mm(o, slot(u, rwkv(ch, n // 2, R_KK)), state[ch][:, n // 2], start=True, stop=False)
                        last = mm(o, att[ch][:, IN_V, n], tok[ch][:, n // 2], start=False, stop=True)
                    pe_steps.done(last, f"{ch}_x")
                for ch, name in (("G", "G_v"), ("A", "A_p"), ("B", "B_p")):
                    dve_steps.wait(pe, f"{ch}_tt64", c)
                    if ch == "G":
                        dve_steps.wait(pe, "G_x", c)
                    else:
                        act_steps.wait(pe, f"{ch}_x", c)
                    for n in range(HEADS):
                        last = mm(banks(bank[ch] + 1)[:, n], TT[ch][:, n], X[ch][:, n], start=True, stop=True)
                    pe_steps.done(last, name)
                act_steps.wait(pe, "G_v", c)
                for n in range(HEADS):
                    last = mm(banks(bank["G"] + 1)[:, n], tok["G"][:, n], new["G"][:, n], start=True, stop=True)
                pe_steps.done(last, "G_s")
                for ch in "AB":
                    dve_steps.wait(pe, f"{ch}_p", c)
                    for pair in range(2):
                        o = banks(bank[ch])[:, pair]
                        mm(o, tok[ch][:, 2 + pair], tok[ch][:, pair], start=True, stop=False)
                        last = mm(o, tok[ch][:, 4 + pair], new[ch][:, pair], start=False, stop=True)
                    pe_steps.done(last, f"{ch}_d")
                for n in range(HEADS):
                    mm(banks(bank["G"])[:, n], state["G"][:, n], slot(u, S_Q + 2 * n + 1), start=True, stop=False)
                    last = mm(banks(bank["G"])[:, n], new["G"][:, n], att["G"][:, OUT_NEW, n], start=False, stop=True)
                pe_steps.done(last, "G_o")
                for ch in "AB":
                    for n in range(HEADS):
                        o = banks(bank[ch] + 1)[:, n]
                        mm(o, state[ch][:, n // 2], slot(u, rwkv(ch, n // 2, R_R)), start=True, stop=False)
                        mm(o, tok[ch][:, n // 2], att[ch][:, OUT_V, n], start=False, stop=False)
                        last = mm(o, new[ch][:, n // 2], att[ch][:, OUT_NEW, n], start=False, stop=True)
                    pe_steps.done(last, f"{ch}_y")

            with pe.Fori(0, NT // 2) as i:
                for u in range(2):
                    tile_of(2 * i + u, u, i)

        @block.scalar
        def _(act):
            act_steps.open(act)

            def copy(name, out, src):
                act_steps.done(nc.scalar.copy(out, src), name)

            def part_heads(u, loads):
                act.wait_ge(loaded[u], 16 * loads)
                for ch in "AB":
                    first = rwkv(ch, 0, R_KK)
                    of_pairs = tile[:, u, first * P:(first + 2 * R_SLOTS) * P].rearrange("p (a s t) -> p a s t", a=2, t=P)[:, :, 0:2]
                    for e in range(2):
                        rows = slice(64 * e, 64 * e + 64)
                        nc.scalar.copy(headed[ch][rows, e], of_pairs[rows]).then_inc(heads_apart, 1)

            def tile_of(c, u, i, last):
                def tokens(ch):
                    pe_steps.wait(act, f"{ch}_tokens", c)
                    copy(f"{ch}_tokens", tok[ch][:, 0:4], banks(token_bank[ch]))
                    copy(f"{ch}_tokens2", tok[ch][:, 4:6], banks(token_bank[ch] + 1)[:, 0:2])

                for b in LEVELS:
                    for ch in CH:
                        if b == LEVELS[0] and ch != "G":
                            tokens(ch)
                        pe_steps.wait(act, f"{ch}_x{b}", c)
                        copy(f"{ch}_xc{b}", X[ch][:], banks(bank[ch]))
                for ch in "AB":
                    pe_steps.wait(act, f"{ch}_x", c)
                    copy(f"{ch}_x", X[ch][:], banks(bank[ch]))
                pe_steps.wait(act, "G_v", c)
                copy("G_v", new["G"][:], banks(bank["G"] + 1))
                if not last:
                    part_heads(1 - u, i + 1 + u)
                pe_steps.wait(act, "G_o", c)
                copy("G_o", merged[:, 0:4, bass.ds(c * P, P)], banks(bank["G"]))
                for ch in "AB":
                    pe_steps.wait(act, f"{ch}_y", c)
                    first = 4 + 2 * "AB".index(ch)
                    for e, name in enumerate((f"{ch}_y", f"{ch}_y2")):
                        rows = slice(64 * e, 64 * e + 64)
                        copy(name, merged[rows, first:first + 2, bass.ds(c * P, P)],
                             banks(bank[ch] + 1)[rows, e:e + 3:2])

            act.wait_ge(ready, 1)
            part_heads(0, 1)
            with act.Fori(0, NT // 2 - 1) as i:
                for u in range(2):
                    tile_of(2 * i + u, u, i, False)
            for u in range(2):
                tile_of(NT - 2 + u, u, NT // 2 - 1, u == 1)

        @block.gpsimd
        def _(pool):
            pool_steps.open(pool)
            pool.wait_ge(setup, 16)
            tt = nc.gpsimd.tensor_tensor

            def coupled(ch, k, c):
                if k >= 2:
                    pe_steps.wait(pool, f"{ch}_x{LEVELS[k - 2]}", c)
                pool_steps.done(tt(level[ch][:, k % 2], att[ch][:, NT_], over_heads(6 + k), ALU.mult), f"{ch}_m{LEVELS[k]}")

            def tile_of(c):
                for ch in CH:
                    dve_steps.wait(pool, f"{ch}_n", c)
                    pe_steps.wait(pool, f"{ch}_p" if ch != "G" else "G_v", c - 1)
                    pool_steps.done(tt(X[ch][:], att[ch][:, NT_], over_heads(5), ALU.mult), f"{ch}_m1")
                    pool_steps.wait(pool, f"{ch}_m1", c)
                    pool_steps.done(tt(TT[ch][:], X[ch][:], over_heads(0), ALU.add), f"{ch}_tt")
                    coupled(ch, 0, c)
                for k in range(1, len(LEVELS)):
                    for ch in CH:
                        coupled(ch, k, c)

            with pool.Fori(0, NT // 2) as i:
                for u in range(2):
                    tile_of(2 * i + u)

        @block.vector
        def _(dve):
            dve_steps.open(dve)
            for ch in CH:
                nc.vector.memset(state[ch][:], 0.0)
                nc.vector.memset(att[ch][:], 0.0)
                if ch != "G":
                    nc.vector.memset(headed[ch][:], 0.0)
            nc.vector.memset(gate[:], 0.0).then_inc(ready, 1)
            dve.wait_ge(setup, 16)
            dve.wait_ge(ready, 1)
            tt = nc.vector.tensor_tensor

            def masked(ch, c):
                pe_steps.wait(dve, f"{ch}_products", c)
                pe_steps.wait(dve, f"{ch}_y", c - 1)
                pool_steps.wait(dve, f"{ch}_m64", c - 1)
                nc.vector.tensor_copy(gate[:, 0:1], gate[:, 1:2])
                for name, j, kind, which in ((f"{ch}_n", 0, NT_, 3), (f"{ch}_att2", 1, OUT_NEW, 2),
                                             (f"{ch}_att3", 2, IN_V, 3), (f"{ch}_att", 3, OUT_V, 2)):
                    dve_steps.done(nc.vector.copy_predicated(att[ch][:, kind], chosen(which), ps[:, first_bank[ch]:first_bank[ch] + 4, j * P:(j + 1) * P]), name)

            def tile_of(c, u, i):
                both = ps[:, first_bank["G"]:first_bank["G"] + 2].rearrange("p b w -> p (b w)").rearrange("p (n k t) -> p n k t", k=2, t=P)
                dve.wait_ge(loaded[u], 16 * (i + 1))
                pe_steps.wait(dve, "G_products", c)
                pool_steps.wait(dve, "G_m64", c - 1)
                dve_steps.done(tt(att["G"][:, NT_], both[:, :, 1], slots(u, S_STRICT, 4), ALU.mult), "G_n")
                dve_steps.done(tt(att["G"][:, OUT_NEW], both[:, :, 0], slots(u, S_INCL, 4), ALU.mult), "G_att")
                pe_steps.wait(dve, "G_tokens", c)
                dve_steps.done(tt(tok["G"][:, 0:4], banks(bank["G"]), columns(u, 2), ALU.mult), "G_kd")
                dve_steps.done(tt(tok["G"][:, 4:8], banks(bank["G"] + 1), columns(u, 0), ALU.mult), "G_vb")

                def transposed(ch, name):
                    dve_steps.done(nc.vector.transpose(T[ch].rearrange("p n t -> p (n t)"), TT[ch].rearrange("p n t -> p (n t)")), name)

                for ch in CH:
                    if ch != "G":
                        masked(ch, c)
                    pool_steps.wait(dve, f"{ch}_tt", c)
                    transposed(ch, f"{ch}_t1")
                for b in LEVELS:
                    for ch in CH:
                        pe_steps.wait(dve, f"{ch}_xt{b}", c)
                        dve_steps.done(tt(TT[ch][:], TT[ch][:], banks(bank[ch] + 1), ALU.add), f"{ch}_tt{b}")
                        if b < 32:
                            dve_steps.wait(dve, f"{ch}_tt{b}", c)
                            transposed(ch, f"{ch}_t{b}")
                        elif b == 32:
                            dve_steps.done(tt(T[ch][:], T[ch][:], banks(bank[ch]), ALU.add), f"{ch}_t{b}")
                pe_steps.wait(dve, "G_ks", c)
                dve_steps.done(tt(delta["G"][:], banks(bank["G"]), columns(u, 1), ALU.mult), "G_xb")
                dve_steps.wait(dve, "G_xb", c)
                dve_steps.done(tt(X["G"][:], delta["G"][:], tok["G"][:, 4:8], ALU.add), "G_x")
                for ch in "AB":
                    pe_steps.wait(dve, f"{ch}_p", c)
                    for e, name in enumerate((f"{ch}_p1", f"{ch}_p")):
                        half = slice(64 * e, 64 * e + 64)
                        dve_steps.done(nc.vector.tensor_copy(new[ch][:, :, half], banks(bank[ch] + 1)[:, e:e + 3:2, half]), name)
                pe_steps.wait(dve, "G_s", c)
                dve_steps.done(tt(delta["G"][:], state["G"][:], columns(u, 3), ALU.mult), "G_sg")
                for ch in "AB":
                    pe_steps.wait(dve, f"{ch}_d", c)
                    dve_steps.done(tt(delta[ch][:], banks(bank[ch])[:, 0:2], mask[:, 4:5].broadcast_to([P, 2, P]), ALU.mult), f"{ch}_d")
                dve_steps.wait(dve, "G_sg", c)
                pe_steps.wait(dve, "G_o", c)
                dve_steps.done(tt(state["G"][:], delta["G"][:], banks(bank["G"] + 1), ALU.add), "G_s")
                for ch in "AB":
                    dve_steps.wait(dve, f"{ch}_d", c)
                    pe_steps.wait(dve, f"{ch}_y", c)
                    dve_steps.done(tt(delta[ch][:], delta[ch][:], state[ch][:], ALU.add), f"{ch}_m")
                    dve_steps.wait(dve, f"{ch}_m", c)
                    for pair, name in enumerate((f"{ch}_s0", f"{ch}_s")):
                        n = 2 * "AB".index(ch) + pair
                        dve_steps.done(nc.vector.tensor_scalar(state[ch][:, pair], delta[ch][:, pair],
                                                               carry[:, bass.ds(c, 1), n], None, ALU.mult), name)

            with dve.Fori(0, NT // 2) as i:
                for u in range(2):
                    tile_of(2 * i + u, u, i)


GN_EPS = 64e-5
HEAD_N = 64


def mixer_gates(nc, merged, z_gate, rwkv_gate, rwkv_bonus, norm_w, gn_w, gn_b, masks, w_out, m, w):
    with Stage(nc, "mo") as st:
        w_raw = st.sbuf("w_raw", [P, 2, D])
        (m_hi, m_lo), (w_hi, w_lo) = m, w
        z, gate, bonus = st.sbuf("z", [P, SEQ]), st.sbuf("gate", [P, SEQ]), st.sbuf("bonus", [P, SEQ])
        g_root, r_root = st.sbuf("g_root", [P, 2, SEQ]), st.sbuf("r_root", [P, 2, SEQ])
        r_value = st.sbuf("r_value", [P, 2, SEQ])
        mask = st.sbuf("mask", [P, 2, P])
        cols = st.sbuf("cols", [P, 12])
        eps = st.sbuf("eps", [P, 2])
        ps = st.psum("ps", [P, 8, HALF])
        setup, ready = st.sem("setup"), st.sem("ready")
        w_loaded = [st.sem(f"w_loaded{u}") for u in range(2)]
        w_rounded, w_split = st.sem("w_rounded"), st.sem("w_split")
        z_loaded, gates_loaded = st.sem("z_loaded"), st.sem("gates_loaded")
        pe_steps = Steps(st.sem("pe_steps"), "R_mean G_sum R_sum")
        squares = Steps(st.sem("squares"), "R_sq G_sq")
        act_steps = Steps(st.sem("act_steps"), "G_ln R_ln G_root R_root G_hi R_hi")
        centred = Steps(st.sem("centred"), "R_centred")
        dve_steps = Steps(st.sem("dve_steps"), "G_scaled G_value R_scaled R_offset R_value")
        pool_steps = Steps(st.sem("pool_steps"), "G_lo R_lo")
        block = st.stack.enter_context(nc.Block())
        BLOCKS = 4
        MEAN, G_SUM, R_SUM = 0, 2, 4

        def bank(n):
            return ps[:, n:n + 2].rearrange("p n t -> p (n t)")

        @block.sync
        def _(sp):
            sp.dma_start(mask[:, 0], masks[:, 1]).then_inc(setup, 16)
            sp.dma_start(mask[:, 1], masks[:, 4]).then_inc(setup, 16)
            for j, v in enumerate((norm_w, gn_w, gn_b)):
                sp.dma_start(cols[:, 4 * j:4 * j + 4], v).then_inc(setup, 16)
            for n in range(BLOCKS):
                dve_steps.wait(sp, "G_value", n - 1)
                sp.dma_start(z[:], z_gate[n]).then_inc(z_loaded, 16)
                dve_steps.wait(sp, "R_value", n - 1)
                sp.dma_start(bonus[:], rwkv_bonus[n]).then_inc(gates_loaded, 16)
                sp.dma_start(gate[:], rwkv_gate[n]).then_inc(gates_loaded, 16)

        @block.gpsimd
        def _(pool):
            pool_steps.open(pool)
            def load(k):
                pool.dma_start(w_raw[:, k % 2], w_out[k * P:(k + 1) * P, :]).then_inc(w_loaded[k % 2], 16)

            for k in range(2):
                load(k)

            def lower(n):
                act_steps.wait(pool, "G_hi", n)
                pool_steps.done(nc.gpsimd.tensor_tensor(m_lo[:, n], g_root[:, n % 2], m_hi[:, n].bitcast(F32), ALU.subtract), "G_lo")
                act_steps.wait(pool, "R_hi", n)
                pool_steps.done(nc.gpsimd.tensor_tensor(m_lo[:, n + 4], r_value[:, n % 2], m_hi[:, n + 4].bitcast(F32), ALU.subtract), "R_lo")

            for n in range(BLOCKS):
                for k in (2 * n, 2 * n + 1):
                    pool.wait_ge(w_rounded, k + 1)
                    nc.gpsimd.tensor_tensor(w_lo[:, k], w_raw[:, k % 2], w_hi[:, k].bitcast(F32), ALU.subtract).then_inc(w_split, 1)
                    if k + 2 < 2 * BLOCKS:
                        pool.wait_ge(w_split, k + 1)
                        load(k + 2)
                lower(n)

        @block.scalar
        def _(act):
            act_steps.open(act)
            squares.open(act)
            act.wait_ge(ready, 1)

            def logarithm(out, n_bank, n_eps, scale, name):
                act_steps.done(nc.scalar.activation(out, bank(n_bank), ACT.Ln, bias=eps[:, n_eps:n_eps + 1], scale=scale), name)

            def exponential(out, ln, name, n):
                act_steps.wait(act, ln, n)
                act_steps.done(nc.scalar.activation(out, out, ACT.Exp, scale=-0.5), name)

            def square(n):
                centred.wait(act, "R_centred", n)
                if n >= 2:
                    pool_steps.wait(act, "R_lo", n - 2)
                squares.done(nc.scalar.activation(r_root[:, n % 2], r_value[:, n % 2], ACT.Square), "R_sq")
                squares.done(nc.scalar.activation(g_root[:, n % 2], merged[:, n], ACT.Square), "G_sq")

            square(0)
            for n in range(BLOCKS):
                u = n % 2
                pe_steps.wait(act, "G_sum", n)
                logarithm(g_root[:, u], G_SUM, 0, 1.0 / P, "G_ln")
                pe_steps.wait(act, "R_sum", n)
                logarithm(r_root[:, u], R_SUM, 1, 1.0 / HEAD_N, "R_ln")
                exponential(g_root[:, u], "G_ln", "G_root", n)
                exponential(r_root[:, u], "R_ln", "R_root", n)
                for k in (2 * n, 2 * n + 1):
                    act.wait_ge(w_loaded[k % 2], 16 * (n + 1))
                    nc.scalar.copy(w_hi[:, k], w_raw[:, k % 2]).then_inc(w_rounded, 1)
                if n < BLOCKS - 1:
                    square(n + 1)
                dve_steps.wait(act, "G_value", n)
                act_steps.done(nc.scalar.copy(m_hi[:, n], g_root[:, u]), "G_hi")
                dve_steps.wait(act, "R_value", n)
                act_steps.done(nc.scalar.copy(m_hi[:, n + 4], r_value[:, u]), "R_hi")

        @block.vector
        def _(dve):
            dve_steps.open(dve)
            centred.open(dve)
            nc.vector.memset(eps[:, 0:1], NORM_EPS)
            nc.vector.memset(eps[:, 1:2], GN_EPS).then_inc(ready, 1)
            dve.wait_ge(setup, 16 * 5)
            stt = nc.vector.scalar_tensor_tensor

            def centre(n):
                pe_steps.wait(dve, "R_mean", n)
                if n >= 2:
                    pool_steps.wait(dve, "R_lo", n - 2)
                centred.done(stt(r_value[:, n % 2], bank(MEAN), -1.0 / HEAD_N, merged[:, n + 4], ALU.mult, ALU.add), "R_centred")

            centre(0)
            for n in range(BLOCKS):
                u = n % 2
                if n < BLOCKS - 1:
                    centre(n + 1)
                act_steps.wait(dve, "G_root", n)
                dve.wait_ge(z_loaded, 16 * (n + 1))
                dve_steps.done(nc.vector.tensor_tensor(z[:], g_root[:, u], z[:], ALU.mult), "G_scaled")
                dve_steps.wait(dve, "G_scaled", n)
                dve_steps.done(stt(g_root[:, u], merged[:, n], cols[:, n:n + 1], z[:], ALU.mult, ALU.mult), "G_value")
                act_steps.wait(dve, "R_root", n)
                dve_steps.done(stt(r_value[:, u], r_value[:, u], cols[:, n + 4:n + 5], r_root[:, u], ALU.mult, ALU.mult), "R_scaled")
                dve_steps.wait(dve, "R_scaled", n)
                dve.wait_ge(gates_loaded, 32 * (n + 1))
                dve_steps.done(stt(r_value[:, u], r_value[:, u], cols[:, n + 8:n + 9], bonus[:], ALU.add, ALU.add), "R_offset")
                dve_steps.wait(dve, "R_offset", n)
                dve_steps.done(nc.vector.tensor_tensor(r_value[:, u], r_value[:, u], gate[:], ALU.mult), "R_value")

        @block.tensor
        def _(pe):
            pe_steps.open(pe)
            pe.wait_ge(setup, 16 * 5)

            def over_channels(which, first_bank, src, name):
                for t in range(NH):
                    last = nc.tensor.matmul(ps[:, first_bank + t], mask[:, which], src[:, t * HALF:(t + 1) * HALF], start=True, stop=True)
                pe_steps.done(last, name)

            for n in range(BLOCKS):
                centred.wait(pe, "R_centred", n - 1)
                over_channels(1, MEAN, merged[:, n + 4], "R_mean")
                squares.wait(pe, "G_sq", n)
                over_channels(0, G_SUM, g_root[:, n % 2], "G_sum")
                over_channels(1, R_SUM, r_root[:, n % 2], "R_sum")


class MixerProduct:

    def __init__(self, nc, m, w, st, made_act, made_dve):
        self.nc, self.m, self.w, self.made_act, self.made_dve = nc, m, w, made_act, made_dve
        self.sums = st.psum("sums", [P, 2, 2, HALF])
        self.summed = st.sem("summed")

    def products(self, pe, n):
        tok = slice(n * P, (n + 1) * P)
        if n >= 2:
            pe.wait_ge(self.made_act, n - 1)
            pe.wait_ge(self.made_dve, n - 1)
        for half in range(2):
            for c in range(8):
                last = split_matmul(self.nc, self.sums[:, n % 2, half], tuple(part[:, c, tok] for part in self.m),
                                    tuple(part[:, c, half * HALF:(half + 1) * HALF] for part in self.w), c == 0, c == 7)
            last.then_inc(self.summed, 1)

    def act(self, act, n, place, u):
        act.wait_ge(self.summed, 2 * n + 1)
        self.nc.scalar.copy(place[:, 0:HALF], self.sums[:, u, 0]).then_inc(self.made_act, 1)

    def dve(self, dve, n, place, u):
        dve.wait_ge(self.summed, 2 * n + 2)
        self.nc.vector.tensor_copy(place[:, HALF:D], self.sums[:, u, 1]).then_inc(self.made_dve, 1)


NE = D_PLE // P


def embedding_branch(nc, x_in, out, branch, post_gain, share, pre_gain, p_in, w_gate, w_proj, last_gain, identity):
    ROWS = NE + ND
    with Stage(nc, "eb") as st:
        w_raw = st.sbuf("w_raw", [P, 2, D])
        w = w_hi, w_lo = st.sbuf("w_hi", [P, ROWS, D], F32R), st.sbuf("w_lo", [P, ROWS, D], F32R)
        p_raw = st.sbuf("p_raw", [P, 2, D_PLE])
        p = p_hi, p_lo = st.sbuf("p_hi", [P, NE, SEQ], F32R), st.sbuf("p_lo", [P, NE, SEQ], F32R)
        x = st.sbuf("x", [P, 2, D])
        squares = st.sbuf("squares", [P, 3, D])
        normed = st.sbuf("normed", [P, 2, D])
        made = st.sbuf("made", [P, 2, D])
        h = st.sbuf("h_hi", [P, 2, ND, P], F32R), st.sbuf("h_lo", [P, 2, ND, P], F32R)
        post_row, pre_row, last_row = (st.sbuf(name, [P, D]) for name in ("post_row", "pre_row", "last_row"))
        stats = st.sbuf("stats", [P, 3, 2, 4])
        turned = st.psum("turned", [P, 2, HALF])
        gate_sums = st.psum("gate_sums", [P, 2, 2, HALF])
        p_sums = st.psum("p_sums", [P, 2, HALF])
        rows_in, row_shared = st.sem("rows_in"), st.sem("row_shared")
        w_loaded = [st.sem(f"w_loaded{u}") for u in range(2)]
        p_loaded = [st.sem(f"p_loaded{u}") for u in range(2)]
        w_rounded, w_split = st.sem("w_rounded"), st.sem("w_split")
        p_turned, p_rounded, p_split = st.sem("p_turned"), st.sem("p_rounded"), st.sem("p_split")
        x_loaded = [st.sem(f"x_loaded{u}") for u in range(2)]
        stored = [st.sem(f"stored{u}") for u in range(2)]
        on_act = {part: Steps(st.sem(f"act_{part}"), names) for part, names in
                  dict(A="squares root", B="squares root", C="hi0 hi1", E="sigmoid", F="squares root").items()}
        on_dve = {part: Steps(st.sem(f"dve_{part}"), names) for part, names in
                  dict(A="mean inverse0 better inverse scaled", B="mean inverse0 better inverse normed", C="lo0 lo1", E="made",
                       F="mean inverse0 better inverse scaled").items()}
        on_pool = {part: Steps(st.sem(f"pool_{part}"), "added") for part in "AF"}
        turns, products = Steps(st.sem("turns"), "turned0 turned1"), Steps(st.sem("products"), "summed")
        block = st.stack.enter_context(nc.Block())
        PARTS = "ABF"

        def in_turn(weights, rows, **parts):
            row = 0
            for k in range(-3, NT):
                for _ in range(rows[k + 3] if k + 3 < len(rows) else 0):
                    weights(row)
                    row += 1
                for part, n in (("B", k + 2), ("E", k), ("A", k + 3), ("F", k), ("C", k + 2)):
                    if part in parts and 0 <= n < NT:
                        parts[part](n, n % 2)

        def quarter(part, u, j):
            return stats[:, PARTS.index(part), u, j:j + 1]

        @block.sync
        def _(sp):
            def load(n):
                sp.dma_start(x[:, n % 2], x_in[n * P:(n + 1) * P, :]).then_inc(x_loaded[n % 2], 16)

            gains = [(post_row, post_gain), (pre_row, pre_gain), (last_row, last_gain)]
            for n in range(2):
                load(n)
            for t in range(NT):
                if t >= 2:
                    sp.wait_ge(p_turned, t - 1)
                sp.dma_start(p_raw[:, t % 2], p_in[t * P:(t + 1) * P, :]).then_inc(p_loaded[t % 2], 16)
                if t < len(gains):
                    sp.dma_start(gains[t][0][:], row_of(gains[t][1])).then_inc(rows_in, 16)
            for n in range(NT + 3):
                if n + 2 < NT:
                    on_pool["A"].wait(sp, "added", n)
                    load(n + 2)
                if n >= 3:
                    on_pool["F"].wait(sp, "added", n - 3)
                    sp.dma_start(out[(n - 3) * P:(n - 2) * P, :], made[:, (n - 3) % 2]).then_inc(stored[(n - 3) % 2], 16)
            for u in range(2):
                sp.wait_ge(stored[u], 16 * (NT // 2))

        @block.scalar
        def _(act):
            for steps in on_act.values():
                steps.open(act)

            def norm(part, n, u, source):
                on_dve[part].wait(act, "mean", n - 1)
                on_act[part].done(nc.scalar.activation(squares[:, PARTS.index(part)], source, ACT.Square, accum_out=quarter(part, u, 0)), "squares")
                on_dve[part].wait(act, "mean", n)
                on_act[part].done(nc.scalar.activation(quarter(part, u, 2), quarter(part, u, 1), ACT.Sqrt), "root")

            def add(n, u):
                on_dve["A"].wait(act, "scaled", n - 2)
                norm("A", n, u, branch[:, n])

            def norm_x(n, u):
                on_pool["A"].wait(act, "added", n)
                on_dve["B"].wait(act, "normed", n - 2)
                norm("B", n, u, branch[:, n])

            def split(n, u):
                products.wait(act, "summed", n - 2)
                for b in range(2):
                    turns.wait(act, f"turned{b}", n)
                    on_act["C"].done(nc.scalar.copy(h[0][:, u, 4 * b:4 * b + 4], turned[:, b].rearrange("p (c t) -> p c t", t=P)), f"hi{b}")

            def make(n, u):
                products.wait(act, "summed", n)
                if n >= 2:
                    act.wait_ge(stored[u], 16 * (n // 2))
                on_act["E"].done(nc.scalar.activation(made[:, u], gate_sums[:, u].rearrange("p b w -> p (b w)"), ACT.Sigmoid), "sigmoid")

            def add_made(n, u):
                on_dve["E"].wait(act, "made", n)
                on_dve["F"].wait(act, "scaled", n - 2)
                norm("F", n, u, made[:, u])

            def weights(k):
                act.wait_ge(w_loaded[k % 2], 16 * (k // 2 + 1))
                nc.scalar.copy(w_hi[:, k], w_raw[:, k % 2]).then_inc(w_rounded, 1)
                if k < NT:
                    act.wait_ge(p_turned, k + 1)
                    nc.scalar.copy(p_hi[:, :, k * P:(k + 1) * P], p_sums[:, k % 2, 0:D_PLE].rearrange("p (e t) -> p e t", t=P)).then_inc(p_rounded, 1)

            in_turn(weights, (4, 3, 3), A=add, B=norm_x, C=split, E=make, F=add_made)

        @block.gpsimd
        def _(pool):
            for steps in on_pool.values():
                steps.open(pool)

            def add(n, u):
                on_dve["A"].wait(pool, "scaled", n)
                pool.wait_ge(x_loaded[u], 16 * (n // 2 + 1))
                on_pool["A"].done(nc.gpsimd.tensor_tensor(branch[:, n], branch[:, n], x[:, u], ALU.add), "added")

            def add_made(n, u):
                on_dve["F"].wait(pool, "scaled", n)
                on_pool["F"].done(nc.gpsimd.tensor_tensor(made[:, u], made[:, u], branch[:, n], ALU.add), "added")

            def weights(k):
                if k >= 2:
                    pool.wait_ge(w_split, k - 1)
                src = w_proj[k * P:(k + 1) * P, :] if k < NE else w_gate[(k - NE) * P:(k - NE + 1) * P, :]
                pool.dma_start(w_raw[:, k % 2], src).then_inc(w_loaded[k % 2], 16)

            in_turn(weights, (6, 3, 1), A=add, F=add_made)

        @block.vector
        def _(dve):
            for steps in on_dve.values():
                steps.open(dve)

            def inverse_root(part, n, u):
                steps, s = on_dve[part], [quarter(part, u, j) for j in range(4)]
                on_act[part].wait(dve, "squares", n)
                steps.done(nc.vector.tensor_scalar(s[1], s[0], 0.25 / D, 0.25 * NORM_EPS, ALU.mult, ALU.add), "mean")
                on_act[part].wait(dve, "root", n)
                steps.done(nc.vector.reciprocal(s[3], s[2]), "inverse0")
                steps.wait(dve, "inverse0", n)
                steps.done(nc.vector.scalar_tensor_tensor(s[0], s[1], s[3], s[2], ALU.mult, ALU.add), "better")
                steps.wait(dve, "better", n)
                steps.done(nc.vector.reciprocal(s[3], s[0]), "inverse")
                steps.wait(dve, "inverse", n)
                return s[3]

            def scaled(part, to, source, root, row, name):
                on_dve[part].done(nc.vector.scalar_tensor_tensor(to, source, root, row, ALU.mult, ALU.mult), name)

            def add(n, u):
                if n == 0:
                    dve.wait_ge(rows_in, 48)
                    nc.vector.tensor_scalar(post_row[:], post_row[:], share, None, ALU.mult).then_inc(row_shared, 1)
                    dve.wait_ge(row_shared, 1)
                scaled("A", branch[:, n], branch[:, n], inverse_root("A", n, u), post_row[:], "scaled")

            def norm_x(n, u):
                root = inverse_root("B", n, u)
                turns.wait(dve, "turned1", n - 2)
                scaled("B", normed[:, u], branch[:, n], root, pre_row[:], "normed")

            def split(n, u):
                for b in range(2):
                    on_act["C"].wait(dve, f"hi{b}", n)
                    part = (slice(None), u, slice(4 * b, 4 * b + 4))
                    on_dve["C"].done(nc.vector.tensor_tensor(h[1][part], turned[:, b].rearrange("p (c t) -> p c t", t=P),
                                                             h[0][part].bitcast(F32), ALU.subtract), f"lo{b}")

            def make(n, u):
                on_act["E"].wait(dve, "sigmoid", n)
                on_dve["E"].done(nc.vector.tensor_tensor(made[:, u], made[:, u], p_sums[:].rearrange("p b w -> p (b w)"), ALU.mult), "made")

            def add_made(n, u):
                scaled("F", made[:, u], made[:, u], inverse_root("F", n, u), last_row[:], "scaled")

            def weights(k):
                dve.wait_ge(w_rounded, k + 1)
                nc.vector.tensor_tensor(w_lo[:, k], w_raw[:, k % 2], w_hi[:, k].bitcast(F32), ALU.subtract).then_inc(w_split, 1)
                if k < NT:
                    dve.wait_ge(p_rounded, k + 1)
                    part = (slice(None), slice(None), slice(k * P, (k + 1) * P))
                    nc.vector.tensor_tensor(p_lo[part], p_sums[:, k % 2, 0:D_PLE].rearrange("p (e t) -> p e t", t=P),
                                            p_hi[part].bitcast(F32), ALU.subtract).then_inc(p_split, 1)

            in_turn(weights, (4, 3, 3), A=add, B=norm_x, C=split, E=make, F=add_made)

        @block.tensor
        def _(pe):
            turns.open(pe)
            products.open(pe)

            def turn(n):
                on_dve["B"].wait(pe, "normed", n)
                on_dve["C"].wait(pe, "lo1", n - 1)
                for b in range(2):
                    for c in range(4):
                        d = 4 * b + c
                        last = nc.tensor.transpose(turned[:, b, c * P:(c + 1) * P], normed[:, n % 2, d * P:(d + 1) * P], identity)
                    turns.done(last, f"turned{b}")

            def multiply(n):
                u, tok = n % 2, slice(n * P, (n + 1) * P)
                on_dve["C"].wait(pe, "lo1", n)
                on_act["E"].wait(pe, "sigmoid", n - 2)
                for half in range(2):
                    cols = slice(half * HALF, (half + 1) * HALF)
                    for d in range(ND):
                        if n == 0:
                            pe.wait_ge(w_split, NE + d + 1)
                        split_matmul(nc, gate_sums[:, u, half], tuple(part[:, u, d] for part in h),
                                     tuple(part[:, NE + d, cols] for part in w), d == 0, d == ND - 1)
                on_dve["E"].wait(pe, "made", n - 1)
                if n == 0:
                    pe.wait_ge(p_split, NT)
                for half in range(2):
                    cols = slice(half * HALF, (half + 1) * HALF)
                    for e in range(NE):
                        last = split_matmul(nc, p_sums[:, half], tuple(part[:, e, tok] for part in p),
                                            tuple(part[:, e, cols] for part in w), e == 0, e == NE - 1)
                products.done(last, "summed")

            for t in range(NT):
                pe.wait_ge(p_loaded[t % 2], 16 * (t // 2 + 1))
                if t >= 2:
                    pe.wait_ge(p_split, t - 1)
                for e in range(NE):
                    last = nc.tensor.transpose(p_sums[:, t % 2, e * P:(e + 1) * P], p_raw[:, t % 2, e * P:(e + 1) * P], identity)
                last.then_inc(p_turned, 1)
            turn(0)
            for n in range(NT):
                if n + 1 < NT:
                    turn(n + 1)
                multiply(n)


def layer(nc, x, p, ffn1_norm_pre, ffn1_w_gate, ffn1_w_up, ffn1_w_down, ffn1_norm_post, mix_norm_pre, w_in, conv_w,
          a_log, dt_bias, norm_w, rwkv_params, w2, a2, g2, w_out, mix_norm_post, ffn2_norm_pre,
          ffn2_w_gate, ffn2_w_up, ffn2_w_down, ffn2_norm_post, ple_norm_pre, ple_w_gate, ple_w_proj, ple_norm_post,
          masks, out):
    def internal(name, shape):
        return nc.dram_tensor(name, shape, F32, kind="Internal").ap()

    x1, x2 = (internal(f"x{n}", [SEQ, D]) for n in (1, 2))
    scratch = internal("tiles", [NT, P, TILE_W])
    z_gate, rwkv_gate, rwkv_bonus = (internal(name, [4, P, SEQ]) for name in ("z_gate", "rwkv_gate", "rwkv_bonus"))

    def h_parts(st):
        return st.sbuf("h_hi", [P, ND, SEQ], F32R), st.sbuf("h_lo", [P, ND, SEQ], F32R)

    with Stage(nc, "layer") as whole:
        identity = whole.sbuf("identity", [P, P])
        carry = whole.sbuf("carry", [P, NT, 4])
        loaded = whole.sem("loaded")
        with nc.Block() as block:
            @block.sync
            def _(sp):
                sp.dma_start(identity[:], masks[:, 0]).then_inc(loaded, 16)
                sp.wait_ge(loaded, 16)

        def weight_places(st):
            shape = [P, 2, 2, ND, P]
            return st.sbuf("ahead_raw", shape), st.sbuf("ahead_hi", shape, F32R), st.sbuf("ahead_lo", shape, F32R)

        def norm_places(up, x_in, post_gain, pre_gain):
            x, rows = (up[0][:, n].rearrange("p k d f -> p k (d f)") for n in range(2))
            places = x, rows[:, 0], rows[:, 1]
            return places, [(x[:, 0], x_in[0:P, :]), (x[:, 1], x_in[P:2 * P, :]),
                            (places[1], row_of(post_gain)), (places[2], row_of(pre_gain))]

        with Stage(nc, "first") as st:
            h = h_parts(st)
            with Stage(nc, "first_weights") as weights:
                up = weight_places(weights)
                gdn_places = tuple(part[:, 0] for part in up)
                with Stage(nc, "first_branch") as inner:
                    branch = inner.sbuf("branch", [P, NT, D])
                    residual_norm(nc, "n1", x, None, None, None, None, ffn1_norm_pre, h, identity[:],
                                  first_chunks(up, ffn1_w_gate, ffn1_w_up))
                    places, after = norm_places(up, x, ffn1_norm_post, mix_norm_pre)
                    swiglu(nc, "f1", h, ffn1_w_gate, ffn1_w_up, ffn1_w_down, branch, up, True, after)
                    with Stage(nc, "gdn_raw") as raw:
                        gdn_raw = raw.sbuf("raw", [P, 2, ND, P])
                        residual_norm(nc, "n2", x, x1, branch, ffn1_norm_post, 0.5, mix_norm_pre, h, identity[:],
                                      first_blocks((gdn_raw, *gdn_places[1:]), w_in, (GDN_SMALL, GDN_V)), loaded=places)
                gdn_projection(nc, h, w_in, conv_w, a_log, dt_bias, masks, scratch, z_gate, gdn_places)
            rwkv_projection(nc, h, w_in, w2, a2, g2, rwkv_params, masks, scratch, rwkv_gate, rwkv_bonus, carry)

        with Stage(nc, "second") as st:
            branch = st.sbuf("branch", [P, NT, D])
            with Stage(nc, "mixer") as inner:
                recurrences(nc, masks, scratch, carry, branch)
            with Stage(nc, "second_h") as with_h:
                h = h_parts(with_h)
                with Stage(nc, "w_out") as inner:
                    w = inner.sbuf("w_hi", [P, ND, D], F32R), inner.sbuf("w_lo", [P, ND, D], F32R)
                    mixer_gates(nc, branch, z_gate, rwkv_gate, rwkv_bonus, norm_w, rwkv_params[:, M_GNW:M_GNW + 4],
                                rwkv_params[:, M_GNB:M_GNB + 4], masks, w_out, h, w)
                    residual_norm(nc, "n3", x1, x2, branch, mix_norm_post, 1.0, ffn2_norm_pre, h, identity[:],
                                  maker=lambda *a: MixerProduct(nc, h, w, *a))
                with Stage(nc, "second_ffn") as inner:
                    up = weight_places(inner)
                    swiglu(nc, "f2", h, ffn2_w_gate, ffn2_w_up, ffn2_w_down, branch, up, False)
            embedding_branch(nc, x2, out, branch, ffn2_norm_post, 0.5, ple_norm_pre, p, ple_w_gate, ple_w_proj, ple_norm_post, identity[:])


def kernel(**inputs):
    import numpy as np
    import concourse.bacc as bacc
    from concourse.bass_utils import run_bass_kernel_spmd

    def rows(*names):
        return np.concatenate([np.asarray(inputs[name]).reshape(-1, P) for name in names]).T

    given = {name: np.asarray(a)[0] for name, a in inputs.items()}
    given["p"] = given["p"][0]
    position = np.arange(P)
    j, i = position[:, None], position[None, :]
    masks = np.zeros((P, MASKS, P), np.float32)
    for n, mask in enumerate([j == i, j >= 0, j <= i, j < i, j // HEAD_N == i // HEAD_N]):
        masks[:, n] = mask
    for level in range(7):
        size = 2 ** level
        masks[:, 5 + level] = (j // (2 * size) == i // (2 * size)) & (j // size < i // size)
    arrays = dict(
        x=given["x"], p=given["p"], ffn1_norm_pre=given["ffn1_norm_pre"], ffn1_w_gate=given["ffn1_w_gate"],
        ffn1_w_up=given["ffn1_w_up"], ffn1_w_down=given["ffn1_w_down"], ffn1_norm_post=given["ffn1_norm_post"],
        mix_norm_pre=given["mix_norm_pre"], w_in=given["w_in"],
        conv_w=given["gdn_conv_w"].reshape(CONV, 12, P).transpose(2, 0, 1),
        a_log=given["gdn_a_log"], dt_bias=given["gdn_dt_bias"],
        norm_w=np.repeat(given["gdn_norm_w"][:, None], 4, axis=1),
        rwkv_params=rows("rwkv_mu", "rwkv_w0", "rwkv_a0", "rwkv_k_k", "rwkv_k_a", "rwkv_r_k", "rwkv_gn_w", "rwkv_gn_b"),
        w2=given["rwkv_w2"], a2=given["rwkv_a2"], g2=given["rwkv_g2"], w_out=given["w_out"],
        mix_norm_post=given["mix_norm_post"], ffn2_norm_pre=given["ffn2_norm_pre"],
        ffn2_w_gate=given["ffn2_w_gate"], ffn2_w_up=given["ffn2_w_up"], ffn2_w_down=given["ffn2_w_down"],
        ffn2_norm_post=given["ffn2_norm_post"], ple_norm_pre=given["ple_norm_pre"], ple_w_gate=given["ple_w_gate"],
        ple_w_proj=given["ple_w_proj"], ple_norm_post=given["ple_norm_post"], masks=masks)
    nc = bacc.Bacc("TRN2", target_bir_lowering=False, num_devices=1)
    launched, args = {}, {}
    for name, a in arrays.items():
        launched[f"in_{name}"] = np.ascontiguousarray(a)
        args[name] = nc.dram_tensor(f"in_{name}", a.shape, mybir.dt.from_np(a.dtype), kind="ExternalInput").ap()
    args["out"] = nc.dram_tensor("out_x", (SEQ, D), F32, kind="ExternalOutput").ap()
    layer(nc, **args)
    result = run_bass_kernel_spmd(nc, [launched], core_ids=[0])
    return result.results[0]["out_x"].reshape(1, SEQ, D)
```
